# Optimizing a Trainium2 kernel written in Bass

```python
import math
import jax, jax.numpy as jnp
from jax import lax
import numpy as np

D_MODEL = 2048
BATCH = 1
SEQ = 512
DEPTH = 1

HEAD_DIM = 128
NSA_HEADS = 8
NSA_KV_GROUPS = 2
NSA_HPG = NSA_HEADS // NSA_KV_GROUPS
FOX_HEADS = 8
CMP_BLOCK = 32
CMP_STRIDE = 16
SLC_BLOCK = 64
SLC_TOPK = 16
WINDOW = 512
Q_BLOCK = 128
REL_BUCKETS = 32
REL_MAX_DIST = 128
D_FF = 5632
CONV_WIDTH = 3
EPS = 1e-6
NEG_INF = -1e30
FORCED_SCORE = 1e4

NSA_Q_DIM = NSA_HEADS * HEAD_DIM
NSA_KV_DIM = NSA_KV_GROUPS * HEAD_DIM
FOX_DIM = FOX_HEADS * HEAD_DIM
IN_SPLITS = (NSA_Q_DIM, NSA_KV_DIM, NSA_KV_DIM, NSA_KV_DIM, NSA_KV_DIM, NSA_KV_DIM, NSA_KV_DIM,
             3 * NSA_HEADS, FOX_DIM, FOX_DIM, FOX_DIM, FOX_HEADS, D_MODEL, D_MODEL)
D_IN = NSA_Q_DIM + 6 * NSA_KV_DIM + 3 * NSA_HEADS + 3 * FOX_DIM + FOX_HEADS + 2 * D_MODEL

kernel_name = "nsa_fox_gated_hybrid_block"

def rms_norm(x, g):
    xf = x.astype(jnp.float32)
    y = xf * lax.rsqrt(jnp.mean(xf * xf, axis=-1, keepdims=True) + EPS)
    return y.astype(x.dtype) * g

def t5_bucket(dist):
    n = jnp.maximum(dist, 0)
    max_exact = REL_BUCKETS // 2
    nf = jnp.maximum(n, 1).astype(jnp.float32)
    large = max_exact + (jnp.log(nf / max_exact) / math.log(REL_MAX_DIST / max_exact)
                         * (REL_BUCKETS - max_exact)).astype(jnp.int32)
    return jnp.where(n < max_exact, n, jnp.minimum(large, REL_BUCKETS - 1))

def rel_bias_dense(dist, table):
    bias = table[t5_bucket(dist)]
    return bias.transpose(2, 0, 1).reshape(NSA_KV_GROUPS, NSA_HPG, *dist.shape)

def masked_softmax(s, mask):
    p = jax.nn.softmax(jnp.where(mask, s, NEG_INF), axis=-1)
    return jnp.where(mask, p, 0.0)

def compress_tokens(kv, pos, w1, w2):
    bsz, seq, grp, dh = kv.shape
    ch = kv.reshape(bsz, seq // CMP_STRIDE, CMP_STRIDE, grp, dh)
    blocks = jnp.concatenate([ch[:, :-1], ch[:, 1:]], axis=2) + pos[:, None, :]
    flat = blocks.transpose(0, 1, 3, 2, 4).reshape(bsz, -1, grp, CMP_BLOCK * dh)
    return jax.nn.gelu(flat @ w1) @ w2

def causal_dwconv(a, w, bias):
    seq = a.shape[1]
    ap = jnp.pad(a, ((0, 0), (CONV_WIDTH - 1, 0), (0, 0)))
    out = bias
    for k in range(CONV_WIDTH):
        out = out + w[k] * ap[:, k:k + seq]
    return out

def nsa_attention(q, k_cmp, v_cmp, k_slc, v_slc, k_win, v_win, gate_logits,
                  pos_k, w1_k, w2_k, pos_v, w1_v, w2_v, rel_table):
    bsz, seq = q.shape[:2]
    scale = HEAD_DIM ** -0.5
    q = q.reshape(bsz, seq, NSA_KV_GROUPS, NSA_HPG, HEAD_DIM)
    kc = compress_tokens(k_cmp, pos_k, w1_k, w2_k)
    vc = compress_tokens(v_cmp, pos_v, w1_v, w2_v)
    n_cmp = kc.shape[1]
    n_slc = seq // SLC_BLOCK
    top_n = min(SLC_TOPK, n_slc)
    c_start = jnp.arange(n_cmp) * CMP_STRIDE
    c_end = c_start + CMP_BLOCK - 1
    s_start = jnp.arange(n_slc) * SLC_BLOCK
    overlap = ((c_start[:, None] < s_start[None, :] + SLC_BLOCK)
               & (c_end[:, None] >= s_start[None, :])).astype(jnp.float32)
    ks_blk = k_slc.reshape(bsz, n_slc, SLC_BLOCK, NSA_KV_GROUPS, HEAD_DIM).transpose(0, 3, 1, 2, 4)
    vs_blk = v_slc.reshape(bsz, n_slc, SLC_BLOCK, NSA_KV_GROUPS, HEAD_DIM).transpose(0, 3, 1, 2, 4)
    pad = ((0, 0), (WINDOW, 0), (0, 0), (0, 0))
    kw_pad = jnp.pad(k_win, pad)
    vw_pad = jnp.pad(v_win, pad)
    gates = jax.nn.sigmoid(gate_logits).reshape(bsz, seq, NSA_KV_GROUPS, NSA_HPG, 3)
    table_g = rel_table.reshape(REL_BUCKETS, NSA_KV_GROUPS, NSA_HPG)
    b_idx = jnp.arange(bsz)[:, None, None, None]
    g_idx = jnp.arange(NSA_KV_GROUPS)[None, :, None, None]
    blk_ids = jnp.arange(n_slc)

    def query_block(qb):
        t0 = qb * Q_BLOCK
        qblk = lax.dynamic_slice_in_dim(q, t0, Q_BLOCK, axis=1)
        tpos = t0 + jnp.arange(Q_BLOCK)
        sc = jnp.einsum('bqghd,bcgd->bghqc', qblk, kc).astype(jnp.float32) * scale
        dist_c = tpos[:, None] - c_end[None, :]
        pc = masked_softmax(sc + rel_bias_dense(dist_c, rel_table), dist_c >= 0)
        o_c = jnp.einsum('bghqc,bcgd->bqghd', pc.astype(vc.dtype), vc)
        imp = jnp.einsum('bghqc,cn->bgqn', pc, overlap)
        cur = tpos // SLC_BLOCK
        valid = s_start[None, :] <= tpos[:, None]
        forced = ((blk_ids[None, :] == 0) | (blk_ids[None, :] == cur[:, None])
                  | (blk_ids[None, :] == cur[:, None] - 1))
        score = jnp.where(valid, jnp.where(forced, FORCED_SCORE, imp), -1.0)
        _, idx = lax.top_k(score, top_n)
        ksel = ks_blk[b_idx, g_idx, idx].reshape(bsz, NSA_KV_GROUPS, Q_BLOCK, top_n * SLC_BLOCK, HEAD_DIM)
        vsel = vs_blk[b_idx, g_idx, idx].reshape(bsz, NSA_KV_GROUPS, Q_BLOCK, top_n * SLC_BLOCK, HEAD_DIM)
        spos = (idx[..., None] * SLC_BLOCK + jnp.arange(SLC_BLOCK)).reshape(bsz, NSA_KV_GROUPS, Q_BLOCK, -1)
        dist_s = tpos[None, None, :, None] - spos
        bias_s = table_g[t5_bucket(dist_s), g_idx].transpose(0, 1, 4, 2, 3)
        ss = jnp.einsum('bqghd,bgqkd->bghqk', qblk, ksel).astype(jnp.float32) * scale
        ps = masked_softmax(ss + bias_s, (dist_s >= 0)[:, :, None])
        o_s = jnp.einsum('bghqk,bgqkd->bqghd', ps.astype(vsel.dtype), vsel)
        kw = lax.dynamic_slice_in_dim(kw_pad, t0, Q_BLOCK + WINDOW, axis=1)
        vw = lax.dynamic_slice_in_dim(vw_pad, t0, Q_BLOCK + WINDOW, axis=1)
        wpos = t0 - WINDOW + jnp.arange(Q_BLOCK + WINDOW)
        dist_w = tpos[:, None] - wpos[None, :]
        mask_w = (dist_w >= 0) & (dist_w < WINDOW) & (wpos[None, :] >= 0)
        sw = jnp.einsum('bqghd,bkgd->bghqk', qblk, kw).astype(jnp.float32) * scale
        pw = masked_softmax(sw + rel_bias_dense(dist_w, rel_table), mask_w)
        o_w = jnp.einsum('bghqk,bkgd->bqghd', pw.astype(vw.dtype), vw)
        g = lax.dynamic_slice_in_dim(gates, t0, Q_BLOCK, axis=1)
        o = g[..., 0:1] * o_c + g[..., 1:2] * o_s + g[..., 2:3] * o_w
        return o.reshape(bsz, Q_BLOCK, NSA_Q_DIM)

    out = lax.map(query_block, jnp.arange(seq // Q_BLOCK))
    return out.transpose(1, 0, 2, 3).reshape(bsz, seq, NSA_Q_DIM)

def fox_attention(q, k, v, f_logit, f_bias):
    bsz, seq = q.shape[:2]
    scale = HEAD_DIM ** -0.5
    q = q.reshape(bsz, seq, FOX_HEADS, HEAD_DIM)
    k = k.reshape(bsz, seq, FOX_HEADS, HEAD_DIM)
    v = v.reshape(bsz, seq, FOX_HEADS, HEAD_DIM)
    log_f = jax.nn.log_sigmoid(f_logit.astype(jnp.float32) + f_bias.astype(jnp.float32))
    cum = lax.cumsum(log_f, axis=1).transpose(0, 2, 1)
    kpos = jnp.arange(seq)

    def query_block(qb):
        t0 = qb * Q_BLOCK
        qblk = lax.dynamic_slice_in_dim(q, t0, Q_BLOCK, axis=1)
        cq = lax.dynamic_slice_in_dim(cum, t0, Q_BLOCK, axis=2)
        tpos = t0 + jnp.arange(Q_BLOCK)
        logits = (jnp.einsum('bqhd,bkhd->bhqk', qblk, k).astype(jnp.float32) * scale
                  + (cq[..., None] - cum[:, :, None, :]))
        p = masked_softmax(logits, kpos[None, :] <= tpos[:, None])
        o = jnp.einsum('bhqk,bkhd->bqhd', p.astype(v.dtype), v)
        return o.reshape(bsz, Q_BLOCK, FOX_DIM)

    out = lax.map(query_block, jnp.arange(seq // Q_BLOCK))
    return out.transpose(1, 0, 2, 3).reshape(bsz, seq, FOX_DIM)

def setup_inputs(seed: int = 0) -> dict:
    key = jax.random.key(seed)
    ks = jax.random.split(key, 24)
    f32 = jnp.float32

    def w(k, shape, fan_in):
        return jax.random.normal(k, shape, f32) * fan_in ** -0.5

    def gain(k, shape):
        return 1.0 + 0.02 * jax.random.normal(k, shape, f32)

    return {
        "x": jax.random.normal(ks[0], (BATCH, SEQ, D_MODEL), f32),
        "attn_norm_g": gain(ks[1], (DEPTH, D_MODEL)),
        "w_in": w(ks[2], (DEPTH, D_MODEL, D_IN), D_MODEL),
        "cmp_pos_k": 0.1 * jax.random.normal(ks[3], (DEPTH, CMP_BLOCK, HEAD_DIM), f32),
        "cmp_w1_k": w(ks[4], (DEPTH, CMP_BLOCK * HEAD_DIM, HEAD_DIM), CMP_BLOCK * HEAD_DIM),
        "cmp_w2_k": w(ks[5], (DEPTH, HEAD_DIM, HEAD_DIM), HEAD_DIM),
        "cmp_pos_v": 0.1 * jax.random.normal(ks[6], (DEPTH, CMP_BLOCK, HEAD_DIM), f32),
        "cmp_w1_v": w(ks[7], (DEPTH, CMP_BLOCK * HEAD_DIM, HEAD_DIM), CMP_BLOCK * HEAD_DIM),
        "cmp_w2_v": w(ks[8], (DEPTH, HEAD_DIM, HEAD_DIM), HEAD_DIM),
        "rel_bias_table": 0.5 * jax.random.normal(ks[9], (REL_BUCKETS, NSA_HEADS), f32),
        "fox_forget_bias": 3.0 + 0.5 * jax.random.normal(ks[10], (DEPTH, FOX_HEADS), f32),
        "w_branch_nsa": w(ks[11], (DEPTH, NSA_Q_DIM, D_MODEL), NSA_Q_DIM),
        "w_branch_fox": w(ks[12], (DEPTH, FOX_DIM, D_MODEL), FOX_DIM),
        "w_out": w(ks[13], (DEPTH, D_MODEL, D_MODEL), D_MODEL),
        "ffn_norm_g": gain(ks[14], (DEPTH, D_MODEL)),
        "w_up": w(ks[15], (DEPTH, D_MODEL, 2 * D_FF), D_MODEL),
        "conv_w": w(ks[16], (DEPTH, CONV_WIDTH, D_FF), CONV_WIDTH),
        "conv_b": 0.02 * jax.random.normal(ks[17], (DEPTH, D_FF), f32),
        "w_down": w(ks[18], (DEPTH, D_FF, D_MODEL), D_FF),
        "final_norm_g": gain(ks[19], (D_MODEL,)),
    }

def reference(x, attn_norm_g, w_in, cmp_pos_k, cmp_w1_k, cmp_w2_k, cmp_pos_v, cmp_w1_v, cmp_w2_v,
              rel_bias_table, fox_forget_bias, w_branch_nsa, w_branch_fox, w_out,
              ffn_norm_g, w_up, conv_w, conv_b, w_down, final_norm_g):
    bsz, seq, _ = x.shape
    offsets = np.cumsum(np.array(IN_SPLITS))[:-1].tolist()
    kv_shape = (bsz, seq, NSA_KV_GROUPS, HEAD_DIM)
    for layer in range(DEPTH):
        h = rms_norm(x, attn_norm_g[layer])
        (q_n, kc_n, vc_n, ks_n, vs_n, kw_n, vw_n, g_n,
         q_f, k_f, v_f, f_l, m_a, m_b) = jnp.split(h @ w_in[layer], offsets, axis=-1)
        y_nsa = nsa_attention(q_n, kc_n.reshape(kv_shape), vc_n.reshape(kv_shape),
                              ks_n.reshape(kv_shape), vs_n.reshape(kv_shape),
                              kw_n.reshape(kv_shape), vw_n.reshape(kv_shape), g_n,
                              cmp_pos_k[layer], cmp_w1_k[layer], cmp_w2_k[layer],
                              cmp_pos_v[layer], cmp_w1_v[layer], cmp_w2_v[layer], rel_bias_table)
        y_fox = fox_attention(q_f, k_f, v_f, f_l, fox_forget_bias[layer])
        merged = (jax.nn.sigmoid(m_a) * (y_nsa @ w_branch_nsa[layer])
                  + jax.nn.sigmoid(m_b) * (y_fox @ w_branch_fox[layer]))
        x = x + merged @ w_out[layer]
        h = rms_norm(x, ffn_norm_g[layer])
        u, v = jnp.split(h @ w_up[layer], 2, axis=-1)
        u = causal_dwconv(u, conv_w[layer], conv_b[layer])
        x = x + (jax.nn.gelu(u) * v) @ w_down[layer]
    return rms_norm(x, final_norm_g)


_drawn_inputs = setup_inputs


def setup_inputs(seed=0):
    import zlib

    import numpy as np

    out = dict(_drawn_inputs(seed))
    spreads = {}
    factors = {'attn_norm_g': 8.0,
     'cmp_pos_k': 8.0,
     'cmp_pos_v': 11.323,
     'ffn_norm_g': 3.572,
     'conv_b': 5.309,
     'final_norm_g': 8.491}
    for name, (base, spread) in spreads.items():
        noise = np.random.default_rng([zlib.crc32(name.encode()), seed]).standard_normal(out[name].shape)
        drawn = base * np.exp(spread * noise) if base else spread * noise
        out[name] = __import__('jax').numpy.asarray(drawn.astype(out[name].dtype))
    for name, factor in factors.items():
        out[name] = (out[name] * factor).astype(out[name].dtype)
    return out
```

```python
from contextlib import ExitStack
from collections import namedtuple
import concourse.bass as bass
from concourse import mybir

P = 128
SEQ, D_MODEL, D_FF = 512, 2048, 5632
HEADS, GROUPS = 8, 2
TOK = SEQ // P
KT = D_MODEL // P
CMP_BLOCK, CMP_STRIDE = 32, 16
N_CMP = SEQ // CMP_STRIDE - 1
CP = 32
REL_BUCKETS, REL_MAX_DIST = 32, 128
CONV = 3
EPS = 1e-6
NEG = -1e30
SCALE = float(P) ** -0.5
CHUNKS = D_FF // (4 * P)
R_LEN = SEQ + P
COL_QN, COL_KV, COL_GN = 0, 1024, 2560
COL_QF, COL_KF, COL_VF, COL_FL = 2584, 3608, 4632, 5656
COL_MA, COL_MB = 5664, 7712
S_KV = 0
S_W1 = S_KV + 12
S_QN = S_W1 + 4
S_GA = S_QN + 8
S_FOX = S_GA + 24
S_GB = S_FOX + 24
S_WO = S_GB + 24
S_U0 = S_WO + 16
S_FF = S_U0 + 4
S_END = S_FF + 12 * (CHUNKS - 1) + 8

TILES = [3, 2, 0, 1]
S_PLACE = {3: (2, 0), 2: (3, 0), 0: (3, 384), 1: (4, 0)}
L_COL = {3: 0, 2: 512, 0: 896, 1: 1024}
PT_COL = {0: 0, 1: 512, 3: 896, 2: 1024}
CMP_COL = 1280

Slot = namedtuple("Slot", "n half par")


def slot(c, per=0, i=None):
    if i is None:
        return Slot(c, c // 2, c % 2)
    return Slot(i * per + c, i * (per // 2) + c // 2, c % 2)


class Chain:

    def __init__(self, eng, sem):
        self.eng, self.sem, self.base, self.k, self.per, self.i = eng, sem, 0, 0, 0, None

    def link(self, ins):
        self.k += 1
        ins.then_inc(self.sem, 1)
        at = self.base + self.k
        self.eng.wait_ge(self.sem, at if self.i is None else self.i * self.per + at)

    def enter(self, i, per):
        self.base, self.k, self.i, self.per = self.base + self.k, 0, i, per

    def leave(self, count):
        assert self.k == self.per, (self.k, self.per)
        self.base, self.k, self.i = self.base + self.per * count, 0, None


def build(nc, x, attn_norm_g, w_in, cmp_pos_k, cmp_w1_k, cmp_w2_k, cmp_pos_v, cmp_w1_v, cmp_w2_v,
          rel_bias_table, fox_forget_bias, w_branch_nsa, w_branch_fox, w_out, ffn_norm_g, w_up, conv_w,
          conv_b, w_down, final_norm_g, c_ident, c_onehot, c_tri, out):
    F32, F32R, BF16 = mybir.dt.float32, mybir.dt.float32r, mybir.dt.bfloat16
    ACT, ALU, AX = mybir.ActivationFunctionType, mybir.AluOpType, mybir.AxisListType
    ds = bass.ds
    KB = 1024
    ctx = ExitStack()
    BASE = 16512

    def at(name, off, shape, dt=F32):
        return nc.alloc_sbuf_tensor_at(name, shape, dt, offset=BASE + off)

    A_, M_, Y_ = 160 * KB, 112 * KB, 144 * KB
    h_hi = at("h_hi", 0, [P, KT, SEQ], F32R)
    h_lo = at("h_lo", 32 * KB, [P, KT, SEQ], F32R)
    w_raw = at("w_raw", 64 * KB, [P, 2, 2048])
    w_hi = at("w_hi", 80 * KB, [P, 2, 2048], F32R)
    w_lo = at("w_lo", 96 * KB, [P, 2, 2048], F32R)
    m32 = at("m32", M_, [P, KT, SEQ])
    kv_fm = at("kv_fm", M_, [P, 12, SEQ])
    bias_n = at("bias_n", M_ + 24 * KB, [P, 2, SEQ])
    q_n = at("q_n", M_ + 28 * KB, [P, SEQ])
    y32 = at("y32", Y_, [P, 8, 512])
    x_in = at("x_in", A_, [P, TOK, D_MODEL])
    wg_raw = at("wg_raw", A_ + 32 * KB, [P, KT, 32])
    wg_hi = at("wg_hi", A_ + 34 * KB, [P, KT, 32], F32R)
    wg_lo = at("wg_lo", A_ + 36 * KB, [P, KT, 32], F32R)
    ones_f = at("ones_f", A_ + 38 * KB, [8, SEQ])
    cum_f = at("cum_f", A_ + 40 * KB, [8, SEQ])
    tri32 = at("tri32", A_ + 42 * KB, [P, P])
    sq_junk = at("sq_junk", Y_, [P, D_MODEL])
    onehot = at("onehot", Y_ + 8 * KB, [33, R_LEN])
    r_sb = at("r_sb", Y_ + 8 * KB + 2560, [8, R_LEN])
    rows = at("rows", Y_ + 13 * KB, [P, 3, P])
    rs_rep = at("rs_rep", Y_ + 14 * KB + 512, [P, P])
    blk32 = at("blk32", A_, [P, CMP_BLOCK, GROUPS * CP])
    blkk_hi = at("blkk_hi", Y_, [P, CMP_BLOCK, GROUPS * CP], F32R)
    blkk_lo = at("blkk_lo", Y_ + 8 * KB, [P, CMP_BLOCK, GROUPS * CP], F32R)
    blkv_hi = at("blkv_hi", A_ + 25 * KB, [P, CMP_BLOCK, GROUPS * CP], F32R)
    blkv_lo = at("blkv_lo", A_ + 33 * KB, [P, CMP_BLOCK, GROUPS * CP], F32R)
    v_tm = at("v_tm", A_ + 8 * KB, [P, 4, TOK, P])
    w2_sb = at("w2_sb", A_ + 16 * KB, [P, 2, P])
    g4 = at("g4", A_ + 17 * KB, [P, GROUPS, TOK, P])
    vc4 = at("vc4", A_ + 21 * KB, [P, GROUPS, TOK, P])
    kc_fm = at("kc_fm", A_, [P, GROUPS * CP])
    gk = at("gk", A_ + 256, [P, GROUPS * CP])
    gv = at("gv", A_ + 512, [P, GROUPS * CP])
    l_slc = at("l_slc", A_ + 25 * KB, [P, 1280])
    p_cmp = at("p_cmp", A_ + 30 * KB, [P, TOK, CP])
    l_win = at("l_win", A_ + 30 * KB + 512, [P, 1280])
    pt_n = at("pt_n", A_ + 35 * KB + 512, [P, 1408])
    y_hi = at("y_hi", A_, [P, 8, SEQ], F32R)
    y_lo = at("y_lo", A_ + 16 * KB, [P, 8, SEQ], F32R)
    gate_t = at("gate_t", A_ + 32 * KB, [P, 2, SEQ])
    q_f = at("q_f", A_, [P, SEQ])
    k_f = at("k_f", A_ + 2 * KB, [P, SEQ])
    vf_fm = at("vf_fm", A_ + 4 * KB, [P, SEQ])
    vf_tm = at("vf_tm", A_ + 6 * KB, [P, TOK, P])
    l_fox = at("l_fox", A_ + 8 * KB, [P, 1280])
    pt_f = at("pt_f", A_ + 13 * KB, [P, 1280])
    bias_f = at("bias_f", A_ + 36 * KB, [P, 2, SEQ])
    x1 = at("x1", A_, [P, TOK, D_MODEL])
    gfin = at("gfin", A_ + 32 * KB, [P, D_MODEL])
    x1_new = at("x1_new", Y_, [P, TOK, 512])
    sq2 = at("sq2", Y_ + 8 * KB, [P, 512])
    rs_rep2 = at("rs_rep2", Y_ + 14 * KB, [P, TOK, P])
    a_hi = at("a_hi", M_, [P, 4, SEQ], F32R)
    a_lo = at("a_lo", M_ + 8 * KB, [P, 4, SEQ], F32R)
    g_rs = at("g_rs", M_ + 16 * KB, [P, 4, SEQ])
    u_pad = at("u_pad", Y_, [P, 2, SEQ + CONV - 1])
    conv_t = at("conv_t", Y_ + 4128, [P, 2, SEQ])
    a_t = at("a_t", Y_ + 4128 + 4 * KB, [P, 2, SEQ])
    sq3 = at("sq3", M_ + 24 * KB, [P, 512])
    o = 202 * KB + 512
    ident = at("ident", o, [P, P]); o += 512
    ident_b = at("ident_b", o, [P, P], BF16); o += 256
    tri_b = at("tri_b", o, [P, P], BF16); o += 256
    cols = at("cols", o, [P, 272]); o += 1088
    rbc = at("rbc", o, [P, SEQ]); o += 2048
    gates = at("gates", o, [P, TOK, 24]); o += 384
    l_cmp = at("l_cmp", o, [P, TOK, CP]); o += 512
    st = at("st", o, [P, 64]); o += 256
    assert BASE + o <= 229376
    gl = at("gl", Y_ + 15 * KB, [P, TOK, 32])
    fz = at("fz", Y_ + 15 * KB + 512, [P, 3, TOK, 8])
    fb = at("fb", A_ + 42 * KB + 0, [P, 8]) if False else at("fb", Y_ + 15 * KB + 896, [P, 8])
    tabx = at("tabx", Y_ + 15 * KB + 928, [33, 8])

    ss, mx, nmx, sm, rr = (st[:, 0:16], st[:, 16:28], st[:, 28:40], st[:, 40:52], st[:, 52:64])
    G_ATTN, G_FFN, C_B, C_W, C_POS = 0, 16, 32, [76, 120, 164], [208, 240]

    pb = [ctx.enter_context(nc.psum_tensor(f"bank{b}", [P, 512], F32)) for b in range(8)]

    r_dram = nc.dram_tensor("r_dram", [8, R_LEN], F32, kind="Internal").ap()
    e_dram = nc.dram_tensor("e_dram", [8 * P, SEQ], F32, kind="Internal").ap()
    c_dram = nc.dram_tensor("c_dram", [8, SEQ], F32, kind="Internal").ap()

    def sem(name):
        return ctx.enter_context(nc.semaphore(name))

    w_loaded = [sem("w_loaded0"), sem("w_loaded1")]
    w_hi_done = sem("w_hi_done")
    w_ready = sem("w_ready")
    w_used = sem("w_used")
    dve_own, act_own = sem("dve_own"), sem("act_own")
    const_in = sem("const_in")
    x_loaded = [sem(f"x_loaded{c}") for c in range(4)]
    wg_loaded, misc_in, w2_in = sem("wg_loaded"), sem("misc_in"), sem("w2_in")
    cols_t, cols_ok = sem("cols_t"), sem("cols_ok")
    xt_ready, xh_done, xl_done = sem("xt_ready"), sem("xh_done"), sem("xl_done")
    r_ps, r_ok, r_out, e_out = sem("r_ps"), sem("r_ok"), sem("r_out"), sem("e_out")
    ss_done, sqrt_in, sqrt_out, rep_ok, rep_used, rbc_ps, rbc_ok = (
        sem(n) for n in ("ss_done", "sqrt_in", "sqrt_out", "rep_ok", "rep_used", "rbc_ps", "rbc_ok"))
    wg_hi_ok, wg_ok, gl_ps, gl_ok, gates_ok, fz_ok, fe_ok, fl_ok, fcum_ps, fcum_ok, c_out = (
        sem(n) for n in ("wg_hi_ok", "wg_ok", "gl_ps", "gl_ok", "gates_ok", "fz_ok", "fe_ok", "fl_ok",
                         "fcum_ps", "fcum_ok", "c_out"))
    kv_done = sem("kv_done")
    vt_ps, vt_ok = sem("vt_ps"), sem("vt_ok")
    blk_sum, blk_hi, blk_ok = sem("blk_sum"), sem("blk_hi"), sem("blk_ok")
    gelu_ok, kc_ps, kc_ok, g4_ok, vc_ps, vc_ok = (
        sem(n) for n in ("gelu_ok", "kc_ps", "kc_ok", "g4_ok", "vc_ps", "vc_ok"))
    bn_loaded = [sem("bn_loaded0"), sem("bn_loaded1")]
    q_ready = sem("q_ready")
    ns_ready, ns_read = sem("ns_ready"), sem("ns_read")
    max_ready, cmp_shift = sem("max_ready"), sem("cmp_shift")
    exp_done, r_ready, p_ready = sem("exp_done"), sem("r_ready"), sem("p_ready")
    nt_ready, nt_act, nt_dve = sem("nt_ready"), sem("nt_act"), sem("nt_dve")
    npv_done, no_read = sem("npv_done"), sem("no_read")
    yh_ok, y_ok = sem("yh_ok"), sem("y_ok")
    gate_read = [sem("gateA_read"), sem("gateB_read")]
    sig_done = [sem("sigA_done"), sem("sigB_done")]
    br_read = [sem("brA_read"), sem("brB_read")]
    bf_loaded = [sem("bf_loaded0"), sem("bf_loaded1")]
    fproj = sem("fproj")
    fs_ready, fs_read, fmax_ready, fexp_done, fr_ready, fp_ready = (
        sem(n) for n in ("fs_ready", "fs_read", "fmax_ready", "fexp_done", "fr_ready", "fp_ready"))
    fv_ps, fv_ok, ft_ready, ft_act, ft_dve, fpv_done, fo_read = (
        sem(n) for n in ("fv_ps", "fv_ok", "ft_ready", "ft_act", "ft_dve", "fpv_done", "fo_read"))
    mh_ok, ml_ok = sem("mh_ok"), sem("ml_ok")
    xr_loaded, wo_done, x1_add, x1_put, x1t_ps, x1t_read = (
        sem(n) for n in ("xr_loaded", "wo_done", "x1_add", "x1_put", "x1t_ps", "x1t_read"))
    hh_ok, hl_ok = sem("hh_ok"), sem("hl_ok")
    rep2_ok, rbc2_ps, rbc2_ok = sem("rep2_ok"), sem("rbc2_ps"), sem("rbc2_ok")
    up_read, tap2, tap0, gelu2, g_ok = (sem(n) for n in ("up_read", "tap2", "tap0", "gelu2", "g_ok"))
    v_read, ah_ok, a_ok = sem("v_read"), sem("ah_ok"), sem("a_ok")
    dn_done, dn_add = sem("dn_done"), sem("dn_add")
    gf_in, sq3_done, xg_ok, rs3_ok, o_act, o_dve, stored = (
        sem(n) for n in ("gf_in", "sq3_done", "xg_ok", "rs3_ok", "o_act", "o_dve", "stored"))

    win = w_in[0].rearrange("(k p) n -> p k n", p=P)
    wup = w_up[0].rearrange("(k p) n -> p k n", p=P)
    wbr = [w_branch_nsa[0].rearrange("(k p) n -> p k n", p=P), w_branch_fox[0].rearrange("(k p) n -> p k n", p=P)]
    wo4 = w_out[0].rearrange("(s k p) n -> s p k n", p=P, k=4)
    wdn = w_down[0].rearrange("(k p) n -> p k n", p=P)
    w1 = [cmp_w1_k[0].rearrange("(h j d) n -> h d j n", d=P, h=2),
          cmp_w1_v[0].rearrange("(h j d) n -> h d j n", d=P, h=2)]
    x_t = x[0].rearrange("(t p) n -> p t n", p=P)
    out_t = out[0].rearrange("(t p) n -> t p n", p=P)

    waits_met = {"sp": sem("waits_met_sp"), "dve": sem("waits_met_dve"), "pool": sem("waits_met_pool")}

    def hold(eng, on, value):
        eng.wait_ge(on, value)
        eng.sem_inc(waits_met["sp" if eng is nc.sync else "dve" if eng is nc.vector else "pool"], 1)

    block = ctx.enter_context(nc.Block())

    @block.sync
    def _(sp):
        def load(s, src, **view):
            hold(sp, w_ready, s.n + 1)
            sp.dma_start(w_raw[:, s.par, :].rearrange("p (k n) -> p k n", **view), src).then_inc(w_loaded[s.par], 16)

        def load_cols(s, src, col):
            load(s, src[:, :, ds(col, P)], n=P)

        sp.dma_start(ident[:], c_ident).then_inc(const_in, 16)
        sp.dma_start(x_in[:, :, 0:512], x_t[:, :, 0:512]).then_inc(x_loaded[0], 16)
        load_cols(slot(0), win, COL_KV)
        for c in range(1, 4):
            sp.dma_start(x_in[:, :, 512 * c:512 * c + 512], x_t[:, :, 512 * c:512 * c + 512]).then_inc(x_loaded[c], 16)
        load_cols(slot(1), win, COL_KV + P)
        with sp.Fori(0, 5) as i:
            for j in range(2):
                load_cols(slot(2 + j, 2, i), win, i * (2 * P) + (COL_KV + (2 + j) * P))
        for j in range(4):
            load(slot(S_W1 + j), w1[j // 2][j % 2], n=P)
        load_cols(slot(S_QN), win, COL_QN)
        sp.wait_ge(e_out, 16)

        def load_bias_n(s, b, it):
            hold(sp, ns_read, s * 9 + 9)
            head = b * 4 + it
            sp.dma_start(bias_n[:, b, :], e_dram[ds(head * P, P), :]).then_inc(bn_loaded[b], 16)

        load_bias_n(0, 0, 0)
        with sp.Fori(0, 3) as it:
            load_cols(slot(S_QN + 1, 2, it), win, it * P + (COL_QN + 4 * P))
            load_bias_n(it * 2 + 1, 1, it)
            load_cols(slot(S_QN + 2, 2, it), win, it * P + (COL_QN + P))
            load_bias_n(it * 2 + 2, 0, it + 1)
        load_cols(slot(S_QN + 7), win, COL_QN + 7 * P)
        load_bias_n(7, 1, 3)

        def load_merge(base, col, which):
            with sp.Fori(0, 4) as i:
                for pair in range(2):
                    for j in range(2):
                        load_cols(slot(base + 3 * pair + j, 6, i), win, i * (4 * P) + (col + (2 * pair + j) * P))
                    load(slot(base + 3 * pair + 2, 6, i), wbr[which][:, :, ds(i * (4 * P) + 2 * pair * P, 2 * P)], n=2 * P)

        load_merge(S_GA, COL_MA, 0)

        def load_bias_f(h, b):
            hold(sp, fs_read, h * 4 + 1)
            sp.dma_start(bias_f[:, b, :], c_dram[ds(h, 1), :].to_broadcast([P, SEQ])).then_inc(bf_loaded[b], 16)

        for j, col in enumerate((COL_QF, COL_KF, COL_VF)):
            load_cols(slot(S_FOX + j), win, col)
        sp.wait_ge(c_out, 16)
        load_bias_f(0, 0)

        def load_head(c, per, i, h, b):
            for j, col in enumerate((COL_QF, COL_KF, COL_VF)):
                load_cols(slot(c + j, per, i), win, h * P + col)
            load_bias_f(h, b)

        with sp.Fori(0, 3) as i:
            load_head(S_FOX + 3, 6, i, i * 2 + 1, 1)
            load_head(S_FOX + 6, 6, i, i * 2 + 2, 0)
        load_head(S_FOX + 21, 0, None, 7, 1)
        load_merge(S_GB, COL_MB, 1)
        with sp.Fori(0, 4) as i:
            for s4 in range(4):
                load(slot(S_WO + s4, 4, i), wo4[s4][:, :, ds(i * 512, 512)], n=512)
        for j in range(4):
            load_cols(slot(S_U0 + j), wup, j * P)
        with sp.Fori(0, CHUNKS - 1) as c:
            for j in range(4):
                load_cols(slot(S_FF + j, 12, c), wup, c * 512 + (D_FF + j * P))
            for j in range(4):
                load_cols(slot(S_FF + 4 + j, 12, c), wup, c * 512 + (512 + j * P))
            for j in range(4):
                load(slot(S_FF + 8 + j, 12, c), wdn[:, ds(c * 4, 4), 512 * j:512 * j + 512], n=512)
        last = S_FF + 12 * (CHUNKS - 1)
        for j in range(4):
            load_cols(slot(last + j), wup, 2 * D_FF - 512 + j * P)
        for j in range(4):
            load(slot(last + 4 + j), wdn[:, 4 * (CHUNKS - 1):4 * CHUNKS, 512 * j:512 * j + 512], n=512)
        for t in range(TOK):
            sp.wait_ge(o_act, t + 1)
            sp.wait_ge(o_dve, t + 1)
            sp.dma_start(out_t[t], x1[:, t, :]).then_inc(stored, 16)
        sp.wait_ge(stored, 16 * TOK)

    @block.tensor
    def _(pe):
        mm = nc.tensor.matmul
        pe.sem_inc(w_used, 2)

        def three(dst, l_hi, l_lo, r_hi, r_lo, first, final):
            mm(dst, l_hi, r_hi, start=first, stop=False)
            mm(dst, l_hi, r_lo, start=False, stop=False)
            return mm(dst, l_lo, r_hi, start=False, stop=final)

        def slot_cols(s, bank, ks=range(KT)):
            if ks[0] == 0:
                pe.wait_ge(w_ready, s.n + 3)
            for k in ks:
                w = slice(k * P, k * P + P)
                last = three(pb[bank][:], w_hi[:, s.par, w], w_lo[:, s.par, w], h_hi[:, k, :], h_lo[:, k, :],
                             k == 0, k == KT - 1)
            if ks[-1] == KT - 1:
                last.then_inc(w_used, 1)

        def slot_tokens(s, banks, k0, n_k, a, b, first, final, done, free=None):
            pe.wait_ge(w_ready, s.n + 3)
            for t in range(TOK):
                if free is not None:
                    pe.wait_ge(*free(t))
                for k in range(4):
                    w = slice(k * 512, k * 512 + 512)
                    tk = slice(t * P, t * P + P)
                    last = three(pb[banks + t][:], a[:, k0 + k, tk], b[:, k0 + k, tk], w_hi[:, s.par, w],
                                 w_lo[:, s.par, w], first and k == 0, final and k == 3)
                if final and t < TOK - 1:
                    last.then_inc(done, 1)
            last.then_inc(w_used, 1)

        pe.wait_ge(const_in, 16 * 11)
        for j, (c, n) in enumerate(((0, 120), (120, 88), (208, 64))):
            last = nc.tensor.transpose(pb[2][:, c:c + n], rows[0:n, j, :], ident[0:n, 0:n])
        last.then_inc(cols_t, 1)
        pe.wait_ge(misc_in, 32)
        pe.wait_ge(dve_own, 1)
        mm(pb[3][0:8, 0:512], tabx[:], onehot[:, 0:512], start=True, stop=True)
        mm(pb[1][0:8, 0:P], tabx[:], onehot[:, 512:R_LEN], start=True, stop=True).then_inc(r_ps, 1)
        for k in range(KT):
            if k % 4 == 0:
                pe.wait_ge(x_loaded[k // 4], 16)
            if k >= 4:
                pe.wait_ge(xl_done, k - 3)
            for t in range(TOK):
                last = nc.tensor.transpose(pb[4 + k % 4][:, t * P:t * P + P], x_in[:, t, k * P:k * P + P], ident[:])
            last.then_inc(xt_ready, 1)
        pe.wait_ge(xl_done, KT)
        slot_cols(slot(0), 0)
        pe.wait_ge(r_ok, 1)
        slot_cols(slot(1), 1)
        for t in range(TOK):
            pe.wait_ge(rep_ok, t + 1)
            mm(pb[3][:, t * P:t * P + P], rs_rep[:], ident[:], start=True, stop=True).then_inc(rbc_ps, 1)
        pe.wait_ge(wg_ok, 1)
        pe.wait_ge(cols_ok, 1)
        for t in range(TOK):
            for k in range(KT):
                tk = slice(t * P, t * P + P)
                last = three(pb[2][:, t * 32:t * 32 + 32], h_hi[:, k, tk], h_lo[:, k, tk], wg_hi[:, k, :], wg_lo[:, k, :],
                             k == 0, k == KT - 1)
        last.then_inc(gl_ps, 1)
        with pe.Fori(0, 5) as i:
            for j in range(2):
                pe.wait_ge(kv_done, i * 2 + (j + 1))
                slot_cols(slot(2 + j, 2, i), j)
        pe.wait_ge(fl_ok, 1)
        pe.wait_ge(rbc_ok, 1)
        for t in range(TOK):
            last = mm(pb[3][0:8, t * P:t * P + P], fz[:, 2, t, :], ident[:], start=True, stop=True)
        last.then_inc(fcum_ps, 1)
        for kv in range(2):
            b_hi, b_lo = (blkk_hi, blkk_lo) if kv == 0 else (blkv_hi, blkv_lo)
            pe.wait_ge(blk_ok, kv + 1)
            for half in range(2):
                s = slot(S_W1 + 2 * kv + half)
                pe.wait_ge(w_ready, s.n + 3)
                if kv == 0 and half == 0:
                    pe.wait_ge(gl_ok, 1)
                for j in range(16):
                    w, pos = slice(j * P, j * P + P), 16 * half + j
                    last = three(pb[2][:, kv * 128:kv * 128 + 64], w_hi[:, s.par, w], w_lo[:, s.par, w], b_hi[:, pos, :],
                                 b_lo[:, pos, :], pos == 0, pos == CMP_BLOCK - 1)
                last.then_inc(w_used, 1)
            if kv == 0:
                pe.wait_ge(kv_done, 12)
                for v, src in enumerate((6, 7, 10, 11)):
                    for j in range(TOK):
                        last = nc.tensor.transpose(pb[4 + v][:, j * P:j * P + P], kv_fm[:, src, j * P:j * P + P], ident[:])
                    last.then_inc(vt_ps, 1)
        slot_cols(slot(S_QN), 0)
        pe.wait_ge(gelu_ok, 1)
        pe.wait_ge(w2_in, 32)
        pe.wait_ge(fcum_ok, 1)
        mm(pb[3][:, 0:64], w2_sb[:, 0, :], gk[:], start=True, stop=True).then_inc(kc_ps, 1)
        pe.wait_ge(g4_ok, 1)
        pe.wait_ge(vt_ok, 4)
        for g in range(GROUPS):
            for t in range(TOK):
                last = mm(pb[5 + g][:, t * P:t * P + P], g4[:, g, t, :], w2_sb[:, 1, :], start=True, stop=True)
        last.then_inc(vc_ps, 1)
        pe.wait_ge(kc_ok, 1)
        pe.wait_ge(vc_ok, 1)

        def scores(i, q, k, bias_mm):
            b, c = S_PLACE[i]
            dst = pb[b][:, c:c + P * (i + 1)]
            last = mm(dst, q[:, i * P:i * P + P], k[:, 0:P * (i + 1)], start=True, stop=not bias_mm)
            if bias_mm:
                last = mm(pb[b][:, c + P * i:c + P * i + P], ident_b[:], tri_b[:], start=False, stop=True)
            return last

        def transposes(js, bank, lt):
            for j in js:
                c = PT_COL[j] - PT_COL[js[0]]
                for i in range(j, TOK):
                    last = nc.tensor.transpose(pb[bank][:, c + (i - j) * P:c + (i - j) * P + P],
                                               lt[:, L_COL[i] + j * P:L_COL[i] + j * P + P], ident[:])
            return last

        def weigh(j, v, pt, first, final):
            return mm(pb[7][:, j * P:SEQ], v[:, j, :], pt[:, PT_COL[j]:PT_COL[j] + SEQ - j * P], start=first, stop=final)

        def nsa_step(s, g, filler):
            pe.wait_ge(q_ready, s + 1)
            pe.wait_ge(ns_read, s * 9 + 18)
            for i in range(TOK):
                last = mm(pb[g][:, CP * i:CP * i + CP], q_n[:, i * P:i * P + P], kc_fm[:, g * CP:g * CP + CP],
                          start=True, stop=True)
            last.then_inc(ns_ready, 1)
            for u, kind in enumerate((4, 8)):
                for k, i in enumerate(TILES):
                    if u == 1:
                        pe.wait_ge(ns_read, s * 9 + (18 + 2 + max(k, 2) if k else 18 + 2))
                    scores(i, q_n, kv_fm[:, kind + g, :], False).then_inc(ns_ready, 1)
            if filler is not None:
                slot_cols(filler, 1 - g)
            for u in range(2):
                lt = (l_slc, l_win)[u]
                pe.wait_ge(p_ready, s * 3 + (2 if u == 0 else 3))
                pe.wait_ge(nt_act, s * 4 + (2 * u + 2))
                transposes([0], 5, lt).then_inc(nt_ready, 1)
                pe.wait_ge(nt_dve, s * 2 + (u + 1))
                transposes([1, 3], 6, lt).then_inc(nt_ready, 1)
                pe.wait_ge(nt_act, s * 4 + (2 * u + 3))
                last = transposes([2], 5, lt)
                if u == 0:
                    last = nc.tensor.transpose(pb[5][:, 256:384], p_cmp[:].rearrange("p t c -> p (t c)"), ident[:])
                last.then_inc(nt_ready, 1)
                if u == 0:
                    pe.wait_ge(no_read, s + 1)
                v = v_tm[:, 2 * u + g]
                weigh(0, v, pt_n, u == 0, False)
                pe.wait_ge(nt_dve, s * 2 + (u + 2))
                weigh(1, v, pt_n, False, False)
                weigh(3, v, pt_n, False, False)
                pe.wait_ge(nt_act, s * 4 + (2 * u + 4))
                last = weigh(2, v, pt_n, False, u == 1)
                if u == 0:
                    for i in range(TOK):
                        last = mm(pb[7][:, i * P:i * P + P], vc4[:, g, i, :], pt_n[:, CMP_COL:CMP_COL + P], start=False, stop=False)
                last.then_inc(npv_done, 1)

        with pe.Fori(0, 3) as it:
            nsa_step(it * 2, 0, slot(S_QN + 1, 2, it))
            nsa_step(it * 2 + 1, 1, slot(S_QN + 2, 2, it))
        nsa_step(6, 0, slot(S_QN + 7))
        nsa_step(7, 1, None)

        def merge(base, which, count):
            with pe.Fori(0, count) as i:
                for pair in range(2):
                    for j in range(2):
                        pe.wait_ge(gate_read[which], i * 4 + (2 * pair + j + 1))
                        slot_cols(slot(base + 3 * pair + j, 6, i), j)
                    s = slot(base + 3 * pair + 2, 6, i)
                    pe.wait_ge(w_ready, s.n + 3)
                    pe.wait_ge(y_ok, 2 * which + 2)
                    pe.wait_ge(br_read[which], i * 2 + (pair + 1))
                    for j in range(2):
                        for k in range(8):
                            w = slice(k * 2 * P + j * P, k * 2 * P + j * P + P)
                            last = three(pb[2 + j][:], w_hi[:, s.par, w], w_lo[:, s.par, w], y_hi[:, k, :], y_lo[:, k, :],
                                         k == 0, k == 7)
                    last.then_inc(w_used, 1)

        merge(S_GA, 0, 4)

        def fox_slot(s, m, bank):
            pe.wait_ge(fproj, m + 1)
            slot_cols(s, bank)

        for j in range(3):
            fox_slot(slot(S_FOX + j), j, j % 2)

        def fox_step(h, c, per, i, fill):
            pe.wait_ge(fproj, h * 3 + 4)
            for k, t in enumerate(TILES):
                pe.wait_ge(fs_read, h * 4 + (7 if k == 1 else 5 + k))
                if k == 3:
                    pe.wait_ge(fv_ok, h + 1)
                scores(t, q_f, k_f, True).then_inc(fs_ready, 1)
            if fill:
                fox_slot(slot(c, per, i), h * 3 + 3, c % 2)
            pe.wait_ge(fproj, h * 3 + 5)
            pe.wait_ge(fs_read, h * 4 + 12)
            for j in range(TOK):
                last = nc.tensor.transpose(pb[4][:, j * P:j * P + P], vf_fm[:, j * P:j * P + P], ident[:])
            last.then_inc(fv_ps, 1)
            pe.wait_ge(fp_ready, h + 1)
            pe.wait_ge(ft_act, h * 2 + 2)
            transposes([0], 5, l_fox).then_inc(ft_ready, 1)
            pe.wait_ge(ft_dve, h + 1)
            transposes([1, 3], 6, l_fox).then_inc(ft_ready, 1)
            pe.wait_ge(ft_act, h * 2 + 3)
            transposes([2], 5, l_fox).then_inc(ft_ready, 1)
            if fill:
                fox_slot(slot(c + 1, per, i), h * 3 + 4, (c + 1) % 2)
            pe.wait_ge(fo_read, h + 1)
            pe.wait_ge(fv_ok, h + 2)
            weigh(0, vf_tm, pt_f, True, False)
            pe.wait_ge(ft_dve, h + 2)
            weigh(1, vf_tm, pt_f, False, False)
            weigh(3, vf_tm, pt_f, False, False)
            pe.wait_ge(ft_act, h * 2 + 4)
            weigh(2, vf_tm, pt_f, False, True).then_inc(fpv_done, 1)
            if fill:
                fox_slot(slot(c + 2, per, i), h * 3 + 5, c % 2)

        with pe.Fori(0, 3) as i:
            fox_step(i * 2, S_FOX + 3, 6, i, True)
            fox_step(i * 2 + 1, S_FOX + 6, 6, i, True)
        fox_step(6, S_FOX + 21, 0, None, True)
        fox_step(7, 0, 0, None, False)
        merge(S_GB, 1, 4)

        def wo_slot(c, per, i, sub, free):
            slot_tokens(slot(c, per, i), 0, 4 * sub, 4, h_hi, h_lo, sub == 0, sub == 3, wo_done, free)

        def x1_transposes(g):
            pe.wait_ge(x1_add, g * 4 + 4)
            for k in range(4):
                pe.wait_ge(x1t_read, g * 4 + (k + 1))
                for t in range(TOK):
                    last = nc.tensor.transpose(pb[4 + k][:, t * P:t * P + P], x1_new[:, t, k * P:k * P + P], ident[:])
                last.then_inc(x1t_ps, 1)

        pe.wait_ge(ml_ok, 1)
        wo_slot(S_WO, 0, None, 0, lambda t: (br_read[1], 8 if t < 2 else 9))
        pe.wait_ge(ml_ok, 4)
        with pe.Fori(0, 3) as g:
            for sub in range(1, 4):
                wo_slot(S_WO + sub, 4, g, sub, None)
            wo_slot(S_WO + 4, 4, g, 0, lambda t: (x1_add, g * 4 + (t + 1)))
            x1_transposes(g)
        for sub in range(1, 4):
            wo_slot(S_WO + 12 + sub, 0, None, sub, None)

        pe.wait_ge(hl_ok, 3)
        s0 = slot(S_U0)
        pe.wait_ge(x1_add, 14)
        slot_cols(s0, 0, range(0, 12))
        x1_transposes(3)
        pe.wait_ge(hl_ok, 4)
        slot_cols(s0, 0, range(12, KT))
        slot_cols(slot(S_U0 + 1), 1)
        pe.wait_ge(rep2_ok, 1)
        pe.wait_ge(x1t_read, 20)
        for t in range(TOK):
            last = mm(pb[6][:, t * P:t * P + P], rs_rep2[:, t, :], ident[:], start=True, stop=True)
        last.then_inc(rbc2_ps, 1)
        for j in (2, 3):
            pe.wait_ge(up_read, j - 1)
            slot_cols(slot(S_U0 + j), j % 2)

        def v_slots(c, per, i, u_n):
            for j in range(4):
                if j < 2:
                    pe.wait_ge(up_read, u_n + (3 + j))
                else:
                    pe.wait_ge(v_read, u_n + (j - 1))
                slot_cols(slot(c + j, per, i), j % 2)

        def down_slots(c, per, i, chunk):
            for j in range(4):
                if j == 0:
                    pe.wait_ge(a_ok, chunk * 4 + 4)
                slot_tokens(slot(c + j, per, i), 2, 0, 4, a_hi, a_lo, True, True, dn_done, lambda t: (dn_add, chunk * 16 + (4 * j + t + 1)))

        pe.wait_ge(x1_add, 16)
        with pe.Fori(0, CHUNKS - 1) as c:
            v_slots(S_FF, 12, c, c * 4)
            for j in range(4):
                if j < 2:
                    pe.wait_ge(v_read, c * 4 + (3 + j))
                else:
                    pe.wait_ge(up_read, c * 4 + (4 + j - 1))
                slot_cols(slot(S_FF + 4 + j, 12, c), j % 2)
            down_slots(S_FF + 8, 12, c, c)
        tail = S_FF + 12 * (CHUNKS - 1)
        v_slots(tail, 0, None, 4 * (CHUNKS - 1))
        down_slots(tail + 4, 0, None, CHUNKS - 1)

    @block.scalar
    def _(act):
        A = nc.scalar.activation
        own = Chain(act, act_own)

        def hi(s):
            act.wait_ge(w_loaded[s.par], s.half * 16 + 16)
            act.wait_ge(w_used, s.n + 1)
            A(w_hi[:, s.par, :], w_raw[:, s.par, :], ACT.Copy).then_inc(w_hi_done, 1)

        for src, (j, r0, n) in ((attn_norm_g[0], (0, 0, 16)), (ffn_norm_g[0], (0, 16, 16)), (conv_b[0], (0, 32, 44)),
                                (conv_w[0, 0], (0, 76, 44)), (conv_w[0, 1], (1, 0, 44)), (conv_w[0, 2], (1, 44, 44))):
            act.dma_start(rows[r0:r0 + n, j, :], src.rearrange("(a b) -> a b", b=P)).then_inc(const_in, 16)
        act.dma_start(rows[0:32, 2, :], cmp_pos_k[0]).then_inc(const_in, 16)
        act.dma_start(rows[32:64, 2, :], cmp_pos_v[0]).then_inc(const_in, 16)
        act.dma_start(tri32[:], c_tri).then_inc(const_in, 16)
        act.dma_start(fb[:], fox_forget_bias[0:1, :].to_broadcast([P, 8])).then_inc(const_in, 16)
        act.dma_start(onehot[:], c_onehot).then_inc(misc_in, 16)
        act.dma_start(tabx[0:32, :], rel_bias_table).then_inc(misc_in, 16)
        act.dma_start(wg_raw[:, :, 0:24], win[:, :, COL_GN:COL_GN + 24]).then_inc(wg_loaded, 16)
        act.dma_start(wg_raw[:, :, 24:32], win[:, :, COL_FL:COL_FL + 8]).then_inc(wg_loaded, 16)
        act.wait_ge(cols_ok, 1)
        for k in range(KT):
            act.wait_ge(xt_ready, k + 1)
            A(h_hi[:, k, :], pb[4 + k % 4][:], ACT.Copy, scale=cols[:, G_ATTN + k:G_ATTN + k + 1]).then_inc(xh_done, 1)
        hi(slot(0))
        hi(slot(1))
        for t in range(TOK):
            if t:
                act.wait_ge(ss_done, t)
            A(sq_junk[:], x_in[:, t, :], ACT.Square, accum_out=ss[:, t:t + 1]).then_inc(ss_done, 1)
        act.wait_ge(wg_loaded, 32)
        A(wg_hi[:], wg_raw[:], ACT.Copy).then_inc(wg_hi_ok, 1)
        act.wait_ge(r_ok, 1)
        act.dma_start(r_dram, r_sb[:]).then_inc(r_out, 16)
        act.wait_ge(r_out, 16)
        act.dma_start(e_dram.rearrange("(h p) c -> h p c", p=P),
                      bass.AP(tensor=r_dram.tensor, offset=P - 1, ap=[[R_LEN, HEADS], [-1, P], [1, SEQ]])).then_inc(e_out, 16)
        act.wait_ge(sqrt_in, 1)
        A(ss[:, 8:12], ss[:, 4:8], ACT.Sqrt).then_inc(sqrt_out, 1)
        hi(slot(2))
        act.wait_ge(gl_ok, 1)
        A(gates[:], gl[:, :, 0:24], ACT.Sigmoid).then_inc(gates_ok, 1)
        act.wait_ge(fz_ok, 1)
        own.link(A(fz[:, 1], fz[:, 2], ACT.Abs))
        own.link(A(fz[:, 1], fz[:, 1], ACT.Exp, scale=-1.0))
        A(fz[:, 1], fz[:, 1], ACT.Ln, bias=1.0).then_inc(fe_ok, 1)
        with act.Fori(0, 5) as i:
            for j in range(2):
                hi(slot(3 + j, 2, i))
        act.wait_ge(fcum_ok, 1)
        act.dma_start(c_dram, cum_f[:]).then_inc(c_out, 16)
        act.wait_ge(blk_sum, 1)
        A(blkk_hi[:], blk32[:], ACT.Copy).then_inc(blk_hi, 1)
        hi(slot(S_W1 + 1))
        act.wait_ge(blk_sum, 2)
        A(blkv_hi[:], blk32[:], ACT.Copy).then_inc(blk_hi, 1)
        hi(slot(S_W1 + 2))
        hi(slot(S_W1 + 3))
        for v in range(4):
            act.wait_ge(vt_ps, v + 1)
            A(v_tm[:, v].rearrange("p j d -> p (j d)"), pb[4 + v][:], ACT.Copy).then_inc(vt_ok, 1)
        act.wait_ge(w_ready, S_W1 + 5)
        act.dma_start(w2_sb[:, 0, :], cmp_w2_k[0]).then_inc(w2_in, 16)
        act.dma_start(w2_sb[:, 1, :], cmp_w2_v[0]).then_inc(w2_in, 16)
        hi(slot(S_QN))
        hi(slot(S_QN + 1))
        act.wait_ge(w_used, S_W1 + 4 + 2)
        A(gv[:], pb[2][:, 128:192], ACT.Gelu_apprx_tanh)
        A(gk[:], pb[2][:, 0:64], ACT.Gelu_apprx_tanh).then_inc(gelu_ok, 1)
        act.wait_ge(kc_ps, 1)
        A(kc_fm[:], pb[3][:, 0:64], ACT.Copy).then_inc(kc_ok, 1)

        def exps(lt, c):
            for i in TILES:
                cols_ = slice(L_COL[i], L_COL[i] + P * (i + 1))
                last = A(lt[:, cols_], lt[:, cols_], ACT.Exp, bias=nmx[:, c + i:c + i + 1], accum_out=sm[:, c + i:c + i + 1])
            return last

        def nsa_step(s, head, fill):
            if fill is not None:
                hi(fill)
            act.wait_ge(cmp_shift, s + 1)
            A(p_cmp[:], p_cmp[:], ACT.Exp).then_inc(exp_done, 1)
            act.wait_ge(max_ready, s * 2 + 1)
            exps(l_slc, 4).then_inc(exp_done, 1)
            act.wait_ge(max_ready, s * 2 + 2)
            exps(l_win, 8).then_inc(exp_done, 1)
            for u in range(2):
                act.wait_ge(nt_ready, s * 6 + (3 * u + 1) + 6)
                act.wait_ge(npv_done, s * 2 + (u + 1))
                A(pt_n[:, 0:512], pb[5][:], ACT.Copy).then_inc(nt_act, 1)
                act.wait_ge(nt_ready, s * 6 + (3 * u + 3) + 6)
                n = 384 if u == 0 else 256
                A(pt_n[:, 1024:1024 + n], pb[5][:, 0:n], ACT.Copy).then_inc(nt_act, 1)
            act.wait_ge(npv_done, s * 2 + 3)
            A(y32[:, ds(head, 1), :].rearrange("p a n -> p (a n)"), pb[7][:], ACT.Copy).then_inc(no_read, 1)

        act.sem_inc(nt_act, 2)
        act.sem_inc(no_read, 1)
        with act.Fori(0, 3) as it:
            nsa_step(it * 2, it, slot(S_QN + 2, 2, it))
            nsa_step(it * 2 + 1, it + 4, slot(S_QN + 3, 2, it))
        nsa_step(6, 3, slot(S_QN + 8))
        nsa_step(7, 7, None)

        def merge(base, which):
            def iteration(c, per, i, count, last):
                for pair in range(2):
                    for j in range(2):
                        hi(slot(c + 3 * pair + j + 1, per, i))
                        if pair == 0 and j == 0 and which == 0 and last is None:
                            pass
                        act.wait_ge(gate_read[which], count + (2 * pair + j + 3))
                        A(gate_t[:, j, :], gate_t[:, j, :], ACT.Sigmoid).then_inc(sig_done[which], 1)
                    hi(slot(c + 3 * pair + 3, per, i))
            if which == 0:
                act.wait_ge(npv_done, 2 * HEADS + 1)
                act.wait_ge(no_read, HEADS + 1)
            else:
                act.wait_ge(fpv_done, HEADS + 1)
                act.wait_ge(fo_read, HEADS + 1)
            for q in range(2):
                A(y_hi[:, 4 * q:4 * q + 4, :], y32[:, 4 * q:4 * q + 4, :], ACT.Copy).then_inc(yh_ok, 1)
            with act.Fori(0, 3 if which else 4) as i:
                iteration(base, 6, i, i * 4, None)
            if which:
                iteration(base + 18, 0, None, 12, True)

        merge(S_GA, 0)
        act.sem_inc(ft_act, 2)
        act.sem_inc(fo_read, 1)
        act.sem_inc(fv_ok, 1)

        for j in range(3):
            hi(slot(S_FOX + j + 1))

        def fox_step(h, c, per, i, fill):
            if fill:
                hi(slot(c + 1, per, i))
            act.wait_ge(fmax_ready, h + 1)
            exps(l_fox, 4).then_inc(fexp_done, 1)
            if fill:
                hi(slot(c + 2, per, i))
            act.wait_ge(fv_ps, h + 1)
            act.wait_ge(fpv_done, h + 1)
            A(vf_tm[:].rearrange("p j d -> p (j d)"), pb[4][:], ACT.Copy).then_inc(fv_ok, 1)
            act.wait_ge(ft_ready, h * 3 + 1)
            A(pt_f[:, 0:512], pb[5][:], ACT.Copy).then_inc(ft_act, 1)
            act.wait_ge(ft_ready, h * 3 + 3)
            A(pt_f[:, 1024:1280], pb[5][:, 0:256], ACT.Copy).then_inc(ft_act, 1)
            if fill:
                hi(slot(c + 3, per, i))
            act.wait_ge(fpv_done, h + 2)
            A(y32[:, ds(h, 1), :].rearrange("p a n -> p (a n)"), pb[7][:], ACT.Copy).then_inc(fo_read, 1)

        with act.Fori(0, 3) as i:
            fox_step(i * 2, S_FOX + 3, 6, i, True)
            fox_step(i * 2 + 1, S_FOX + 6, 6, i, True)
        fox_step(6, S_FOX + 21, 0, None, True)
        fox_step(7, 0, 0, None, False)
        merge(S_GB, 1)
        for q in range(4):
            act.wait_ge(br_read[1], 8 if q < 3 else 9)
            A(h_hi[:, 4 * q:4 * q + 4, :], m32[:, 4 * q:4 * q + 4, :], ACT.Copy).then_inc(mh_ok, 1)
        act.wait_ge(w_used, S_WO + 2)
        for c in range(4):
            act.dma_start(x1[:, :, 512 * c:512 * c + 512], x_t[:, :, 512 * c:512 * c + 512]).then_inc(xr_loaded, 16)

        def wo_out(g):
            for t in range(TOK):
                act.wait_ge(x1_add, g * 4 + (t + 1))
                own.link(A(sq2[:], x1_new[:, t, :], ACT.Square, accum_out=x1_ss(g, t)))
                A(x1[:, t, ds(g * 512, 512)], x1_new[:, t, :], ACT.Copy).then_inc(x1_put, 1)

        def x1_ss(g, t):
            return ssq[:, ds(g * 4 + t, 1)] if not isinstance(g, int) else ssq[:, 4 * g + t:4 * g + t + 1]

        def wo_trans(g):
            for k in range(4):
                act.wait_ge(x1t_ps, g * 4 + (k + 2))
                A(m32[:, ds(g * 4 + k, 1), :].rearrange("p a n -> p (a n)"), pb[4 + k][:], ACT.Copy,
                  scale=cols[:, ds(g * 4 + (G_FFN + k), 1)]).then_inc(x1t_read, 1)

        ssq = ss
        act.sem_inc(x1t_read, 4)
        hi(slot(S_WO + 1))
        own.enter(None, 0)
        with act.Fori(0, 3) as g:
            own.enter(g, 4)
            for sub in range(1, 4):
                hi(slot(S_WO + sub + 1, 4, g))
            wo_out(g)
            hi(slot(S_WO + 5, 4, g))
            wo_trans(g)
        own.leave(3)
        for sub in range(1, 4):
            hi(slot(S_WO + 12 + sub + 1))
            act.wait_ge(x1t_read, 16)
            A(h_hi[:, 4 * sub - 4:4 * sub, :], m32[:, 4 * sub - 4:4 * sub, :], ACT.Copy).then_inc(hh_ok, 1)
        wo_out(3)
        wo_trans(3)
        act.wait_ge(x1t_read, 20)
        act.wait_ge(w_used, S_U0 + 2)
        A(h_hi[:, 12:16, :], m32[:, 12:16, :], ACT.Copy).then_inc(hh_ok, 1)
        act.wait_ge(sqrt_in, 2)
        A(nmx[:, 4:8], nmx[:, 0:4], ACT.Sqrt).then_inc(sqrt_out, 1)

        def conv_tap(n, f, j):
            if not isinstance(n, int) or n >= 2:
                act.wait_ge(g_ok, n - 1)
            act.wait_ge(up_read, n + 1)
            A(conv_t[:, j % 2, :], u_pad[:, j % 2, 2:SEQ + 2], ACT.Identity, bias=cols[:, ds(f + C_B, 1)],
              scale=cols[:, ds(f + C_W[2], 1)]).then_inc(tap2, 1)
            act.wait_ge(tap0, n + 1)
            A(conv_t[:, j % 2, :], conv_t[:, j % 2, :], ACT.Gelu_apprx_tanh).then_inc(gelu2, 1)

        def hidden_hi(n, j):
            act.wait_ge(v_read, n + 1)
            A(a_hi[:, j, :], a_t[:, j % 2, :], ACT.Copy).then_inc(ah_ok, 1)

        for j in range(4):
            hi(slot(S_U0 + j + 1))
            conv_tap(j, j, j)
        with act.Fori(0, CHUNKS - 1) as c:
            for j in range(4):
                hi(slot(S_FF + j + 1, 12, c))
                hidden_hi(c * 4 + j, j)
            for j in range(4):
                hi(slot(S_FF + 5 + j, 12, c))
                conv_tap(c * 4 + (4 + j), c * 4 + (4 + j), j)
            for j in range(4):
                hi(slot(S_FF + 9 + j, 12, c))
        tail = S_FF + 12 * (CHUNKS - 1)
        for j in range(4):
            hi(slot(tail + j + 1))
            hidden_hi(4 * (CHUNKS - 1) + j, j)
        for j in range(4):
            if j < 3:
                hi(slot(tail + 5 + j))
            for t in range(TOK):
                act.wait_ge(dn_add, 16 * (CHUNKS - 1) + 4 * j + t + 1 + 4)
                own.link(A(sq3[:], x1[:, t, 512 * j:512 * j + 512], ACT.Square, accum_out=ss[:, 4 * j + t:4 * j + t + 1]))
            act.sem_inc(sq3_done, 1)
        act.wait_ge(sqrt_in, 3)
        A(nmx[:, 4:8], nmx[:, 0:4], ACT.Sqrt).then_inc(sqrt_out, 1)
        act.wait_ge(rs3_ok, 1)
        act.wait_ge(xg_ok, 3)
        for t in range(TOK):
            A(x1[:, t, 0:1536], x1[:, t, 0:1536], ACT.Copy, scale=rr[:, t:t + 1]).then_inc(o_act, 1)

    @block.vector
    def _(dve):
        V = nc.vector
        own = Chain(dve, dve_own)
        link = own.link

        def lo(s):
            dve.wait_ge(w_hi_done, s.n + 1)
            V.tensor_tensor(w_lo[:, s.par, :], w_raw[:, s.par, :], w_hi[:, s.par, :].bitcast(F32), ALU.subtract).then_inc(w_ready, 1)

        def rstd(total, v, t0, t1, dst, nth):
            V.tensor_scalar(v, total, 1.0 / D_MODEL, EPS, ALU.mult, ALU.add).then_inc(sqrt_in, 1)
            dve.wait_ge(sqrt_in, nth)
            dve.wait_ge(sqrt_out, nth)
            link(V.reciprocal(t0, t0))
            link(V.tensor_tensor(t1, v, t0, ALU.mult))
            link(V.tensor_tensor(t1, t1, t0, ALU.mult))
            link(V.tensor_scalar(t1, t1, -0.5, 1.5, ALU.mult, ALU.add))
            link(V.tensor_tensor(dst, t0, t1, ALU.mult))

        link(V.memset(tabx[32:33, :], NEG))
        dve.sem_inc(w_ready, 2)
        dve.wait_ge(const_in, 16 * 11)
        V.tensor_copy(ident_b[:], ident[:])
        V.tensor_copy(tri_b[:], tri32[:])
        V.memset(ones_f[:], 1.0)
        V.memset(l_cmp[:], NEG)
        dve.wait_ge(cols_t, 1)
        V.tensor_copy(cols[:], pb[2][:, 0:272]).then_inc(cols_ok, 1)
        dve.wait_ge(cols_ok, 1)
        dve.wait_ge(r_ps, 1)
        V.tensor_copy(r_sb[:, 0:512], pb[3][0:8, 0:512])
        V.tensor_copy(r_sb[:, 512:R_LEN], pb[1][0:8, 0:P]).then_inc(r_ok, 1)
        for k in range(KT):
            dve.wait_ge(xh_done, k + 1)
            V.scalar_tensor_tensor(h_lo[:, k, :], pb[4 + k % 4][:], cols[:, G_ATTN + k:G_ATTN + k + 1],
                                   h_hi[:, k, :].bitcast(F32), ALU.mult, ALU.subtract).then_inc(xl_done, 1)
        lo(slot(0))
        lo(slot(1))
        dve.wait_ge(wg_hi_ok, 1)
        V.tensor_tensor(wg_lo[:], wg_raw[:], wg_hi[:].bitcast(F32), ALU.subtract).then_inc(wg_ok, 1)
        dve.wait_ge(ss_done, TOK)
        rstd(ss[:, 0:4], ss[:, 4:8], ss[:, 8:12], ss[:, 12:16], rr[:, 0:4], 1)
        for t in range(TOK):
            if t:
                dve.wait_ge(rbc_ps, t)
            V.tensor_copy(rs_rep[:], rr[:, t:t + 1].to_broadcast([P, P])).then_inc(rep_ok, 1)
        dve.wait_ge(rbc_ps, TOK)
        V.tensor_copy(rbc[:], pb[3][:]).then_inc(rbc_ok, 1)
        dve.wait_ge(rbc_ok, 1)

        def kv_out(n, bank, after):
            dve.wait_ge(w_used, after + 3)
            V.tensor_tensor(kv_fm[:, ds(n, 1), :].rearrange("p a n -> p (a n)"), pb[bank][:], rbc[:], ALU.mult).then_inc(kv_done, 1)

        kv_out(0, 0, 0)
        lo(slot(2))
        kv_out(1, 1, 1)
        dve.wait_ge(gl_ps, 1)
        for t in range(TOK):
            last = V.tensor_scalar(gl[:, t, :], pb[2][:, t * 32:t * 32 + 32], rr[:, t:t + 1], None, ALU.mult)
        last.then_inc(gl_ok, 1)
        dve.wait_ge(gl_ok, 1)
        for t in range(TOK):
            last = V.tensor_tensor(fz[:, 2, t, :], gl[:, t, 24:32], fb[:], ALU.add)
        last.then_inc(fz_ok, 1)
        dve.wait_ge(fz_ok, 1)
        link(V.tensor_scalar(fz[:, 0], fz[:, 2], 0.0, None, ALU.min))
        dve.wait_ge(fe_ok, 1)
        V.tensor_tensor(fz[:, 2], fz[:, 1], fz[:, 0], ALU.subtract).then_inc(fl_ok, 1)
        with dve.Fori(0, 5) as i:
            for j in range(2):
                lo(slot(3 + j, 2, i))
                kv_out(i * 2 + (2 + j), j, slot(2 + j, 2, i).n)
        dve.wait_ge(fcum_ps, 1)
        V.tensor_tensor_scan(cum_f[:], ones_f[:], pb[3][0:8, :], 0.0, ALU.mult, ALU.add).then_inc(fcum_ok, 1)

        def blocks(kv):
            for g in range(GROUPS):
                src = kv_fm[:, 2 * kv + g, :]
                src = bass.AP(tensor=src.tensor, offset=src.offset, ap=[src.ap[0], [1, CMP_BLOCK], [CMP_STRIDE, N_CMP]])
                pos = cols[:, C_POS[kv]:C_POS[kv] + CMP_BLOCK].unsqueeze(2).to_broadcast([P, CMP_BLOCK, N_CMP])
                last = V.tensor_tensor(blk32[:, :, g * CP:g * CP + N_CMP], src, pos, ALU.add)
            return last

        V.memset(g4[:], 0.0)
        link(V.memset(blk32[:], 0.0))
        blocks(0).then_inc(blk_sum, 1)
        dve.wait_ge(blk_hi, 1)
        V.tensor_tensor(blkk_lo[:], blk32[:], blkk_hi[:].bitcast(F32), ALU.subtract).then_inc(blk_ok, 1)
        lo(slot(S_W1 + 1))
        dve.wait_ge(blk_ok, 1)
        blocks(1).then_inc(blk_sum, 1)
        dve.wait_ge(blk_hi, 2)
        dve.wait_ge(c_out, 16)
        V.tensor_tensor(blkv_lo[:], blk32[:], blkv_hi[:].bitcast(F32), ALU.subtract).then_inc(blk_ok, 1)
        lo(slot(S_W1 + 2))
        lo(slot(S_W1 + 3))
        lo(slot(S_QN))
        lo(slot(S_QN + 1))
        dve.wait_ge(gelu_ok, 1)
        for g in range(GROUPS):
            for t in range(TOK):
                last = V.tensor_copy(g4[:, g, t, t * CP:t * CP + CP], gv[:, g * CP:g * CP + CP])
        last.then_inc(g4_ok, 1)
        dve.wait_ge(vc_ps, 1)
        for g in range(GROUPS):
            last = V.tensor_copy(vc4[:, g].rearrange("p t d -> p (t d)"), pb[5 + g][:])
        last.then_inc(vc_ok, 1)

        def q_out(dst, bank, after, done, scale):
            dve.wait_ge(w_used, after + 3)
            if scale is None:
                V.tensor_tensor(dst, pb[bank][:], rbc[:], ALU.mult).then_inc(done, 1)
            else:
                V.scalar_tensor_tensor(dst, pb[bank][:], scale, rbc[:], ALU.mult, ALU.mult).then_inc(done, 1)

        q_out(q_n[:], 0, S_QN, q_ready, SCALE)

        def logits(lt, bias, c, ready, base, done):
            for k, i in enumerate(TILES):
                b, col = S_PLACE[i]
                n = P * (i + 1)
                hold(dve, ready, base + (3 if k == 1 else k + 1))
                V.tensor_tensor_reduce(out=lt[:, L_COL[i]:L_COL[i] + n], in0=pb[b][:, col:col + n], in1=bias(i), scale=1.0,
                                       scalar=-3.0e38, op0=ALU.add, op1=ALU.max, accum_out=mx[:, c + i:c + i + 1]).then_inc(done, 1)

        def nsa_step(s, g, it, bias_n_use, head, fill):
            dve.wait_ge(bn_loaded[g], bias_n_use * 16 + 16)
            dve.wait_ge(ns_ready, s * 9 + 1)
            for i in range(TOK):
                n = (96 + P * i) // CMP_STRIDE + 1
                start = SEQ - P - P * i + CMP_BLOCK - 1
                b = bias_n[:, g, start:start + (n - 1) * CMP_STRIDE + 1:CMP_STRIDE]
                last = V.tensor_tensor(l_cmp[:, i, 0:n], pb[g][:, CP * i:CP * i + n], b, ALU.add)
            last.then_inc(ns_read, 1)
            dve.wait_ge(ns_read, s * 9 + 19)
            link(V.tensor_reduce(mx[:, 0:4], l_cmp[:], AX.X, ALU.max))
            link(V.tensor_scalar(nmx[:, 0:4], mx[:, 0:4], -1.0e20, -1.0, ALU.max, ALU.mult))
            V.tensor_tensor(p_cmp[:], l_cmp[:], nmx[:, 0:4].unsqueeze(2).to_broadcast([P, TOK, CP]), ALU.add).then_inc(cmp_shift, 1)
            for u, lt in enumerate((l_slc, l_win)):
                logits(lt, lambda i: bias_n[:, g, SEQ - P - P * i:SEQ], 4 + 4 * u, ns_ready, s * 9 + (1 + 4 * u), ns_read)
                dve.wait_ge(ns_read, s * 9 + (23 + 4 * u))
                V.tensor_scalar(nmx[:, 4 + 4 * u:8 + 4 * u], mx[:, 4 + 4 * u:8 + 4 * u], -1.0, None, ALU.mult).then_inc(max_ready, 1)
            if fill is not None:
                lo(fill)
            for u in range(3):
                c = slice(4 * u, 4 * u + 4)
                dve.wait_ge(exp_done, s * 3 + (u + 1))
                if u == 0:
                    link(V.tensor_reduce(sm[:, 0:4], p_cmp[:], AX.X, ALU.add))
                    link(V.tensor_scalar(sm[:, 0:4], sm[:, 0:4], 1.0e-30, None, ALU.max))
                link(V.reciprocal(rr[:, c], sm[:, c]))
                V.tensor_tensor(rr[:, c], rr[:, c], gates[:, :, ds(head * 3 + u, 1)].rearrange("p t a -> p (t a)"),
                                ALU.mult).then_inc(r_ready, 1)
            if fill is not None:
                q_out(q_n[:], 1 - g, fill.n - 1, q_ready, SCALE)
            for u in range(2):
                dve.wait_ge(nt_ready, s * 6 + (3 * u + 2) + 6)
                dve.wait_ge(npv_done, s * 2 + (u + 1))
                V.tensor_copy(pt_n[:, 512:1024], pb[6][:]).then_inc(nt_dve, 1)

        dve.wait_ge(gates_ok, 1)
        with dve.Fori(0, 3) as it:
            own.enter(it, 14)
            nsa_step(it * 2, 0, it, it, it, slot(S_QN + 2, 2, it))
            nsa_step(it * 2 + 1, 1, it, it, it + 4, slot(S_QN + 3, 2, it))
        own.leave(3)
        nsa_step(6, 0, 3, 3, 3, slot(S_QN + 8))
        nsa_step(7, 1, 3, 3, 7, None)

        def merge(base, which):
            for q in range(2):
                dve.wait_ge(yh_ok, 2 * which + q + 1)
                V.tensor_tensor(y_lo[:, 4 * q:4 * q + 4, :], y32[:, 4 * q:4 * q + 4, :], y_hi[:, 4 * q:4 * q + 4, :].bitcast(F32),
                                ALU.subtract).then_inc(y_ok, 1)

            def iteration(c, per, i, nth, pairs, last):
                for pair in range(2):
                    for j in range(2):
                        s = slot(c + 3 * pair + j, per, i)
                        lo(slot(c + 3 * pair + j + 1, per, i))
                        dve.wait_ge(w_used, s.n + 3)
                        V.tensor_tensor(gate_t[:, j, :], pb[j][:], rbc[:], ALU.mult).then_inc(gate_read[which], 1)
                    s = slot(c + 3 * pair + 2, per, i)
                    lo(slot(c + 3 * pair + 3, per, i))
                    if last and pair == 1:
                        for q in range(3):
                            merged_lo(q)
                    dve.wait_ge(sig_done[which], nth + (2 * pair + 2))
                    dve.wait_ge(w_used, s.n + 3)
                    for j in range(2):
                        dst = m32[:, ds(nth + (2 * pair + j), 1), :].rearrange("p a n -> p (a n)")
                        if which == 0:
                            r = V.tensor_tensor(dst, pb[2 + j][:], gate_t[:, j, :], ALU.mult)
                        else:
                            link(V.tensor_tensor(gate_t[:, j, :], pb[2 + j][:], gate_t[:, j, :], ALU.mult))
                            r = V.tensor_tensor(dst, dst, gate_t[:, j, :], ALU.add)
                    r.then_inc(br_read[which], 1)
                    if which == 0 or True:
                        dve.wait_ge(br_read[which], pairs + (pair + 2))

            with dve.Fori(0, 3 if which else 4) as i:
                own.enter(i, 4 if which else 0)
                iteration(base, 6, i, i * 4, i * 2, False)
            own.leave(3 if which else 4)
            if which:
                iteration(base + 18, 0, None, 12, 6, True)

        def merged_lo(q):
            dve.wait_ge(mh_ok, q + 1)
            V.tensor_tensor(h_lo[:, 4 * q:4 * q + 4, :], m32[:, 4 * q:4 * q + 4, :], h_hi[:, 4 * q:4 * q + 4, :].bitcast(F32),
                            ALU.subtract).then_inc(ml_ok, 1)

        merge(S_GA, 0)

        for j in range(3):
            lo(slot(S_FOX + j + 1))
            q_out((q_f, k_f, vf_fm)[j][:], j % 2, S_FOX + j, fproj, SCALE if j == 0 else None)

        def fox_step(h, b, use, c, per, i, fill):
            dve.wait_ge(bf_loaded[b], use * 16 + 16)
            logits(l_fox, lambda t: bias_f[:, b, 0:P * (t + 1)], 4, fs_ready, h * 4, fs_read)
            dve.wait_ge(fs_read, h * 4 + 12)
            V.tensor_scalar(nmx[:, 4:8], mx[:, 4:8], -1.0, None, ALU.mult).then_inc(fmax_ready, 1)
            if fill:
                lo(slot(c + 1, per, i))
            dve.wait_ge(fexp_done, h + 1)
            V.reciprocal(rr[:, 4:8], sm[:, 4:8]).then_inc(fr_ready, 1)
            if fill:
                q_out(q_f[:], c % 2, slot(c, per, i).n, fproj, SCALE)
                lo(slot(c + 2, per, i))
            dve.wait_ge(ft_ready, h * 3 + 2)
            dve.wait_ge(fpv_done, h + 1)
            V.tensor_copy(pt_f[:, 512:1024], pb[6][:]).then_inc(ft_dve, 1)
            if fill:
                q_out(k_f[:], (c + 1) % 2, slot(c + 1, per, i).n, fproj, None)
                lo(slot(c + 3, per, i))
                q_out(vf_fm[:], c % 2, slot(c + 2, per, i).n, fproj, None)

        with dve.Fori(0, 3) as i:
            fox_step(i * 2, 0, i, S_FOX + 3, 6, i, True)
            fox_step(i * 2 + 1, 1, i, S_FOX + 6, 6, i, True)
        fox_step(6, 0, 3, S_FOX + 21, 0, None, True)
        fox_step(7, 1, 3, 0, 0, None, False)
        merge(S_GB, 1)
        merged_lo(3)

        def wo_add(g, after):
            for t in range(TOK):
                if t < TOK - 1:
                    dve.wait_ge(wo_done, g * 3 + (t + 1))
                else:
                    dve.wait_ge(w_used, after + 3)
                if t == 0:
                    dve.wait_ge(x1t_ps, g * 4 + 1)
                    dve.wait_ge(x1_put, g * 4 + 1)
                V.tensor_tensor(x1_new[:, t, :], pb[t][:], x1[:, t, ds(g * 512, 512)], ALU.add).then_inc(x1_add, 1)

        lo(slot(S_WO + 1))
        dve.wait_ge(xr_loaded, 64)
        with dve.Fori(0, 3) as g:
            for sub in range(1, 4):
                lo(slot(S_WO + sub + 1, 4, g))
            wo_add(g, slot(S_WO + 3, 4, g).n)
            lo(slot(S_WO + 5, 4, g))
        def h2_lo(q):
            dve.wait_ge(hh_ok, q + 1)
            V.tensor_tensor(h_lo[:, 4 * q:4 * q + 4, :], m32[:, 4 * q:4 * q + 4, :], h_hi[:, 4 * q:4 * q + 4, :].bitcast(F32),
                            ALU.subtract).then_inc(hl_ok, 1)
        for sub in range(1, 4):
            lo(slot(S_WO + 12 + sub + 1))
            h2_lo(sub - 1)
        wo_add(3, S_U0 - 1)
        h2_lo(3)
        dve.wait_ge(x1_put, 4 * TOK + 1)
        link(V.tensor_reduce(mx[:, 0:4], ss.rearrange("p (g t) -> p t g", t=TOK), AX.X, ALU.add))
        rstd(mx[:, 0:4], nmx[:, 0:4], nmx[:, 4:8], nmx[:, 8:12], rr[:, 0:4], 2)
        for t in range(TOK):
            last = V.tensor_copy(rs_rep2[:, t, :], rr[:, t:t + 1].to_broadcast([P, P]))
        last.then_inc(rep2_ok, 1)
        V.memset(u_pad[:, :, 0:CONV - 1], 0.0)
        lo(slot(S_U0 + 1))
        dve.wait_ge(rbc2_ps, 1)
        link(V.tensor_copy(rbc[:], pb[6][:]))
        dve.sem_inc(rbc2_ok, 1)

        def up_out(n, f, j, bank_slot):
            dve.wait_ge(w_used, bank_slot.n + 3)
            V.tensor_tensor(u_pad[:, j % 2, 2:SEQ + 2], pb[j % 2][:], rbc[:], ALU.mult).then_inc(up_read, 1)
            dve.wait_ge(up_read, n + 1)
            dve.wait_ge(tap2, n + 1)
            link(V.scalar_tensor_tensor(conv_t[:, j % 2, :], u_pad[:, j % 2, 1:SEQ + 1], cols[:, ds(f + C_W[1], 1)],
                                        conv_t[:, j % 2, :], ALU.mult, ALU.add))
            V.scalar_tensor_tensor(conv_t[:, j % 2, :], u_pad[:, j % 2, 0:SEQ], cols[:, ds(f + C_W[0], 1)],
                                   conv_t[:, j % 2, :], ALU.mult, ALU.add).then_inc(tap0, 1)

        def hidden(n, j, s, g_n):
            dve.wait_ge(w_used, s.n + 3)
            dve.wait_ge(g_ok, g_n + 1)
            V.tensor_tensor(a_t[:, j % 2, :], pb[j % 2][:], g_rs[:, j, :], ALU.mult).then_inc(v_read, 1)
            dve.wait_ge(ah_ok, n + 1)
            V.tensor_tensor(a_lo[:, j, :], a_t[:, j % 2, :], a_hi[:, j, :].bitcast(F32), ALU.subtract).then_inc(a_ok, 1)

        def down_add(c, per, i, chunk, j):
            s = slot(c + j, per, i)
            for t in range(TOK):
                if t < TOK - 1:
                    dve.wait_ge(dn_done, chunk * 12 + (3 * j + t + 1))
                else:
                    dve.wait_ge(w_used, s.n + 3)
                d = x1[:, t, 512 * j:512 * j + 512]
                V.tensor_tensor(d, pb[2 + t][:], d, ALU.add).then_inc(dn_add, 1)

        for j in range(4):
            if j:
                lo(slot(S_U0 + j + 1))
            up_out(j, j, j, slot(S_U0 + j))
        with dve.Fori(0, CHUNKS - 1) as c:
            own.enter(c, 4)
            for j in range(4):
                lo(slot(S_FF + j + 1, 12, c))
                hidden(c * 4 + j, j, slot(S_FF + j, 12, c), c * 4 + j)
            for j in range(4):
                lo(slot(S_FF + 5 + j, 12, c))
                up_out(c * 4 + (4 + j), c * 4 + (4 + j), j, slot(S_FF + 4 + j, 12, c))
            for j in range(4):
                lo(slot(S_FF + 9 + j, 12, c))
                down_add(S_FF + 8, 12, c, c, j)
        own.leave(CHUNKS - 1)
        tail = S_FF + 12 * (CHUNKS - 1)
        for j in range(4):
            lo(slot(tail + j + 1))
            hidden(4 * (CHUNKS - 1) + j, j, slot(tail + j), 4 * (CHUNKS - 1) + j)
        for j in range(4):
            if j < 3:
                lo(slot(tail + 5 + j))
            down_add(tail + 4, 0, None, CHUNKS - 1, j)
        dve.wait_ge(sq3_done, 4)
        link(V.tensor_reduce(mx[:, 0:4], ss.rearrange("p (g t) -> p t g", t=TOK), AX.X, ALU.add))
        rstd(mx[:, 0:4], nmx[:, 0:4], nmx[:, 4:8], nmx[:, 8:12], rr[:, 0:4], 3)
        dve.sem_inc(rs3_ok, 1)
        dve.wait_ge(gf_in, 16)
        for t in range(TOK):
            d = x1[:, t, 1536:2048]
            V.scalar_tensor_tensor(d, d, rr[:, t:t + 1], gfin[:, 1536:2048], ALU.mult, ALU.mult).then_inc(o_dve, 1)

    @block.gpsimd
    def _(pool):
        G = nc.gpsimd
        for s_, n in ((ns_read, 18), (nt_ready, 6), (nt_dve, 1), (npv_done, 1), (gate_read[0], 2), (gate_read[1], 2),
                      (br_read[0], 1), (br_read[1], 1), (fproj, 2), (fs_read, 8), (ft_dve, 1), (fpv_done, 1),
                      (x1t_ps, 1), (x1_put, 1), (dn_add, 4)):
            pool.sem_inc(s_, n)

        def scale(lt, c):
            for i in TILES:
                d = lt[:, L_COL[i]:L_COL[i] + P * (i + 1)]
                last = G.tensor_scalar(d, d, rr[:, c + i:c + i + 1], None, ALU.mult)
            return last

        with pool.Fori(0, HEADS) as s:
            hold(pool, r_ready, s * 3 + 1)
            G.tensor_tensor(p_cmp[:], p_cmp[:], rr[:, 0:4].unsqueeze(2).to_broadcast([P, TOK, CP]), ALU.mult).then_inc(p_ready, 1)
            hold(pool, r_ready, s * 3 + 2)
            scale(l_slc, 4).then_inc(p_ready, 1)
            hold(pool, r_ready, s * 3 + 3)
            scale(l_win, 8).then_inc(p_ready, 1)
        with pool.Fori(0, HEADS) as h:
            hold(pool, fr_ready, h + 1)
            scale(l_fox, 4).then_inc(fp_ready, 1)
        pool.wait_ge(rbc2_ok, 1)
        pool.dma_start(gfin[:], final_norm_g.rearrange("(a n) -> a n", a=1).to_broadcast([P, D_MODEL])).then_inc(gf_in, 16)

        def g_out(n, j):
            hold(pool, gelu2, n + 1)
            G.tensor_tensor(g_rs[:, j, :], conv_t[:, j % 2, :], rbc[:], ALU.mult).then_inc(g_ok, 1)

        with pool.Fori(0, CHUNKS) as c:
            for j in range(4):
                g_out(c * 4 + j, j)
        pool.wait_ge(gf_in, 16)
        for j in range(3):
            pool.wait_ge(sq3_done, j + 1)
            d = x1[:, :, 512 * j:512 * j + 512]
            g = gfin[:, 512 * j:512 * j + 512].unsqueeze(1).to_broadcast([P, TOK, 512])
            G.tensor_tensor(d, d, g, ALU.mult).then_inc(xg_ok, 1)

    ctx.close()


_INS = ['x', 'attn_norm_g', 'w_in', 'cmp_pos_k', 'cmp_w1_k', 'cmp_w2_k', 'cmp_pos_v', 'cmp_w1_v', 'cmp_w2_v',
        'rel_bias_table', 'fox_forget_bias', 'w_branch_nsa', 'w_branch_fox', 'w_out', 'ffn_norm_g', 'w_up', 'conv_w',
        'conv_b', 'w_down', 'final_norm_g']


def _constants():
    import math
    import numpy as np
    ident = np.eye(P, dtype=np.float32)
    onehot = np.zeros((REL_BUCKETS + 1, R_LEN), np.float32)
    exact = REL_BUCKETS // 2
    for j in range(R_LEN):
        dist = SEQ - 1 - j
        if dist < 0:
            onehot[REL_BUCKETS, j] = 1
        elif dist < exact:
            onehot[dist, j] = 1
        else:
            b = exact + int(math.log(dist / exact) / math.log(REL_MAX_DIST / exact) * (REL_BUCKETS - exact))
            onehot[min(b, REL_BUCKETS - 1), j] = 1
    tri = np.where(np.arange(P)[None, :] > np.arange(P)[:, None], np.float32(NEG), np.float32(0)).astype(np.float32)
    return {"c_ident": ident, "c_onehot": onehot, "c_tri": tri}


def kernel(**inputs):
    import numpy as _np
    import concourse.bacc as _bacc
    from concourse import mybir as _mybir
    from concourse.bass_utils import run_bass_kernel_spmd as _run

    nc = _bacc.Bacc("TRN2", target_bir_lowering=False, num_devices=1)
    arrays, args = {}, []
    given = {n: _np.ascontiguousarray(inputs[n]) for n in _INS}
    given.update(_constants())
    for name, a in given.items():
        arrays[f"in_{name}_dram"] = a
        args.append(nc.dram_tensor(f"in_{name}_dram", a.shape, _mybir.dt.from_np(a.dtype), kind="ExternalInput").ap())
    args.append(nc.dram_tensor("out_0_dram", (1, SEQ, D_MODEL), _mybir.dt.float32, kind="ExternalOutput").ap())
    build(nc, *args)
    r = _run(nc, [arrays], core_ids=[0])
    return r.results[0]["out_0_dram"]
```

```python
from contextlib import ExitStack
from collections import namedtuple
import concourse.bass as bass
from concourse import mybir

P = 128
SEQ, D_MODEL, D_FF = 512, 2048, 5632
HEADS, GROUPS = 8, 2
TOK = SEQ // P
KT = D_MODEL // P
CMP_BLOCK, CMP_STRIDE = 32, 16
N_CMP = SEQ // CMP_STRIDE - 1
CP = 32
NG = 32
X_COLS = 2 * CP + 2
REL_BUCKETS, REL_MAX_DIST = 32, 128
CONV = 3
EPS = 1e-6
NEG = -1e30
SCALE = float(P) ** -0.5
CHUNKS = D_FF // (4 * P)
R_LEN = SEQ + P
COL_QN, COL_KV, COL_GN = 0, 1024, 2560
COL_QF, COL_KF, COL_VF, COL_FL = 2584, 3608, 4632, 5656
COL_MA, COL_MB = 5664, 7712
S_KV = 0
S_KW = S_KV + 4
S_QN = S_KW + 12
S_GA = S_QN + 8
S_FOX = S_GA + 24
S_GB = S_FOX + 24
S_WO = S_GB + 24
S_U0 = S_WO + 16
S_FF = S_U0 + 4
S_END = S_FF + 12 * (CHUNKS - 1) + 8

TILES = [3, 2, 0, 1]
S_PLACE = {3: (2, 0), 2: (3, 0), 0: (3, 384), 1: (4, 0)}
L_COL = {3: 0, 2: 512, 0: 896, 1: 1024}
PT_COL = {0: 0, 1: 512, 3: 896, 2: 1024}
CMP_COL = 1280

Slot = namedtuple("Slot", "n half par")


def slot(c, per=0, i=None):
    if i is None:
        return Slot(c, c // 2, c % 2)
    return Slot(i * per + c, i * (per // 2) + c // 2, c % 2)


class Chain:

    def __init__(self, eng, sem):
        self.eng, self.sem, self.base, self.k, self.per, self.i = eng, sem, 0, 0, 0, None

    def link(self, ins):
        self.k += 1
        ins.then_inc(self.sem, 1)
        at = self.base + self.k
        self.eng.wait_ge(self.sem, at if self.i is None else self.i * self.per + at)

    def enter(self, i, per):
        self.base, self.k, self.i, self.per = self.base + self.k, 0, i, per

    def leave(self, count):
        assert self.k == self.per, (self.k, self.per)
        self.base, self.k, self.i = self.base + self.per * count, 0, None


def build(nc, x, attn_norm_g, w_in, cmp_pos_k, cmp_w1_k, cmp_w2_k, cmp_pos_v, cmp_w1_v, cmp_w2_v,
          rel_bias_table, fox_forget_bias, w_branch_nsa, w_branch_fox, w_out, ffn_norm_g, w_up, conv_w,
          conv_b, w_down, final_norm_g, c_ident, c_onehot, c_tri, c_sel, out):
    F32, F32R, BF16 = mybir.dt.float32, mybir.dt.float32r, mybir.dt.bfloat16
    ACT, ALU, AX = mybir.ActivationFunctionType, mybir.AluOpType, mybir.AxisListType
    ds = bass.ds
    KB = 1024
    ctx = ExitStack()
    BASE = 16512

    def at(name, off, shape, dt=F32):
        return nc.alloc_sbuf_tensor_at(name, shape, dt, offset=BASE + off)

    A_, M_, Y_ = 160 * KB, 112 * KB, 144 * KB
    h_hi = at("h_hi", 0, [P, KT, SEQ], F32R)
    h_lo = at("h_lo", 32 * KB, [P, KT, SEQ], F32R)
    w_raw = at("w_raw", 64 * KB, [P, 2, 2048])
    w_hi = at("w_hi", 80 * KB, [P, 2, 2048], F32R)
    w_lo = at("w_lo", 96 * KB, [P, 2, 2048], F32R)
    m32 = at("m32", M_, [P, KT, SEQ])
    kv_fm = at("kv_fm", M_, [P, 12, SEQ])
    bias_n = at("bias_n", M_ + 24 * KB, [P, 2, SEQ])
    q_n = at("q_n", M_ + 28 * KB, [P, SEQ])
    y32 = at("y32", Y_, [P, 8, 512])
    x_in = at("x_in", A_, [P, TOK, D_MODEL])
    wg_raw = at("wg_raw", A_ + 32 * KB, [P, KT, NG])
    wg_hi = at("wg_hi", A_ + 34 * KB, [P, KT, NG], F32R)
    wg_lo = at("wg_lo", A_ + 36 * KB, [P, KT, NG], F32R)
    ones_f = at("ones_f", A_ + 38 * KB, [8, SEQ])
    cum_f = at("cum_f", A_ + 40 * KB, [8, SEQ])
    tri32 = at("tri32", A_ + 42 * KB, [P, P])
    sq_junk = at("sq_junk", Y_, [P, D_MODEL])
    onehot = at("onehot", Y_ + 8 * KB, [33, R_LEN])
    r_sb = at("r_sb", Y_ + 8 * KB + 2560, [8, R_LEN])
    rows = at("rows", Y_ + 13 * KB, [P, 3, P])
    sel = at("sel", Y_ + 14 * KB + 512, [X_COLS, 2, GROUPS * CP])
    rs_rep = at("rs_rep", Y_, [P, TOK, P])
    gl = at("gl", A_ + 8 * KB, [NG, SEQ])
    fz = at("fz", A_ + 10 * KB, [HEADS, 3, SEQ])
    xs_hi = at("xs_hi", Y_, [P, CMP_STRIDE, X_COLS], F32R)
    xs_lo = at("xs_lo", A_, [P, CMP_STRIDE, X_COLS], F32R)
    halves = at("halves", A_ + 5 * KB, [X_COLS, 2, 2 * P])
    v_tm = at("v_tm", A_ + 8 * KB, [P, 4, TOK, P])
    w2_sb = at("w2_sb", A_ + 16 * KB, [P, 2, P])
    g4 = at("g4", A_ + 17 * KB, [P, GROUPS, TOK, P])
    vc4 = at("vc4", A_ + 21 * KB, [P, GROUPS, TOK, P])
    kc_fm = at("kc_fm", A_, [P, GROUPS * CP])
    gk = at("gk", A_ + 256, [P, GROUPS * CP])
    gv = at("gv", A_ + 512, [P, GROUPS * CP])
    l_slc = at("l_slc", A_ + 25 * KB, [P, 1280])
    p_cmp = at("p_cmp", A_ + 30 * KB, [P, TOK, CP])
    l_win = at("l_win", A_ + 30 * KB + 512, [P, 1280])
    pt_n = at("pt_n", A_ + 35 * KB + 512, [P, 1408])
    y_hi = at("y_hi", A_, [P, 8, SEQ], F32R)
    y_lo = at("y_lo", A_ + 16 * KB, [P, 8, SEQ], F32R)
    gate_t = at("gate_t", A_ + 32 * KB, [P, 2, SEQ])
    q_f = at("q_f", A_, [P, SEQ])
    k_f = at("k_f", A_ + 2 * KB, [P, SEQ])
    vf_fm = at("vf_fm", A_ + 4 * KB, [P, SEQ])
    vf_tm = at("vf_tm", A_ + 6 * KB, [P, TOK, P])
    l_fox = at("l_fox", A_ + 8 * KB, [P, 1280])
    pt_f = at("pt_f", A_ + 13 * KB, [P, 1280])
    bias_f = at("bias_f", A_ + 36 * KB, [P, 2, SEQ])
    x1 = at("x1", A_, [P, TOK, D_MODEL])
    gfin = at("gfin", A_ + 32 * KB, [P, D_MODEL])
    x1_new = at("x1_new", Y_, [P, TOK, 512])
    sq2 = at("sq2", Y_ + 8 * KB, [P, 512])
    rs_rep2 = at("rs_rep2", Y_ + 14 * KB, [P, TOK, P])
    a_hi = at("a_hi", M_, [P, 4, SEQ], F32R)
    a_lo = at("a_lo", M_ + 8 * KB, [P, 4, SEQ], F32R)
    g_rs = at("g_rs", M_ + 16 * KB, [P, 4, SEQ])
    u_pad = at("u_pad", Y_, [P, 2, SEQ + CONV - 1])
    conv_t = at("conv_t", Y_ + 4128, [P, 2, SEQ])
    a_t = at("a_t", Y_ + 4128 + 4 * KB, [P, 2, SEQ])
    sq3 = at("sq3", M_ + 24 * KB, [P, 512])
    o = 202 * KB + 512
    ident = at("ident", o, [P, P]); o += 512
    ident_b = at("ident_b", o, [P, P], BF16); o += 256
    tri_b = at("tri_b", o, [P, P], BF16); o += 256
    cols = at("cols", o, [P, 272]); o += 1088
    rbc = at("rbc", o, [P, SEQ]); o += 2048
    gates = at("gates", o, [P, TOK, 24]); o += 384
    l_cmp = at("l_cmp", o, [P, TOK, CP]); o += 512
    st = at("st", o, [P, 64]); o += 256
    assert BASE + o <= 229376
    fb = at("fb", Y_ + 15 * KB + 896, [HEADS, 1])
    tabx = at("tabx", Y_ + 15 * KB + 928, [33, 8])

    ss, mx, nmx, sm, rr = (st[:, 0:16], st[:, 16:28], st[:, 28:40], st[:, 40:52], st[:, 52:64])
    G_ATTN, G_FFN, C_B, C_W, C_POS = 0, 16, 32, [76, 120, 164], 208

    pb = [ctx.enter_context(nc.psum_tensor(f"bank{b}", [P, 512], F32)) for b in range(8)]

    r_dram = nc.dram_tensor("r_dram", [8, R_LEN], F32, kind="Internal").ap()
    e_dram = nc.dram_tensor("e_dram", [8 * P, SEQ], F32, kind="Internal").ap()
    c_dram = nc.dram_tensor("c_dram", [8, SEQ], F32, kind="Internal").ap()

    def sem(name):
        return ctx.enter_context(nc.semaphore(name))

    w_loaded = [sem("w_loaded0"), sem("w_loaded1")]
    w1_loaded = sem("w1_loaded")
    w_hi_done = sem("w_hi_done")
    w_ready = sem("w_ready")
    w_used = sem("w_used")
    dve_own, act_own = sem("dve_own"), sem("act_own")
    ident_in, const_in = sem("ident_in"), sem("const_in")
    x_loaded = [sem(f"x_loaded{c}") for c in range(4)]
    wg_loaded, misc_in, w2_in = sem("wg_loaded"), sem("misc_in"), sem("w2_in")
    cols_t, cols_ok = sem("cols_t"), sem("cols_ok")
    xt_ready, xh_done, xl_done = sem("xt_ready"), sem("xh_done"), sem("xl_done")
    r_ps, r_ok, r_out, e_out = sem("r_ps"), sem("r_ok"), sem("r_out"), sem("e_out")
    ss_done, sqrt_in, sqrt_out, rep_ok, rep_used, rbc_ps, rbc_ok = (
        sem(n) for n in ("ss_done", "sqrt_in", "sqrt_out", "rep_ok", "rep_used", "rbc_ps", "rbc_ok"))
    wg_hi_ok, wg_ok, gl_ps, gl_ok, gt_ps, gates_ok, fz_ok, fe_ok, fcum_ok, c_out = (
        sem(n) for n in ("wg_hi_ok", "wg_ok", "gl_ps", "gl_ok", "gt_ps", "gates_ok", "fz_ok", "fe_ok", "fcum_ok", "c_out"))
    kv_done = sem("kv_done")
    vt_ps, vt_ok = sem("vt_ps"), sem("vt_ok")
    xs_hi_ok, xs_ok, halves_ok, blk_ps = sem("xs_hi_ok"), sem("xs_ok"), sem("halves_ok"), sem("blk_ps")
    gelu_ok, kc_ps, kc_ok, g4_ok, vc_ps, vc_ok = (
        sem(n) for n in ("gelu_ok", "kc_ps", "kc_ok", "g4_ok", "vc_ps", "vc_ok"))
    bn_loaded = [sem("bn_loaded0"), sem("bn_loaded1")]
    q_ready = sem("q_ready")
    ns_ready, ns_read = sem("ns_ready"), sem("ns_read")
    max_ready, cmp_shift = sem("max_ready"), sem("cmp_shift")
    exp_done, r_ready, p_ready = sem("exp_done"), sem("r_ready"), sem("p_ready")
    nt_ready, nt_act, nt_dve = sem("nt_ready"), sem("nt_act"), sem("nt_dve")
    npv_done, no_read = sem("npv_done"), sem("no_read")
    yh_ok, y_ok = sem("yh_ok"), sem("y_ok")
    gate_read = [sem("gateA_read"), sem("gateB_read")]
    sig_done = [sem("sigA_done"), sem("sigB_done")]
    br_read = [sem("brA_read"), sem("brB_read")]
    bf_loaded = [sem("bf_loaded0"), sem("bf_loaded1")]
    fproj = sem("fproj")
    fs_ready, fs_read, fmax_ready, fexp_done, fr_ready, fp_ready = (
        sem(n) for n in ("fs_ready", "fs_read", "fmax_ready", "fexp_done", "fr_ready", "fp_ready"))
    fv_ps, fv_ok, ft_ready, ft_act, ft_dve, fpv_done, fo_read = (
        sem(n) for n in ("fv_ps", "fv_ok", "ft_ready", "ft_act", "ft_dve", "fpv_done", "fo_read"))
    mh_ok, ml_ok = sem("mh_ok"), sem("ml_ok")
    xr_loaded, wo_done, x1_add, x1_put, x1t_ps, x1t_read = (
        sem(n) for n in ("xr_loaded", "wo_done", "x1_add", "x1_put", "x1t_ps", "x1t_read"))
    hh_ok, hl_ok = sem("hh_ok"), sem("hl_ok")
    rep2_ok, rbc2_ps, rbc2_ok = sem("rep2_ok"), sem("rbc2_ps"), sem("rbc2_ok")
    up_read, tap2, tap0, gelu2, g_ok = (sem(n) for n in ("up_read", "tap2", "tap0", "gelu2", "g_ok"))
    v_read, ah_ok, a_ok = sem("v_read"), sem("ah_ok"), sem("a_ok")
    dn_done, dn_add = sem("dn_done"), sem("dn_add")
    gf_in, sq3_done, xg_ok, rs3_ok, o_act, o_dve, stored = (
        sem(n) for n in ("gf_in", "sq3_done", "xg_ok", "rs3_ok", "o_act", "o_dve", "stored"))

    win = w_in[0].rearrange("(k p) n -> p k n", p=P)
    wup = w_up[0].rearrange("(k p) n -> p k n", p=P)
    wbr = [w_branch_nsa[0].rearrange("(k p) n -> p k n", p=P), w_branch_fox[0].rearrange("(k p) n -> p k n", p=P)]
    wo4 = w_out[0].rearrange("(s k p) n -> s p k n", p=P, k=4)
    wdn = w_down[0].rearrange("(k p) n -> p k n", p=P)
    w1 = [w[0].rearrange("(h q j d) n -> q d h j n", d=P, h=2, q=2) for w in (cmp_w1_k, cmp_w1_v)]
    x_t = x[0].rearrange("(t p) n -> p t n", p=P)
    out_t = out[0].rearrange("(t p) n -> t p n", p=P)

    def strides(i, g):
        return kv_fm[:, ds(i * 2 + g, 1), :].rearrange("p a (c j) -> p j (a c)", j=CMP_STRIDE)

    def positions(i):
        return cols[:, ds(i * CMP_BLOCK + C_POS, CMP_BLOCK)].rearrange("p (h j) -> p j h", h=2)

    waits_met = {"sp": sem("waits_met_sp"), "dve": sem("waits_met_dve"), "pool": sem("waits_met_pool")}

    def hold(eng, on, value):
        eng.wait_ge(on, value)
        eng.sem_inc(waits_met["sp" if eng is nc.sync else "dve" if eng is nc.vector else "pool"], 1)

    block = ctx.enter_context(nc.Block())

    @block.sync
    def _(sp):
        def load(s, src, **view):
            hold(sp, w_ready, s.n + 1)
            sp.dma_start(w_raw[:, s.par, :].rearrange("p (k n) -> p k n", **view), src).then_inc(w_loaded[s.par], 16)

        def load_cols(s, src, col):
            load(s, src[:, :, ds(col, P)], n=P)

        def load_row(src, j, r0, n):
            sp.dma_start(rows[r0:r0 + n, j, :], src.rearrange("(a b) -> a b", b=P)).then_inc(const_in, 16)

        sp.dma_start(ident[:], c_ident).then_inc(ident_in, 16)
        for c in range(4):
            sp.dma_start(x_in[:, :, 512 * c:512 * c + 512], x_t[:, :, 512 * c:512 * c + 512]).then_inc(x_loaded[c], 16)
            if c == 0:
                load_row(attn_norm_g[0], 0, 0, 16)
                load_row(ffn_norm_g[0], 0, 16, 16)
                load_row(conv_b[0], 0, 32, 44)
            if c < 2:
                load_cols(slot(c), win, COL_KV + c * P)
        for c in range(2, 4):
            load_cols(slot(c), win, COL_KV + c * P)
        for kv in range(2):
            for q in range(2):
                for j in range(2):
                    load_cols(slot(S_KW + 6 * kv + 3 * q + j), win, COL_KV + (4 + 4 * kv + 2 * q + j) * P)
                s = slot(S_KW + 6 * kv + 3 * q + 2)
                hold(sp, w_ready, s.n + 1)
                for half, done in ((0, w1_loaded), (1, w_loaded[s.par])):
                    sp.dma_start(w_raw[:, s.par, 1024 * half:1024 * half + 1024].rearrange("p (j n) -> p j n", n=P),
                                 w1[kv][q, :, half]).then_inc(done, 16)
        load_cols(slot(S_QN), win, COL_QN)
        sp.wait_ge(e_out, 16)

        def load_bias_n(s, b, it):
            hold(sp, ns_read, s * 9 + 9)
            head = b * 4 + it
            sp.dma_start(bias_n[:, b, :], e_dram[ds(head * P, P), :]).then_inc(bn_loaded[b], 16)

        load_bias_n(0, 0, 0)
        with sp.Fori(0, 3) as it:
            load_cols(slot(S_QN + 1, 2, it), win, it * P + (COL_QN + 4 * P))
            load_bias_n(it * 2 + 1, 1, it)
            load_cols(slot(S_QN + 2, 2, it), win, it * P + (COL_QN + P))
            load_bias_n(it * 2 + 2, 0, it + 1)
        load_cols(slot(S_QN + 7), win, COL_QN + 7 * P)
        load_bias_n(7, 1, 3)

        def load_merge(base, col, which):
            with sp.Fori(0, 4) as i:
                for pair in range(2):
                    for j in range(2):
                        load_cols(slot(base + 3 * pair + j, 6, i), win, i * (4 * P) + (col + (2 * pair + j) * P))
                    load(slot(base + 3 * pair + 2, 6, i), wbr[which][:, :, ds(i * (4 * P) + 2 * pair * P, 2 * P)], n=2 * P)

        load_merge(S_GA, COL_MA, 0)

        def load_bias_f(h, b):
            hold(sp, fs_read, h * 4 + 1)
            sp.dma_start(bias_f[:, b, :], c_dram[ds(h, 1), :].to_broadcast([P, SEQ])).then_inc(bf_loaded[b], 16)

        for j, col in enumerate((COL_QF, COL_KF, COL_VF)):
            load_cols(slot(S_FOX + j), win, col)
        sp.wait_ge(c_out, 16)
        load_bias_f(0, 0)

        def load_head(c, per, i, h, b):
            for j, col in enumerate((COL_QF, COL_KF, COL_VF)):
                load_cols(slot(c + j, per, i), win, h * P + col)
            load_bias_f(h, b)

        with sp.Fori(0, 3) as i:
            load_head(S_FOX + 3, 6, i, i * 2 + 1, 1)
            load_head(S_FOX + 6, 6, i, i * 2 + 2, 0)
        load_head(S_FOX + 21, 0, None, 7, 1)
        load_merge(S_GB, COL_MB, 1)
        with sp.Fori(0, 4) as i:
            for s4 in range(4):
                load(slot(S_WO + s4, 4, i), wo4[s4][:, :, ds(i * 512, 512)], n=512)
        for j in range(4):
            load_cols(slot(S_U0 + j), wup, j * P)
        with sp.Fori(0, CHUNKS - 1) as c:
            for j in range(4):
                load_cols(slot(S_FF + j, 12, c), wup, c * 512 + (D_FF + j * P))
            for j in range(4):
                load_cols(slot(S_FF + 4 + j, 12, c), wup, c * 512 + (512 + j * P))
            for j in range(4):
                load(slot(S_FF + 8 + j, 12, c), wdn[:, ds(c * 4, 4), 512 * j:512 * j + 512], n=512)
        last = S_FF + 12 * (CHUNKS - 1)
        for j in range(4):
            load_cols(slot(last + j), wup, 2 * D_FF - 512 + j * P)
        for j in range(4):
            load(slot(last + 4 + j), wdn[:, 4 * (CHUNKS - 1):4 * CHUNKS, 512 * j:512 * j + 512], n=512)
        for t in range(TOK):
            sp.wait_ge(o_act, t + 1)
            sp.wait_ge(o_dve, t + 1)
            sp.dma_start(out_t[t], x1[:, t, :]).then_inc(stored, 16)
        sp.wait_ge(stored, 16 * TOK)

    @block.tensor
    def _(pe):
        mm = nc.tensor.matmul
        pe.sem_inc(w_used, 2)

        def three(dst, l_hi, l_lo, r_hi, r_lo, first, final):
            mm(dst, l_hi, r_hi, start=first, stop=False)
            mm(dst, l_hi, r_lo, start=False, stop=False)
            return mm(dst, l_lo, r_hi, start=False, stop=final)

        def slot_cols(s, bank, ks=range(KT)):
            if ks[0] == 0:
                pe.wait_ge(w_ready, s.n + 3)
            for k in ks:
                w = slice(k * P, k * P + P)
                last = three(pb[bank][:], w_hi[:, s.par, w], w_lo[:, s.par, w], h_hi[:, k, :], h_lo[:, k, :],
                             k == 0, k == KT - 1)
            if ks[-1] == KT - 1:
                last.then_inc(w_used, 1)

        def slot_tokens(s, banks, k0, n_k, a, b, first, final, done, free=None):
            pe.wait_ge(w_ready, s.n + 3)
            for t in range(TOK):
                if free is not None:
                    pe.wait_ge(*free(t))
                for k in range(4):
                    w = slice(k * 512, k * 512 + 512)
                    tk = slice(t * P, t * P + P)
                    last = three(pb[banks + t][:], a[:, k0 + k, tk], b[:, k0 + k, tk], w_hi[:, s.par, w],
                                 w_lo[:, s.par, w], first and k == 0, final and k == 3)
                if final and t < TOK - 1:
                    last.then_inc(done, 1)
            last.then_inc(w_used, 1)

        pe.wait_ge(ident_in, 16)
        for _ in range(10):
            mm(pb[7][:, 0:P], ident[:], ident[:], start=True, stop=True)
        pe.wait_ge(const_in, 16 * 7)
        for j, (c, n) in enumerate(((0, 120), (120, 88), (208, 64))):
            last = nc.tensor.transpose(pb[2][:, c:c + n], rows[0:n, j, :], ident[0:n, 0:n])
        last.then_inc(cols_t, 1)

        def transpose_x(k):
            pe.wait_ge(x_loaded[k // 4], 16)
            if k >= 4:
                pe.wait_ge(xl_done, k - 3)
            for t in range(TOK):
                last = nc.tensor.transpose(pb[4 + k % 4][:, t * P:t * P + P], x_in[:, t, k * P:k * P + P], ident[:])
            last.then_inc(xt_ready, 1)

        for k in range(3):
            transpose_x(k)
        for k in range(KT + 8):
            if k + 3 < KT:
                transpose_x(k + 3)
            if k < KT:
                pe.wait_ge(xl_done, k + 1)
                slot_cols(slot(0), 0, [k])
            if k >= 8:
                slot_cols(slot(1), 1, [k - 8])
            if k == 12:
                pe.wait_ge(misc_in, 48)
                pe.wait_ge(dve_own, 1)
                pe.wait_ge(cols_ok, 1)
                mm(pb[3][0:8, 0:512], tabx[:], onehot[:, 0:512], start=True, stop=True)
                mm(pb[2][0:8, 0:P], tabx[:], onehot[:, 512:R_LEN], start=True, stop=True).then_inc(r_ps, 1)
        pe.wait_ge(r_ok, 1)
        pe.wait_ge(rep_ok, 1)
        for t in range(TOK):
            last = mm(pb[3][:, t * P:t * P + P], rs_rep[:, t, :], ident[:], start=True, stop=True)
        last.then_inc(rbc_ps, 1)
        pe.wait_ge(wg_ok, 1)
        for k in range(KT):
            last = three(pb[2][0:NG, :], wg_hi[:, k, :], wg_lo[:, k, :], h_hi[:, k, :], h_lo[:, k, :], k == 0, k == KT - 1)
        last.then_inc(gl_ps, 1)
        for j in range(2):
            pe.wait_ge(kv_done, j + 1)
            slot_cols(slot(2 + j), j)
        pe.wait_ge(gl_ok, 1)
        pe.wait_ge(rbc_ok, 1)
        for t in range(TOK):
            last = nc.tensor.transpose(pb[3][:, t * NG:t * NG + NG], gl[:, t * P:t * P + P], ident[0:NG, 0:NG])
        last.then_inc(gt_ps, 1)
        with pe.Fori(0, 2) as i:
            for q in range(2):
                for j in range(2):
                    pe.wait_ge(kv_done, i * 4 + (3 + 2 * q + j))
                    slot_cols(slot(S_KW + 3 * q + j, 6, i), j)
                s = slot(S_KW + 3 * q + 2, 6, i)
                pe.wait_ge(w_ready, s.n + 3)
                if q == 0:
                    pe.wait_ge(xs_ok, i + 1)
                    pe.wait_ge(halves_ok, i + 1)
                wh, wl = (w[:, s.par, :].rearrange("p (h j n) -> p j h n", h=2, n=P) for w in (w_hi, w_lo))
                for j in range(8):
                    last = three(pb[2][0:X_COLS, 0:2 * P].rearrange("p (h n) -> p h n", h=2), xs_hi[:, 8 * q + j, :], xs_lo[:, 8 * q + j, :],
                                 wh[:, j], wl[:, j], q == 0 and j == 0, q == 1 and j == 7)
                last.then_inc(w_used, 1)
        pe.wait_ge(kv_done, 12)
        for v, src in enumerate((6, 7, 10, 11)):
            for j in range(TOK):
                last = nc.tensor.transpose(pb[4 + v][:, j * P:j * P + P], kv_fm[:, src, j * P:j * P + P], ident[:])
            last.then_inc(vt_ps, 1)
        pe.wait_ge(halves_ok, 3)
        pe.wait_ge(gates_ok, 1)
        for kv in range(2):
            for half in range(2):
                last = mm(pb[3][:, kv * 64:kv * 64 + 64], halves[:, kv, half * P:half * P + P], sel[:, half, :],
                          start=half == 0, stop=half == 1)
        last.then_inc(blk_ps, 1)
        slot_cols(slot(S_QN), 0)
        pe.wait_ge(gelu_ok, 1)
        pe.wait_ge(w2_in, 32)
        mm(pb[2][:, 0:64], w2_sb[:, 0, :], gk[:], start=True, stop=True).then_inc(kc_ps, 1)
        pe.wait_ge(g4_ok, 1)
        pe.wait_ge(vt_ok, 4)
        for g in range(GROUPS):
            for t in range(TOK):
                last = mm(pb[5 + g][:, t * P:t * P + P], g4[:, g, t, :], w2_sb[:, 1, :], start=True, stop=True)
        last.then_inc(vc_ps, 1)
        pe.wait_ge(kc_ok, 1)
        pe.wait_ge(vc_ok, 1)

        def scores(i, q, k, bias_mm):
            b, c = S_PLACE[i]
            dst = pb[b][:, c:c + P * (i + 1)]
            last = mm(dst, q[:, i * P:i * P + P], k[:, 0:P * (i + 1)], start=True, stop=not bias_mm)
            if bias_mm:
                last = mm(pb[b][:, c + P * i:c + P * i + P], ident_b[:], tri_b[:], start=False, stop=True)
            return last

        def transposes(js, bank, lt):
            for j in js:
                c = PT_COL[j] - PT_COL[js[0]]
                for i in range(j, TOK):
                    last = nc.tensor.transpose(pb[bank][:, c + (i - j) * P:c + (i - j) * P + P],
                                               lt[:, L_COL[i] + j * P:L_COL[i] + j * P + P], ident[:])
            return last

        def weigh(j, v, pt, first, final):
            return mm(pb[7][:, j * P:SEQ], v[:, j, :], pt[:, PT_COL[j]:PT_COL[j] + SEQ - j * P], start=first, stop=final)

        def nsa_step(s, g, filler):
            pe.wait_ge(q_ready, s + 1)
            pe.wait_ge(ns_read, s * 9 + 18)
            for i in range(TOK):
                last = mm(pb[g][:, CP * i:CP * i + CP], q_n[:, i * P:i * P + P], kc_fm[:, g * CP:g * CP + CP],
                          start=True, stop=True)
            last.then_inc(ns_ready, 1)
            for u, kind in enumerate((4, 8)):
                for k, i in enumerate(TILES):
                    if u == 1:
                        pe.wait_ge(ns_read, s * 9 + (18 + 2 + max(k, 2) if k else 18 + 2))
                    scores(i, q_n, kv_fm[:, kind + g, :], False).then_inc(ns_ready, 1)
            if filler is not None:
                slot_cols(filler, 1 - g)
            for u in range(2):
                lt = (l_slc, l_win)[u]
                pe.wait_ge(p_ready, s * 3 + (2 if u == 0 else 3))
                pe.wait_ge(nt_act, s * 4 + (2 * u + 2))
                transposes([0], 5, lt).then_inc(nt_ready, 1)
                pe.wait_ge(nt_dve, s * 2 + (u + 1))
                transposes([1, 3], 6, lt).then_inc(nt_ready, 1)
                pe.wait_ge(nt_act, s * 4 + (2 * u + 3))
                last = transposes([2], 5, lt)
                if u == 0:
                    last = nc.tensor.transpose(pb[5][:, 256:384], p_cmp[:].rearrange("p t c -> p (t c)"), ident[:])
                last.then_inc(nt_ready, 1)
                if u == 0:
                    pe.wait_ge(no_read, s + 1)
                v = v_tm[:, 2 * u + g]
                weigh(0, v, pt_n, u == 0, False)
                pe.wait_ge(nt_dve, s * 2 + (u + 2))
                weigh(1, v, pt_n, False, False)
                weigh(3, v, pt_n, False, False)
                pe.wait_ge(nt_act, s * 4 + (2 * u + 4))
                last = weigh(2, v, pt_n, False, u == 1)
                if u == 0:
                    for i in range(TOK):
                        last = mm(pb[7][:, i * P:i * P + P], vc4[:, g, i, :], pt_n[:, CMP_COL:CMP_COL + P], start=False, stop=False)
                last.then_inc(npv_done, 1)

        with pe.Fori(0, 3) as it:
            nsa_step(it * 2, 0, slot(S_QN + 1, 2, it))
            nsa_step(it * 2 + 1, 1, slot(S_QN + 2, 2, it))
        nsa_step(6, 0, slot(S_QN + 7))
        nsa_step(7, 1, slot(S_GA))

        def merge(base, which):
            def iteration(c, per, i, nth, pairs, more):
                for pair in range(2):
                    for j in range(1 - pair, 2):
                        pe.wait_ge(gate_read[which], nth + (2 * pair + j + 1))
                        slot_cols(slot(c + 3 * pair + j, per, i), j)
                    s = slot(c + 3 * pair + 2, per, i)
                    pe.wait_ge(w_ready, s.n + 3)
                    pe.wait_ge(y_ok, 2 * which + 2)
                    pe.wait_ge(br_read[which], pairs + (pair + 1))
                    for j in range(2):
                        for k in range(8):
                            w = slice(k * 2 * P + j * P, k * 2 * P + j * P + P)
                            last = three(pb[2 + j][:], w_hi[:, s.par, w], w_lo[:, s.par, w], y_hi[:, k, :], y_lo[:, k, :],
                                         k == 0, k == 7)
                    last.then_inc(w_used, 1)
                if more:
                    pe.wait_ge(gate_read[which], nth + 5)
                    slot_cols(slot(c + 6, per, i), 0)

            with pe.Fori(0, 3 if which else 4) as i:
                iteration(base, 6, i, i * 4, i * 2, True)
            if which:
                iteration(base + 18, 0, None, 12, 6, False)

        merge(S_GA, 0)

        def fox_slot(s, m, bank):
            pe.wait_ge(fproj, m + 1)
            slot_cols(s, bank)

        pe.wait_ge(gate_read[0], 18)
        for j in range(1, 3):
            fox_slot(slot(S_FOX + j), j, j % 2)

        def fox_step(h, c, per, i, fill):
            pe.wait_ge(fproj, h * 3 + 4)
            for k, t in enumerate(TILES):
                pe.wait_ge(fs_read, h * 4 + (7 if k == 1 else 5 + k))
                if k == 3:
                    pe.wait_ge(fv_ok, h + 1)
                scores(t, q_f, k_f, True).then_inc(fs_ready, 1)
            fox_slot(slot(c, per, i), h * 3 + 3, c % 2)
            pe.wait_ge(fproj, h * 3 + 5)
            pe.wait_ge(fs_read, h * 4 + 12)
            for j in range(TOK):
                last = nc.tensor.transpose(pb[4][:, j * P:j * P + P], vf_fm[:, j * P:j * P + P], ident[:])
            last.then_inc(fv_ps, 1)
            pe.wait_ge(fp_ready, h + 1)
            pe.wait_ge(ft_act, h * 2 + 2)
            transposes([0], 5, l_fox).then_inc(ft_ready, 1)
            pe.wait_ge(ft_dve, h + 1)
            transposes([1, 3], 6, l_fox).then_inc(ft_ready, 1)
            pe.wait_ge(ft_act, h * 2 + 3)
            transposes([2], 5, l_fox).then_inc(ft_ready, 1)
            if fill > 1:
                fox_slot(slot(c + 1, per, i), h * 3 + 4, (c + 1) % 2)
            pe.wait_ge(fo_read, h + 1)
            pe.wait_ge(fv_ok, h + 2)
            weigh(0, vf_tm, pt_f, True, False)
            pe.wait_ge(ft_dve, h + 2)
            weigh(1, vf_tm, pt_f, False, False)
            weigh(3, vf_tm, pt_f, False, False)
            pe.wait_ge(ft_act, h * 2 + 4)
            weigh(2, vf_tm, pt_f, False, True).then_inc(fpv_done, 1)
            if fill > 1:
                fox_slot(slot(c + 2, per, i), h * 3 + 5, c % 2)

        with pe.Fori(0, 3) as i:
            fox_step(i * 2, S_FOX + 3, 6, i, 3)
            fox_step(i * 2 + 1, S_FOX + 6, 6, i, 3)
        fox_step(6, S_FOX + 21, 0, None, 3)
        fox_step(7, S_GB, 0, None, 1)
        merge(S_GB, 1)

        def wo_slot(c, per, i, sub, free):
            slot_tokens(slot(c, per, i), 0, 4 * sub, 4, h_hi, h_lo, sub == 0, sub == 3, wo_done, free)

        def x1_transposes(g):
            pe.wait_ge(x1_add, g * 4 + 4)
            for k in range(4):
                pe.wait_ge(x1t_read, g * 4 + (k + 1))
                for t in range(TOK):
                    last = nc.tensor.transpose(pb[4 + k][:, t * P:t * P + P], x1_new[:, t, k * P:k * P + P], ident[:])
                last.then_inc(x1t_ps, 1)

        pe.wait_ge(ml_ok, 1)
        wo_slot(S_WO, 0, None, 0, lambda t: (br_read[1], 8 if t < 2 else 9))
        pe.wait_ge(ml_ok, 4)
        with pe.Fori(0, 3) as g:
            for sub in range(1, 4):
                wo_slot(S_WO + sub, 4, g, sub, None)
            wo_slot(S_WO + 4, 4, g, 0, lambda t: (x1_add, g * 4 + (t + 1)))
            x1_transposes(g)
        for sub in range(1, 4):
            wo_slot(S_WO + 12 + sub, 0, None, sub, None)

        pe.wait_ge(hl_ok, 3)
        s0 = slot(S_U0)
        pe.wait_ge(x1_add, 14)
        slot_cols(s0, 0, range(0, 12))
        x1_transposes(3)
        pe.wait_ge(hl_ok, 4)
        slot_cols(s0, 0, range(12, KT))
        slot_cols(slot(S_U0 + 1), 1)
        pe.wait_ge(rep2_ok, 1)
        pe.wait_ge(x1t_read, 20)
        for t in range(TOK):
            last = mm(pb[6][:, t * P:t * P + P], rs_rep2[:, t, :], ident[:], start=True, stop=True)
        last.then_inc(rbc2_ps, 1)
        for j in (2, 3):
            pe.wait_ge(up_read, j - 1)
            slot_cols(slot(S_U0 + j), j % 2)

        def v_slots(c, per, i, u_n):
            for j in range(4):
                if j < 2:
                    pe.wait_ge(up_read, u_n + (3 + j))
                else:
                    pe.wait_ge(v_read, u_n + (j - 1))
                slot_cols(slot(c + j, per, i), j % 2)

        def down_slots(c, per, i, chunk):
            for j in range(4):
                if j == 0:
                    pe.wait_ge(a_ok, chunk * 4 + 4)
                slot_tokens(slot(c + j, per, i), 2, 0, 4, a_hi, a_lo, True, True, dn_done, lambda t: (dn_add, chunk * 16 + (4 * j + t + 1)))

        pe.wait_ge(x1_add, 16)
        with pe.Fori(0, CHUNKS - 1) as c:
            v_slots(S_FF, 12, c, c * 4)
            for j in range(4):
                if j < 2:
                    pe.wait_ge(v_read, c * 4 + (3 + j))
                else:
                    pe.wait_ge(up_read, c * 4 + (4 + j - 1))
                slot_cols(slot(S_FF + 4 + j, 12, c), j % 2)
            down_slots(S_FF + 8, 12, c, c)
        tail = S_FF + 12 * (CHUNKS - 1)
        v_slots(tail, 0, None, 4 * (CHUNKS - 1))
        down_slots(tail + 4, 0, None, CHUNKS - 1)

    @block.scalar
    def _(act):
        A = nc.scalar.activation
        own = Chain(act, act_own)

        def hi(s):
            act.wait_ge(w_loaded[s.par], s.half * 16 + 16)
            act.wait_ge(w_used, s.n + 1)
            A(w_hi[:, s.par, :], w_raw[:, s.par, :], ACT.Copy).then_inc(w_hi_done, 1)

        act.dma_start(rows[76:120, 0, :], conv_w[0, 0].rearrange("(a b) -> a b", b=P)).then_inc(const_in, 16)
        act.dma_start(rows[0:88, 1, :], conv_w[0, 1:3].rearrange("c (a b) -> (c a) b", b=P)).then_inc(const_in, 16)
        act.dma_start(rows[0:32, 2, :], cmp_pos_k[0]).then_inc(const_in, 16)
        act.dma_start(rows[32:64, 2, :], cmp_pos_v[0]).then_inc(const_in, 16)
        act.wait_ge(cols_ok, 1)
        for k in range(KT):
            act.wait_ge(xt_ready, k + 1)
            A(h_hi[:, k, :], pb[4 + k % 4][:], ACT.Copy, scale=cols[:, G_ATTN + k:G_ATTN + k + 1]).then_inc(xh_done, 1)
            if k in (2, 8):
                hi(slot(k // 8))
        for t in range(TOK):
            if t:
                act.wait_ge(ss_done, t)
            A(sq_junk[:], x_in[:, t, :], ACT.Square, accum_out=ss[:, t:t + 1]).then_inc(ss_done, 1)
        act.wait_ge(sqrt_in, 1)
        A(ss[:, 8:12], ss[:, 4:8], ACT.Sqrt).then_inc(sqrt_out, 1)
        act.wait_ge(wg_loaded, 64)
        A(wg_hi[:], wg_raw[:], ACT.Copy).then_inc(wg_hi_ok, 1)
        act.wait_ge(r_ok, 1)
        act.dma_start(r_dram, r_sb[:]).then_inc(r_out, 16)
        hi(slot(2))
        act.wait_ge(r_out, 16)
        act.dma_start(e_dram.rearrange("(h p) c -> h p c", p=P),
                      bass.AP(tensor=r_dram.tensor, offset=P - 1, ap=[[R_LEN, HEADS], [-1, P], [1, SEQ]])).then_inc(e_out, 16)
        act.wait_ge(fz_ok, 1)
        own.link(A(fz[:, 1], fz[:, 2], ACT.Abs))
        own.link(A(fz[:, 1], fz[:, 1], ACT.Exp, scale=-1.0))
        A(fz[:, 1], fz[:, 1], ACT.Ln, bias=1.0).then_inc(fe_ok, 1)
        hi(slot(3))
        act.wait_ge(fcum_ok, 1)
        act.dma_start(c_dram, cum_f[:]).then_inc(c_out, 16)
        hi(slot(S_KW))
        act.wait_ge(gt_ps, 1)
        A(gates[:], pb[3][:, 0:TOK * NG].rearrange("p (t n) -> p t n", n=NG)[:, :, HEADS:NG], ACT.Sigmoid).then_inc(gates_ok, 1)
        with act.Fori(0, 2) as i:
            hi(slot(S_KW + 1, 6, i))
            act.wait_ge(kv_done, i * 2 + 2)
            act.wait_ge(w_used, i * 6 + (S_KW - 1 + 3))
            for g in range(GROUPS):
                A(xs_hi[:, :, g * CP:g * CP + CP], strides(i, g), ACT.Copy)
            A(xs_hi[:, :, 2 * CP:X_COLS], positions(i), ACT.Copy).then_inc(xs_hi_ok, 1)
            for j in range(2, 7):
                if j in (2, 5):
                    act.wait_ge(w1_loaded, i * 32 + (16 if j == 2 else 32))
                hi(slot(S_KW + j, 6, i))
        act.dma_start(w2_sb[:, 0, :], cmp_w2_k[0]).then_inc(w2_in, 16)
        act.dma_start(w2_sb[:, 1, :], cmp_w2_v[0]).then_inc(w2_in, 16)
        act.wait_ge(blk_ps, 1)
        A(gv[:], pb[3][:, 64:128], ACT.Gelu_apprx_tanh)
        A(gk[:], pb[3][:, 0:64], ACT.Gelu_apprx_tanh).then_inc(gelu_ok, 1)
        hi(slot(S_QN + 1))
        for v in range(4):
            act.wait_ge(vt_ps, v + 1)
            A(v_tm[:, v].rearrange("p j d -> p (j d)"), pb[4 + v][:], ACT.Copy).then_inc(vt_ok, 1)
        act.wait_ge(kc_ps, 1)
        A(kc_fm[:], pb[2][:, 0:64], ACT.Copy).then_inc(kc_ok, 1)

        def exps(lt, c):
            for i in TILES:
                cols_ = slice(L_COL[i], L_COL[i] + P * (i + 1))
                last = A(lt[:, cols_], lt[:, cols_], ACT.Exp, bias=nmx[:, c + i:c + i + 1], accum_out=sm[:, c + i:c + i + 1])
            return last

        def nsa_step(s, head, fill):
            hi(fill)
            act.wait_ge(cmp_shift, s + 1)
            A(p_cmp[:], p_cmp[:], ACT.Exp).then_inc(exp_done, 1)
            act.wait_ge(max_ready, s * 2 + 1)
            exps(l_slc, 4).then_inc(exp_done, 1)
            act.wait_ge(max_ready, s * 2 + 2)
            exps(l_win, 8).then_inc(exp_done, 1)
            for u in range(2):
                act.wait_ge(nt_ready, s * 6 + (3 * u + 1) + 6)
                act.wait_ge(npv_done, s * 2 + (u + 1))
                A(pt_n[:, 0:512], pb[5][:], ACT.Copy).then_inc(nt_act, 1)
                act.wait_ge(nt_ready, s * 6 + (3 * u + 3) + 6)
                n = 384 if u == 0 else 256
                A(pt_n[:, 1024:1024 + n], pb[5][:, 0:n], ACT.Copy).then_inc(nt_act, 1)
            act.wait_ge(npv_done, s * 2 + 3)
            A(y32[:, ds(head, 1), :].rearrange("p a n -> p (a n)"), pb[7][:], ACT.Copy).then_inc(no_read, 1)

        act.sem_inc(nt_act, 2)
        act.sem_inc(no_read, 1)
        with act.Fori(0, 3) as it:
            nsa_step(it * 2, it, slot(S_QN + 2, 2, it))
            nsa_step(it * 2 + 1, it + 4, slot(S_QN + 3, 2, it))
        nsa_step(6, 3, slot(S_QN + 8))
        nsa_step(7, 7, slot(S_GA + 1))

        def merge(base, which):
            def iteration(c, per, i, count, last):
                for pair in range(2):
                    for j in range(2):
                        act.wait_ge(gate_read[which], count + (2 * pair + j + 3))
                        A(gate_t[:, j, :], gate_t[:, j, :], ACT.Sigmoid).then_inc(sig_done[which], 1)
                        hi(slot(c + 3 * pair + j + 2, per, i))
                    if last and pair == 1:
                        for q in range(3):
                            merged_hi(q)
                    hi(slot(c + 3 * pair + 4, per, i))

            if which == 0:
                act.wait_ge(npv_done, 2 * HEADS + 1)
                act.wait_ge(no_read, HEADS + 1)
            else:
                act.wait_ge(fpv_done, HEADS + 1)
                act.wait_ge(fo_read, HEADS + 1)
            for q in range(2):
                A(y_hi[:, 4 * q:4 * q + 4, :], y32[:, 4 * q:4 * q + 4, :], ACT.Copy).then_inc(yh_ok, 1)
            with act.Fori(0, 3 if which else 4) as i:
                iteration(base, 6, i, i * 4, False)
            if which:
                iteration(base + 18, 0, None, 12, True)
                merged_hi(3)

        def merged_hi(q):
            act.wait_ge(br_read[1], 8 if q < 3 else 9)
            A(h_hi[:, 4 * q:4 * q + 4, :], m32[:, 4 * q:4 * q + 4, :], ACT.Copy).then_inc(mh_ok, 1)

        merge(S_GA, 0)
        act.sem_inc(ft_act, 2)
        act.sem_inc(fo_read, 1)
        act.sem_inc(fv_ok, 1)

        for j in range(1, 3):
            hi(slot(S_FOX + j + 1))

        def fox_step(h, c, per, i, fill):
            hi(slot(c + 1, per, i))
            act.wait_ge(fmax_ready, h + 1)
            exps(l_fox, 4).then_inc(fexp_done, 1)
            act.wait_ge(fv_ps, h + 1)
            act.wait_ge(fpv_done, h + 1)
            A(vf_tm[:].rearrange("p j d -> p (j d)"), pb[4][:], ACT.Copy).then_inc(fv_ok, 1)
            act.wait_ge(ft_ready, h * 3 + 1)
            A(pt_f[:, 0:512], pb[5][:], ACT.Copy).then_inc(ft_act, 1)
            act.wait_ge(ft_ready, h * 3 + 3)
            A(pt_f[:, 1024:1280], pb[5][:, 0:256], ACT.Copy).then_inc(ft_act, 1)
            if fill > 1:
                hi(slot(c + 2, per, i))
                hi(slot(c + 3, per, i))
            act.wait_ge(fpv_done, h + 2)
            A(y32[:, ds(h, 1), :].rearrange("p a n -> p (a n)"), pb[7][:], ACT.Copy).then_inc(fo_read, 1)

        with act.Fori(0, 3) as i:
            fox_step(i * 2, S_FOX + 3, 6, i, 3)
            fox_step(i * 2 + 1, S_FOX + 6, 6, i, 3)
        fox_step(6, S_FOX + 21, 0, None, 3)
        fox_step(7, S_GB, 0, None, 1)
        merge(S_GB, 1)
        act.wait_ge(w_used, S_WO + 2)
        for c in range(4):
            act.dma_start(x1[:, :, 512 * c:512 * c + 512], x_t[:, :, 512 * c:512 * c + 512]).then_inc(xr_loaded, 16)

        def wo_out(g):
            for t in range(TOK):
                act.wait_ge(x1_add, g * 4 + (t + 1))
                own.link(A(sq2[:], x1_new[:, t, :], ACT.Square, accum_out=x1_ss(g, t)))
                A(x1[:, t, ds(g * 512, 512)], x1_new[:, t, :], ACT.Copy).then_inc(x1_put, 1)

        def x1_ss(g, t):
            return ssq[:, ds(g * 4 + t, 1)] if not isinstance(g, int) else ssq[:, 4 * g + t:4 * g + t + 1]

        def wo_trans(g):
            for k in range(4):
                act.wait_ge(x1t_ps, g * 4 + (k + 2))
                A(m32[:, ds(g * 4 + k, 1), :].rearrange("p a n -> p (a n)"), pb[4 + k][:], ACT.Copy,
                  scale=cols[:, ds(g * 4 + (G_FFN + k), 1)]).then_inc(x1t_read, 1)

        ssq = ss
        act.sem_inc(x1t_read, 4)
        with act.Fori(0, 3) as g:
            own.enter(g, 4)
            for sub in range(1, 4):
                hi(slot(S_WO + sub + 1, 4, g))
            wo_out(g)
            hi(slot(S_WO + 5, 4, g))
            wo_trans(g)
        own.leave(3)
        for sub in range(1, 4):
            hi(slot(S_WO + 12 + sub + 1))
            act.wait_ge(x1t_read, 16)
            A(h_hi[:, 4 * sub - 4:4 * sub, :], m32[:, 4 * sub - 4:4 * sub, :], ACT.Copy).then_inc(hh_ok, 1)
        wo_out(3)
        wo_trans(3)
        act.wait_ge(x1t_read, 20)
        act.wait_ge(w_used, S_U0 + 2)
        A(h_hi[:, 12:16, :], m32[:, 12:16, :], ACT.Copy).then_inc(hh_ok, 1)
        act.wait_ge(sqrt_in, 2)
        A(nmx[:, 4:8], nmx[:, 0:4], ACT.Sqrt).then_inc(sqrt_out, 1)

        def conv_tap(n, f, j):
            if not isinstance(n, int) or n >= 2:
                act.wait_ge(g_ok, n - 1)
            act.wait_ge(up_read, n + 1)
            A(conv_t[:, j % 2, :], u_pad[:, j % 2, 2:SEQ + 2], ACT.Identity, bias=cols[:, ds(f + C_B, 1)],
              scale=cols[:, ds(f + C_W[2], 1)]).then_inc(tap2, 1)
            act.wait_ge(tap0, n + 1)
            A(conv_t[:, j % 2, :], conv_t[:, j % 2, :], ACT.Gelu_apprx_tanh).then_inc(gelu2, 1)

        def hidden_hi(n, j):
            act.wait_ge(v_read, n + 1)
            A(a_hi[:, j, :], a_t[:, j % 2, :], ACT.Copy).then_inc(ah_ok, 1)

        for j in range(4):
            hi(slot(S_U0 + j + 1))
            conv_tap(j, j, j)
        with act.Fori(0, CHUNKS - 1) as c:
            for j in range(4):
                hi(slot(S_FF + j + 1, 12, c))
                hidden_hi(c * 4 + j, j)
            for j in range(4):
                hi(slot(S_FF + 5 + j, 12, c))
                conv_tap(c * 4 + (4 + j), c * 4 + (4 + j), j)
            for j in range(4):
                hi(slot(S_FF + 9 + j, 12, c))
        tail = S_FF + 12 * (CHUNKS - 1)
        for j in range(4):
            hi(slot(tail + j + 1))
            hidden_hi(4 * (CHUNKS - 1) + j, j)
        for j in range(4):
            if j < 3:
                hi(slot(tail + 5 + j))
            for t in range(TOK):
                act.wait_ge(dn_add, 16 * (CHUNKS - 1) + 4 * j + t + 1 + 4)
                own.link(A(sq3[:], x1[:, t, 512 * j:512 * j + 512], ACT.Square, accum_out=ss[:, 4 * j + t:4 * j + t + 1]))
            act.sem_inc(sq3_done, 1)
        act.wait_ge(sqrt_in, 3)
        A(nmx[:, 4:8], nmx[:, 0:4], ACT.Sqrt).then_inc(sqrt_out, 1)
        act.wait_ge(rs3_ok, 1)
        act.wait_ge(xg_ok, 3)
        for t in range(TOK):
            A(x1[:, t, 0:1536], x1[:, t, 0:1536], ACT.Copy, scale=rr[:, t:t + 1]).then_inc(o_act, 1)

    @block.vector
    def _(dve):
        V = nc.vector
        own = Chain(dve, dve_own)
        link = own.link

        def lo(s):
            dve.wait_ge(w_hi_done, s.n + 1)
            V.tensor_tensor(w_lo[:, s.par, :], w_raw[:, s.par, :], w_hi[:, s.par, :].bitcast(F32), ALU.subtract).then_inc(w_ready, 1)

        def rstd(total, v, t0, t1, dst, nth):
            V.tensor_scalar(v, total, 1.0 / D_MODEL, EPS, ALU.mult, ALU.add).then_inc(sqrt_in, 1)
            dve.wait_ge(sqrt_in, nth)
            dve.wait_ge(sqrt_out, nth)
            link(V.reciprocal(t0, t0))
            link(V.tensor_tensor(t1, v, t0, ALU.mult))
            link(V.tensor_tensor(t1, t1, t0, ALU.mult))
            link(V.tensor_scalar(t1, t1, -0.5, 1.5, ALU.mult, ALU.add))
            link(V.tensor_tensor(dst, t0, t1, ALU.mult))

        link(V.memset(tabx[32:33, :], NEG))
        dve.sem_inc(w_ready, 2)
        V.memset(ones_f[:], 1.0)
        V.memset(l_cmp[:], NEG)
        dve.wait_ge(ident_in, 16)
        V.tensor_copy(ident_b[:], ident[:])
        dve.wait_ge(cols_t, 1)
        V.tensor_copy(cols[:], pb[2][:, 0:272]).then_inc(cols_ok, 1)
        dve.wait_ge(cols_ok, 1)
        for k in range(KT):
            dve.wait_ge(xh_done, k + 1)
            V.scalar_tensor_tensor(h_lo[:, k, :], pb[4 + k % 4][:], cols[:, G_ATTN + k:G_ATTN + k + 1],
                                   h_hi[:, k, :].bitcast(F32), ALU.mult, ALU.subtract).then_inc(xl_done, 1)
            if k in (2, 8):
                lo(slot(k // 8))
        dve.wait_ge(misc_in, 48)
        V.tensor_copy(tri_b[:], tri32[:])
        dve.wait_ge(r_ps, 1)
        V.tensor_copy(r_sb[:, 0:512], pb[3][0:8, 0:512])
        V.tensor_copy(r_sb[:, 512:R_LEN], pb[2][0:8, 0:P]).then_inc(r_ok, 1)
        dve.wait_ge(ss_done, TOK)
        rstd(ss[:, 0:4], ss[:, 4:8], ss[:, 8:12], ss[:, 12:16], rr[:, 0:4], 1)
        for t in range(TOK):
            last = V.tensor_copy(rs_rep[:, t, :], rr[:, t:t + 1].to_broadcast([P, P]))
        last.then_inc(rep_ok, 1)
        dve.wait_ge(wg_hi_ok, 1)
        V.tensor_tensor(wg_lo[:], wg_raw[:], wg_hi[:].bitcast(F32), ALU.subtract).then_inc(wg_ok, 1)
        lo(slot(2))
        dve.wait_ge(rbc_ps, 1)
        V.tensor_copy(rbc[:], pb[3][:]).then_inc(rbc_ok, 1)
        dve.wait_ge(rbc_ok, 1)

        def kv_out(n, bank, after):
            dve.wait_ge(w_used, after + 3)
            V.tensor_tensor(kv_fm[:, ds(n, 1), :].rearrange("p a n -> p (a n)"), pb[bank][:], rbc[:], ALU.mult).then_inc(kv_done, 1)

        kv_out(0, 0, 0)
        kv_out(1, 1, 1)
        dve.wait_ge(gl_ps, 1)
        V.tensor_tensor(gl[:], pb[2][0:NG, :], rbc[0:NG, :], ALU.mult).then_inc(gl_ok, 1)
        dve.wait_ge(gl_ok, 1)
        V.tensor_scalar(fz[:, 2], gl[0:HEADS, :], fb[:], None, ALU.add).then_inc(fz_ok, 1)
        dve.wait_ge(fz_ok, 1)
        link(V.tensor_scalar(fz[:, 0], fz[:, 2], 0.0, None, ALU.min))
        dve.wait_ge(fe_ok, 1)
        link(V.tensor_tensor(fz[:, 2], fz[:, 1], fz[:, 0], ALU.subtract))
        V.tensor_tensor_scan(cum_f[:], ones_f[:], fz[:, 2], 0.0, ALU.mult, ALU.add).then_inc(fcum_ok, 1)
        lo(slot(3))
        kv_out(2, 0, 2)
        lo(slot(S_KW))
        kv_out(3, 1, 3)
        V.memset(g4[:], 0.0)
        with dve.Fori(0, 2) as i:
            for q in range(2):
                for j in range(2):
                    lo(slot(S_KW + 3 * q + j + 1, 6, i))
                    if q == 0 and j == 0:
                        dve.wait_ge(xs_hi_ok, i + 1)
                        for g in range(GROUPS):
                            c = slice(g * CP, g * CP + CP)
                            V.tensor_tensor(xs_lo[:, :, c], strides(i, g), xs_hi[:, :, c].bitcast(F32), ALU.subtract)
                        c = slice(2 * CP, X_COLS)
                        V.tensor_tensor(xs_lo[:, :, c], positions(i), xs_hi[:, :, c].bitcast(F32), ALU.subtract).then_inc(xs_ok, 1)
                    kv_out(i * 4 + (4 + 2 * q + j), j, slot(S_KW + 3 * q + j, 6, i).n)
                lo(slot(S_KW + 3 * q + 3, 6, i))
            dve.wait_ge(w_used, i * 6 + (S_KW + 5 + 3))
            V.tensor_copy(halves[:, ds(i, 1), :].rearrange("p a n -> p (a n)"), pb[2][0:X_COLS, 0:2 * P]).then_inc(halves_ok, 1)
        dve.wait_ge(c_out, 16)
        lo(slot(S_QN + 1))
        dve.wait_ge(gelu_ok, 1)
        for g in range(GROUPS):
            for t in range(TOK):
                last = V.tensor_copy(g4[:, g, t, t * CP:t * CP + CP], gv[:, g * CP:g * CP + CP])
        last.then_inc(g4_ok, 1)
        dve.wait_ge(vt_ok, 4)
        dve.wait_ge(vc_ps, 1)
        for g in range(GROUPS):
            last = V.tensor_copy(vc4[:, g].rearrange("p t d -> p (t d)"), pb[5 + g][:])
        last.then_inc(vc_ok, 1)

        def q_out(dst, bank, after, done, scale):
            dve.wait_ge(w_used, after + 3)
            if scale is None:
                V.tensor_tensor(dst, pb[bank][:], rbc[:], ALU.mult).then_inc(done, 1)
            else:
                V.scalar_tensor_tensor(dst, pb[bank][:], scale, rbc[:], ALU.mult, ALU.mult).then_inc(done, 1)

        q_out(q_n[:], 0, S_QN, q_ready, SCALE)

        def logits(lt, bias, c, ready, base, done):
            for k, i in enumerate(TILES):
                b, col = S_PLACE[i]
                n = P * (i + 1)
                hold(dve, ready, base + (3 if k == 1 else k + 1))
                V.tensor_tensor_reduce(out=lt[:, L_COL[i]:L_COL[i] + n], in0=pb[b][:, col:col + n], in1=bias(i), scale=1.0,
                                       scalar=-3.0e38, op0=ALU.add, op1=ALU.max, accum_out=mx[:, c + i:c + i + 1]).then_inc(done, 1)

        def nsa_step(s, g, it, bias_n_use, head, fill):
            dve.wait_ge(bn_loaded[g], bias_n_use * 16 + 16)
            dve.wait_ge(ns_ready, s * 9 + 1)
            for i in range(TOK):
                n = (96 + P * i) // CMP_STRIDE + 1
                start = SEQ - P - P * i + CMP_BLOCK - 1
                b = bias_n[:, g, start:start + (n - 1) * CMP_STRIDE + 1:CMP_STRIDE]
                last = V.tensor_tensor(l_cmp[:, i, 0:n], pb[g][:, CP * i:CP * i + n], b, ALU.add)
            last.then_inc(ns_read, 1)
            dve.wait_ge(ns_read, s * 9 + 19)
            link(V.tensor_reduce(mx[:, 0:4], l_cmp[:], AX.X, ALU.max))
            link(V.tensor_scalar(nmx[:, 0:4], mx[:, 0:4], -1.0e20, -1.0, ALU.max, ALU.mult))
            V.tensor_tensor(p_cmp[:], l_cmp[:], nmx[:, 0:4].unsqueeze(2).to_broadcast([P, TOK, CP]), ALU.add).then_inc(cmp_shift, 1)
            for u, lt in enumerate((l_slc, l_win)):
                logits(lt, lambda i: bias_n[:, g, SEQ - P - P * i:SEQ], 4 + 4 * u, ns_ready, s * 9 + (1 + 4 * u), ns_read)
                dve.wait_ge(ns_read, s * 9 + (23 + 4 * u))
                V.tensor_scalar(nmx[:, 4 + 4 * u:8 + 4 * u], mx[:, 4 + 4 * u:8 + 4 * u], -1.0, None, ALU.mult).then_inc(max_ready, 1)
            lo(fill)
            for u in range(3):
                c = slice(4 * u, 4 * u + 4)
                dve.wait_ge(exp_done, s * 3 + (u + 1))
                if u == 0:
                    link(V.tensor_reduce(sm[:, 0:4], p_cmp[:], AX.X, ALU.add))
                    link(V.tensor_scalar(sm[:, 0:4], sm[:, 0:4], 1.0e-30, None, ALU.max))
                link(V.reciprocal(rr[:, c], sm[:, c]))
                V.tensor_tensor(rr[:, c], rr[:, c], gates[:, :, ds(head * 3 + u, 1)].rearrange("p t a -> p (t a)"),
                                ALU.mult).then_inc(r_ready, 1)
            if not isinstance(s, int) or s < HEADS - 1:
                q_out(q_n[:], 1 - g, fill.n - 1, q_ready, SCALE)
            for u in range(2):
                dve.wait_ge(nt_ready, s * 6 + (3 * u + 2) + 6)
                dve.wait_ge(npv_done, s * 2 + (u + 1))
                V.tensor_copy(pt_n[:, 512:1024], pb[6][:]).then_inc(nt_dve, 1)

        dve.wait_ge(gates_ok, 1)
        with dve.Fori(0, 3) as it:
            own.enter(it, 14)
            nsa_step(it * 2, 0, it, it, it, slot(S_QN + 2, 2, it))
            nsa_step(it * 2 + 1, 1, it, it, it + 4, slot(S_QN + 3, 2, it))
        own.leave(3)
        nsa_step(6, 0, 3, 3, 3, slot(S_QN + 8))
        nsa_step(7, 1, 3, 3, 7, slot(S_GA + 1))

        def merge(base, which):
            for q in range(2):
                dve.wait_ge(yh_ok, 2 * which + q + 1)
                V.tensor_tensor(y_lo[:, 4 * q:4 * q + 4, :], y32[:, 4 * q:4 * q + 4, :], y_hi[:, 4 * q:4 * q + 4, :].bitcast(F32),
                                ALU.subtract).then_inc(y_ok, 1)

            def iteration(c, per, i, nth, pairs, last):
                for pair in range(2):
                    for j in range(2):
                        dve.wait_ge(w_used, slot(c + 3 * pair + j, per, i).n + 3)
                        V.tensor_tensor(gate_t[:, j, :], pb[j][:], rbc[:], ALU.mult).then_inc(gate_read[which], 1)
                        lo(slot(c + 3 * pair + j + 2, per, i))
                    if last and pair == 1:
                        for q in range(3):
                            merged_lo(q)
                    dve.wait_ge(sig_done[which], nth + (2 * pair + 2))
                    dve.wait_ge(w_used, slot(c + 3 * pair + 2, per, i).n + 3)
                    for j in range(2):
                        dst = m32[:, ds(nth + (2 * pair + j), 1), :].rearrange("p a n -> p (a n)")
                        if which == 0:
                            r = V.tensor_tensor(dst, pb[2 + j][:], gate_t[:, j, :], ALU.mult)
                        else:
                            link(V.tensor_tensor(gate_t[:, j, :], pb[2 + j][:], gate_t[:, j, :], ALU.mult))
                            r = V.tensor_tensor(dst, dst, gate_t[:, j, :], ALU.add)
                    r.then_inc(br_read[which], 1)
                    dve.wait_ge(br_read[which], pairs + (pair + 2))
                    lo(slot(c + 3 * pair + 4, per, i))

            with dve.Fori(0, 3 if which else 4) as i:
                own.enter(i, 4 if which else 0)
                iteration(base, 6, i, i * 4, i * 2, False)
            own.leave(3 if which else 4)
            if which:
                iteration(base + 18, 0, None, 12, 6, True)

        def merged_lo(q):
            dve.wait_ge(mh_ok, q + 1)
            V.tensor_tensor(h_lo[:, 4 * q:4 * q + 4, :], m32[:, 4 * q:4 * q + 4, :], h_hi[:, 4 * q:4 * q + 4, :].bitcast(F32),
                            ALU.subtract).then_inc(ml_ok, 1)

        merge(S_GA, 0)

        for j in range(3):
            if j:
                lo(slot(S_FOX + j + 1))
            q_out((q_f, k_f, vf_fm)[j][:], j % 2, S_FOX + j, fproj, SCALE if j == 0 else None)

        def fox_step(h, b, use, c, per, i, fill):
            dve.wait_ge(bf_loaded[b], use * 16 + 16)
            logits(l_fox, lambda t: bias_f[:, b, 0:P * (t + 1)], 4, fs_ready, h * 4, fs_read)
            dve.wait_ge(fs_read, h * 4 + 12)
            V.tensor_scalar(nmx[:, 4:8], mx[:, 4:8], -1.0, None, ALU.mult).then_inc(fmax_ready, 1)
            lo(slot(c + 1, per, i))
            dve.wait_ge(fexp_done, h + 1)
            V.reciprocal(rr[:, 4:8], sm[:, 4:8]).then_inc(fr_ready, 1)
            if fill > 1:
                q_out(q_f[:], c % 2, slot(c, per, i).n, fproj, SCALE)
            dve.wait_ge(ft_ready, h * 3 + 2)
            dve.wait_ge(fpv_done, h + 1)
            V.tensor_copy(pt_f[:, 512:1024], pb[6][:]).then_inc(ft_dve, 1)
            if fill > 1:
                lo(slot(c + 2, per, i))
                q_out(k_f[:], (c + 1) % 2, slot(c + 1, per, i).n, fproj, None)
                lo(slot(c + 3, per, i))
                q_out(vf_fm[:], c % 2, slot(c + 2, per, i).n, fproj, None)

        with dve.Fori(0, 3) as i:
            fox_step(i * 2, 0, i, S_FOX + 3, 6, i, 3)
            fox_step(i * 2 + 1, 1, i, S_FOX + 6, 6, i, 3)
        fox_step(6, 0, 3, S_FOX + 21, 0, None, 3)
        fox_step(7, 1, 3, S_GB, 0, None, 1)
        merge(S_GB, 1)
        merged_lo(3)

        def wo_add(g, after):
            for t in range(TOK):
                if t < TOK - 1:
                    dve.wait_ge(wo_done, g * 3 + (t + 1))
                else:
                    dve.wait_ge(w_used, after + 3)
                if t == 0:
                    dve.wait_ge(x1t_ps, g * 4 + 1)
                    dve.wait_ge(x1_put, g * 4 + 1)
                V.tensor_tensor(x1_new[:, t, :], pb[t][:], x1[:, t, ds(g * 512, 512)], ALU.add).then_inc(x1_add, 1)

        dve.wait_ge(xr_loaded, 64)
        with dve.Fori(0, 3) as g:
            for sub in range(1, 4):
                lo(slot(S_WO + sub + 1, 4, g))
            wo_add(g, slot(S_WO + 3, 4, g).n)
            lo(slot(S_WO + 5, 4, g))
        def h2_lo(q):
            dve.wait_ge(hh_ok, q + 1)
            V.tensor_tensor(h_lo[:, 4 * q:4 * q + 4, :], m32[:, 4 * q:4 * q + 4, :], h_hi[:, 4 * q:4 * q + 4, :].bitcast(F32),
                            ALU.subtract).then_inc(hl_ok, 1)
        for sub in range(1, 4):
            lo(slot(S_WO + 12 + sub + 1))
            h2_lo(sub - 1)
        wo_add(3, S_U0 - 1)
        h2_lo(3)
        dve.wait_ge(x1_put, 4 * TOK + 1)
        link(V.tensor_reduce(mx[:, 0:4], ss.rearrange("p (g t) -> p t g", t=TOK), AX.X, ALU.add))
        rstd(mx[:, 0:4], nmx[:, 0:4], nmx[:, 4:8], nmx[:, 8:12], rr[:, 0:4], 2)
        for t in range(TOK):
            last = V.tensor_copy(rs_rep2[:, t, :], rr[:, t:t + 1].to_broadcast([P, P]))
        last.then_inc(rep2_ok, 1)
        V.memset(u_pad[:, :, 0:CONV - 1], 0.0)
        lo(slot(S_U0 + 1))
        dve.wait_ge(rbc2_ps, 1)
        link(V.tensor_copy(rbc[:], pb[6][:]))
        dve.sem_inc(rbc2_ok, 1)

        def up_out(n, f, j, bank_slot):
            dve.wait_ge(w_used, bank_slot.n + 3)
            V.tensor_tensor(u_pad[:, j % 2, 2:SEQ + 2], pb[j % 2][:], rbc[:], ALU.mult).then_inc(up_read, 1)
            dve.wait_ge(up_read, n + 1)
            dve.wait_ge(tap2, n + 1)
            link(V.scalar_tensor_tensor(conv_t[:, j % 2, :], u_pad[:, j % 2, 1:SEQ + 1], cols[:, ds(f + C_W[1], 1)],
                                        conv_t[:, j % 2, :], ALU.mult, ALU.add))
            V.scalar_tensor_tensor(conv_t[:, j % 2, :], u_pad[:, j % 2, 0:SEQ], cols[:, ds(f + C_W[0], 1)],
                                   conv_t[:, j % 2, :], ALU.mult, ALU.add).then_inc(tap0, 1)

        def hidden(n, j, s, g_n):
            dve.wait_ge(w_used, s.n + 3)
            dve.wait_ge(g_ok, g_n + 1)
            V.tensor_tensor(a_t[:, j % 2, :], pb[j % 2][:], g_rs[:, j, :], ALU.mult).then_inc(v_read, 1)
            dve.wait_ge(ah_ok, n + 1)
            V.tensor_tensor(a_lo[:, j, :], a_t[:, j % 2, :], a_hi[:, j, :].bitcast(F32), ALU.subtract).then_inc(a_ok, 1)

        def down_add(c, per, i, chunk, j):
            s = slot(c + j, per, i)
            for t in range(TOK):
                if t < TOK - 1:
                    dve.wait_ge(dn_done, chunk * 12 + (3 * j + t + 1))
                else:
                    dve.wait_ge(w_used, s.n + 3)
                d = x1[:, t, 512 * j:512 * j + 512]
                V.tensor_tensor(d, pb[2 + t][:], d, ALU.add).then_inc(dn_add, 1)

        for j in range(4):
            if j:
                lo(slot(S_U0 + j + 1))
            up_out(j, j, j, slot(S_U0 + j))
        with dve.Fori(0, CHUNKS - 1) as c:
            own.enter(c, 4)
            for j in range(4):
                lo(slot(S_FF + j + 1, 12, c))
                hidden(c * 4 + j, j, slot(S_FF + j, 12, c), c * 4 + j)
            for j in range(4):
                lo(slot(S_FF + 5 + j, 12, c))
                up_out(c * 4 + (4 + j), c * 4 + (4 + j), j, slot(S_FF + 4 + j, 12, c))
            for j in range(4):
                lo(slot(S_FF + 9 + j, 12, c))
                down_add(S_FF + 8, 12, c, c, j)
        own.leave(CHUNKS - 1)
        tail = S_FF + 12 * (CHUNKS - 1)
        for j in range(4):
            lo(slot(tail + j + 1))
            hidden(4 * (CHUNKS - 1) + j, j, slot(tail + j), 4 * (CHUNKS - 1) + j)
        for j in range(4):
            if j < 3:
                lo(slot(tail + 5 + j))
            down_add(tail + 4, 0, None, CHUNKS - 1, j)
        dve.wait_ge(sq3_done, 4)
        link(V.tensor_reduce(mx[:, 0:4], ss.rearrange("p (g t) -> p t g", t=TOK), AX.X, ALU.add))
        rstd(mx[:, 0:4], nmx[:, 0:4], nmx[:, 4:8], nmx[:, 8:12], rr[:, 0:4], 3)
        dve.sem_inc(rs3_ok, 1)
        dve.wait_ge(gf_in, 16)
        for t in range(TOK):
            d = x1[:, t, 1536:2048]
            V.scalar_tensor_tensor(d, d, rr[:, t:t + 1], gfin[:, 1536:2048], ALU.mult, ALU.mult).then_inc(o_dve, 1)

    @block.gpsimd
    def _(pool):
        G = nc.gpsimd
        pool.dma_start(onehot[:], c_onehot).then_inc(misc_in, 16)
        pool.dma_start(tabx[0:32, :], rel_bias_table).then_inc(misc_in, 16)
        pool.dma_start(tri32[:], c_tri).then_inc(misc_in, 16)
        pool.dma_start(wg_raw[:, :, 0:HEADS], win[:, :, COL_FL:COL_FL + HEADS]).then_inc(wg_loaded, 16)
        pool.dma_start(wg_raw[:, :, HEADS:NG], win[:, :, COL_GN:COL_GN + NG - HEADS]).then_inc(wg_loaded, 16)
        pool.dma_start(fb[:], fox_forget_bias.rearrange("a h -> h a")).then_inc(wg_loaded, 16)
        pool.dma_start(sel[:], c_sel).then_inc(wg_loaded, 16)
        for s_, n in ((ns_read, 18), (nt_ready, 6), (nt_dve, 1), (npv_done, 1), (gate_read[0], 2), (gate_read[1], 2),
                      (br_read[0], 1), (br_read[1], 1), (fproj, 2), (fs_read, 8), (ft_dve, 1), (fpv_done, 1),
                      (x1t_ps, 1), (x1_put, 1), (dn_add, 4), (halves_ok, 1)):
            pool.sem_inc(s_, n)

        def scale(lt, c):
            for i in TILES:
                d = lt[:, L_COL[i]:L_COL[i] + P * (i + 1)]
                last = G.tensor_scalar(d, d, rr[:, c + i:c + i + 1], None, ALU.mult)
            return last

        with pool.Fori(0, HEADS) as s:
            hold(pool, r_ready, s * 3 + 1)
            G.tensor_tensor(p_cmp[:], p_cmp[:], rr[:, 0:4].unsqueeze(2).to_broadcast([P, TOK, CP]), ALU.mult).then_inc(p_ready, 1)
            hold(pool, r_ready, s * 3 + 2)
            scale(l_slc, 4).then_inc(p_ready, 1)
            hold(pool, r_ready, s * 3 + 3)
            scale(l_win, 8).then_inc(p_ready, 1)
        with pool.Fori(0, HEADS) as h:
            hold(pool, fr_ready, h + 1)
            scale(l_fox, 4).then_inc(fp_ready, 1)
        pool.wait_ge(rbc2_ok, 1)
        pool.dma_start(gfin[:], final_norm_g.rearrange("(a n) -> a n", a=1).to_broadcast([P, D_MODEL])).then_inc(gf_in, 16)

        def g_out(n, j):
            hold(pool, gelu2, n + 1)
            G.tensor_tensor(g_rs[:, j, :], conv_t[:, j % 2, :], rbc[:], ALU.mult).then_inc(g_ok, 1)

        with pool.Fori(0, CHUNKS) as c:
            for j in range(4):
                g_out(c * 4 + j, j)
        pool.wait_ge(gf_in, 16)
        for j in range(3):
            pool.wait_ge(sq3_done, j + 1)
            d = x1[:, :, 512 * j:512 * j + 512]
            g = gfin[:, 512 * j:512 * j + 512].unsqueeze(1).to_broadcast([P, TOK, 512])
            G.tensor_tensor(d, d, g, ALU.mult).then_inc(xg_ok, 1)

    ctx.close()


_INS = ['x', 'attn_norm_g', 'w_in', 'cmp_pos_k', 'cmp_w1_k', 'cmp_w2_k', 'cmp_pos_v', 'cmp_w1_v', 'cmp_w2_v',
        'rel_bias_table', 'fox_forget_bias', 'w_branch_nsa', 'w_branch_fox', 'w_out', 'ffn_norm_g', 'w_up', 'conv_w',
        'conv_b', 'w_down', 'final_norm_g']


def _constants():
    import math
    import numpy as np
    ident = np.eye(P, dtype=np.float32)
    onehot = np.zeros((REL_BUCKETS + 1, R_LEN), np.float32)
    exact = REL_BUCKETS // 2
    for j in range(R_LEN):
        dist = SEQ - 1 - j
        if dist < 0:
            onehot[REL_BUCKETS, j] = 1
        elif dist < exact:
            onehot[dist, j] = 1
        else:
            b = exact + int(math.log(dist / exact) / math.log(REL_MAX_DIST / exact) * (REL_BUCKETS - exact))
            onehot[min(b, REL_BUCKETS - 1), j] = 1
    sel = np.zeros((X_COLS, 2, GROUPS * CP), np.float32)
    for half in range(2):
        for g in range(GROUPS):
            for c in range(N_CMP):
                sel[g * CP + c + half, half, g * CP + c] = 1
                sel[GROUPS * CP + half, half, g * CP + c] = 1
    tri = np.where(np.arange(P)[None, :] > np.arange(P)[:, None], np.float32(NEG), np.float32(0)).astype(np.float32)
    return {"c_ident": ident, "c_onehot": onehot, "c_tri": tri, "c_sel": sel}


def kernel(**inputs):
    import numpy as _np
    import concourse.bacc as _bacc
    from concourse import mybir as _mybir
    from concourse.bass_utils import run_bass_kernel_spmd as _run

    nc = _bacc.Bacc("TRN2", target_bir_lowering=False, num_devices=1)
    arrays, args = {}, []
    given = {n: _np.ascontiguousarray(inputs[n]) for n in _INS}
    given.update(_constants())
    for name, a in given.items():
        arrays[f"in_{name}_dram"] = a
        args.append(nc.dram_tensor(f"in_{name}_dram", a.shape, _mybir.dt.from_np(a.dtype), kind="ExternalInput").ap())
    args.append(nc.dram_tensor("out_0_dram", (1, SEQ, D_MODEL), _mybir.dt.float32, kind="ExternalOutput").ap())
    build(nc, *args)
    r = _run(nc, [arrays], core_ids=[0])
    return r.results[0]["out_0_dram"]
```

```python
from contextlib import ExitStack
from collections import namedtuple
import concourse.bass as bass
from concourse import mybir

P = 128
SEQ, D_MODEL, D_FF = 512, 2048, 5632
HEADS, GROUPS = 8, 2
TOK = SEQ // P
KT = D_MODEL // P
CMP_BLOCK, CMP_STRIDE = 32, 16
N_CMP = SEQ // CMP_STRIDE - 1
CP = 32
NG = 32
X_COLS = 2 * CP + 2
REL_BUCKETS, REL_MAX_DIST = 32, 128
CONV = 3
EPS = 1e-6
NEG = -1e30
SCALE = float(P) ** -0.5
CHUNKS = D_FF // (4 * P)
R_LEN = SEQ + P
COL_QN, COL_KV, COL_GN = 0, 1024, 2560
COL_QF, COL_KF, COL_VF, COL_FL = 2584, 3608, 4632, 5656
COL_MA, COL_MB = 5664, 7712
S_KV = 0
S_KW = S_KV + 4
S_QN = S_KW + 12
S_GA = S_QN + 8
S_FOX = S_GA + 24
S_GB = S_FOX + 24
S_WO = S_GB + 24
S_U0 = S_WO + 16
S_FF = S_U0 + 4
S_END = S_FF + 12 * (CHUNKS - 1) + 8

TILES = [3, 2, 0, 1]
S_PLACE = {3: (2, 0), 2: (3, 0), 0: (3, 384), 1: (4, 0)}
L_COL = {3: 0, 2: 512, 0: 896, 1: 1024}
PT_COL = {0: 0, 1: 512, 3: 896, 2: 1024}
CMP_COL = 1280

Slot = namedtuple("Slot", "n half par")


def slot(c, per=0, i=None):
    if i is None:
        return Slot(c, c // 2, c % 2)
    return Slot(i * per + c, i * (per // 2) + c // 2, c % 2)


class Chain:

    def __init__(self, eng, sem):
        self.eng, self.sem, self.base, self.k, self.per, self.i = eng, sem, 0, 0, 0, None

    def link(self, ins):
        self.k += 1
        ins.then_inc(self.sem, 1)
        at = self.base + self.k
        self.eng.wait_ge(self.sem, at if self.i is None else self.i * self.per + at)

    def enter(self, i, per):
        self.base, self.k, self.i, self.per = self.base + self.k, 0, i, per

    def leave(self, count):
        assert self.k == self.per, (self.k, self.per)
        self.base, self.k, self.i = self.base + self.per * count, 0, None


def build(nc, x, attn_norm_g, w_in, cmp_pos_k, cmp_w1_k, cmp_w2_k, cmp_pos_v, cmp_w1_v, cmp_w2_v,
          rel_bias_table, fox_forget_bias, w_branch_nsa, w_branch_fox, w_out, ffn_norm_g, w_up, conv_w,
          conv_b, w_down, final_norm_g, c_ident, c_onehot, c_tri, c_sel, out):
    F32, F32R, BF16 = mybir.dt.float32, mybir.dt.float32r, mybir.dt.bfloat16
    ACT, ALU, AX = mybir.ActivationFunctionType, mybir.AluOpType, mybir.AxisListType
    ds = bass.ds
    KB = 1024
    ctx = ExitStack()
    BASE = 16512

    def at(name, off, shape, dt=F32):
        return nc.alloc_sbuf_tensor_at(name, shape, dt, offset=BASE + off)

    A_, M_, Y_ = 160 * KB, 112 * KB, 144 * KB
    h_hi = at("h_hi", 0, [P, KT, SEQ], F32R)
    h_lo = at("h_lo", 32 * KB, [P, KT, SEQ], F32R)
    w_raw = at("w_raw", 64 * KB, [P, 2, 2048])
    w_hi = at("w_hi", 80 * KB, [P, 2, 2048], F32R)
    w_lo = at("w_lo", 96 * KB, [P, 2, 2048], F32R)
    m32 = at("m32", M_, [P, KT, SEQ])
    kv_fm = at("kv_fm", M_, [P, 12, SEQ])
    bias_n = at("bias_n", M_ + 24 * KB, [P, 2, SEQ])
    q_n = at("q_n", M_ + 28 * KB, [P, SEQ])
    k_split = at("k_split", M_, [P, 12, SEQ], F32R)
    K_PLACE = [(0, 2), (6, 10)]
    q_hi = at("q_hi", M_ + 30 * KB, [P, SEQ], F32R)
    q_lo = at("q_lo", A_ + 17 * KB, [P, SEQ], F32R)
    y32 = at("y32", Y_, [P, 8, 512])
    x_in = at("x_in", A_, [P, TOK, D_MODEL])
    wg_raw = at("wg_raw", A_ + 32 * KB, [P, KT, NG])
    wg_hi = at("wg_hi", A_ + 34 * KB, [P, KT, NG], F32R)
    wg_lo = at("wg_lo", A_ + 36 * KB, [P, KT, NG], F32R)
    ones_f = at("ones_f", A_ + 38 * KB, [8, SEQ])
    cum_f = at("cum_f", A_ + 40 * KB, [8, SEQ])
    tri32 = at("tri32", A_ + 42 * KB, [P, P])
    sq_junk = at("sq_junk", Y_, [P, D_MODEL])
    onehot = at("onehot", Y_ + 8 * KB, [33, R_LEN])
    r_sb = at("r_sb", Y_ + 8 * KB + 2560, [8, R_LEN])
    rows = at("rows", Y_ + 13 * KB, [P, 3, P])
    sel = at("sel", Y_ + 14 * KB + 512, [X_COLS, 2, GROUPS * CP])
    rs_rep = at("rs_rep", Y_, [P, TOK, P])
    gl = at("gl", A_ + 8 * KB, [NG, SEQ])
    fz = at("fz", A_ + 10 * KB, [HEADS, 3, SEQ])
    xs_hi = at("xs_hi", Y_, [P, CMP_STRIDE, X_COLS], F32R)
    xs_lo = at("xs_lo", A_, [P, CMP_STRIDE, X_COLS], F32R)
    halves = at("halves", A_ + 5 * KB, [X_COLS, 2, 2 * P])
    v_tm = at("v_tm", A_ + 8 * KB, [P, 4, TOK, P])
    w2_sb = at("w2_sb", A_ + 16 * KB, [P, 2, P])
    g4 = at("g4", A_ + 17 * KB, [P, GROUPS, TOK, P])
    vc4 = at("vc4", A_ + 21 * KB, [P, GROUPS, TOK, P])
    kc_fm = at("kc_fm", A_, [P, GROUPS * CP])
    gk = at("gk", A_ + 256, [P, GROUPS * CP])
    gv = at("gv", A_ + 512, [P, GROUPS * CP])
    l_slc = at("l_slc", A_ + 25 * KB, [P, 1280])
    p_cmp = at("p_cmp", A_ + 30 * KB, [P, TOK, CP])
    l_win = at("l_win", A_ + 30 * KB + 512, [P, 1280])
    pt_n = at("pt_n", A_ + 35 * KB + 512, [P, 1408])
    y_hi = at("y_hi", A_, [P, 8, SEQ], F32R)
    y_lo = at("y_lo", A_ + 16 * KB, [P, 8, SEQ], F32R)
    gate_t = at("gate_t", A_ + 32 * KB, [P, 2, SEQ])
    q_f = at("q_f", A_, [P, SEQ])
    k_f = at("k_f", A_ + 2 * KB, [P, SEQ])
    qf_hi = at("qf_hi", A_ + 18 * KB, [P, SEQ], F32R)
    qf_lo = at("qf_lo", A_ + 20 * KB, [P, SEQ], F32R)
    kf_hi = at("kf_hi", A_ + 22 * KB, [P, SEQ], F32R)
    kf_lo = at("kf_lo", A_ + 24 * KB, [P, SEQ], F32R)
    vf_fm = at("vf_fm", A_ + 4 * KB, [P, SEQ])
    vf_tm = at("vf_tm", A_ + 6 * KB, [P, TOK, P])
    l_fox = at("l_fox", A_ + 8 * KB, [P, 1280])
    pt_f = at("pt_f", A_ + 13 * KB, [P, 1280])
    bias_f = at("bias_f", A_ + 36 * KB, [P, 2, SEQ])
    x1 = at("x1", A_, [P, TOK, D_MODEL])
    gfin = at("gfin", A_ + 32 * KB, [P, D_MODEL])
    x1_new = at("x1_new", Y_, [P, TOK, 512])
    sq2 = at("sq2", Y_ + 8 * KB, [P, 512])
    rs_rep2 = at("rs_rep2", Y_ + 14 * KB, [P, TOK, P])
    a_hi = at("a_hi", M_, [P, 4, SEQ], F32R)
    a_lo = at("a_lo", M_ + 8 * KB, [P, 4, SEQ], F32R)
    g_rs = at("g_rs", M_ + 16 * KB, [P, 4, SEQ])
    u_pad = at("u_pad", Y_, [P, 2, SEQ + CONV - 1])
    conv_t = at("conv_t", Y_ + 4128, [P, 2, SEQ])
    a_t = at("a_t", Y_ + 4128 + 4 * KB, [P, 2, SEQ])
    sq3 = at("sq3", M_ + 24 * KB, [P, 512])
    o = 202 * KB + 512
    ident = at("ident", o, [P, P]); o += 512
    ident_b = at("ident_b", o, [P, P], BF16); o += 256
    tri_b = at("tri_b", o, [P, P], BF16); o += 256
    cols = at("cols", o, [P, 272]); o += 1088
    rbc = at("rbc", o, [P, SEQ]); o += 2048
    gates = at("gates", o, [P, TOK, 24]); o += 384
    l_cmp = at("l_cmp", o, [P, TOK, CP]); o += 512
    st = at("st", o, [P, 64]); o += 256
    assert BASE + o <= 229376
    fb = at("fb", Y_ + 15 * KB + 896, [HEADS, 1])
    tabx = at("tabx", Y_ + 15 * KB + 928, [33, 8])

    ss, mx, nmx, sm, rr = (st[:, 0:16], st[:, 16:28], st[:, 28:40], st[:, 40:52], st[:, 52:64])
    G_ATTN, G_FFN, C_B, C_W, C_POS = 0, 16, 32, [76, 120, 164], 208

    pb = [ctx.enter_context(nc.psum_tensor(f"bank{b}", [P, 512], F32)) for b in range(8)]

    r_dram = nc.dram_tensor("r_dram", [8, R_LEN], F32, kind="Internal").ap()
    e_dram = nc.dram_tensor("e_dram", [8 * P, SEQ], F32, kind="Internal").ap()
    c_dram = nc.dram_tensor("c_dram", [8, SEQ], F32, kind="Internal").ap()

    def sem(name):
        return ctx.enter_context(nc.semaphore(name))

    w_loaded = [sem("w_loaded0"), sem("w_loaded1")]
    w1_loaded = sem("w1_loaded")
    w_hi_done = sem("w_hi_done")
    part_hi, part_ready = sem("part_hi"), sem("part_ready")
    w_ready = sem("w_ready")
    w_used = sem("w_used")
    dve_own, act_own = sem("dve_own"), sem("act_own")
    ident_in, const_in = sem("ident_in"), sem("const_in")
    x_loaded = [sem(f"x_loaded{c}") for c in range(4)]
    wg_loaded, misc_in, w2_in = sem("wg_loaded"), sem("misc_in"), sem("w2_in")
    cols_t, cols_ok = sem("cols_t"), sem("cols_ok")
    xt_ready, xh_done, xl_done = sem("xt_ready"), sem("xh_done"), sem("xl_done")
    r_ps, r_ok, r_out, e_out = sem("r_ps"), sem("r_ok"), sem("r_out"), sem("e_out")
    ss_done, sqrt_in, sqrt_out, rep_ok, rbc_ps, rbc_ok = (
        sem(n) for n in ("ss_done", "sqrt_in", "sqrt_out", "rep_ok", "rbc_ps", "rbc_ok"))
    wg_hi_ok, wg_ok, gl_ps, gl_ok, gt_ps, gates_ok, fz_ok, fe_ok, fcum_ok, c_out = (
        sem(n) for n in ("wg_hi_ok", "wg_ok", "gl_ps", "gl_ok", "gt_ps", "gates_ok", "fz_ok", "fe_ok", "fcum_ok", "c_out"))
    kv_done = sem("kv_done")
    vt_ps, vt_ok = sem("vt_ps"), sem("vt_ok")
    xs_hi_ok, xs_ok, halves_ok, blk_ps = sem("xs_hi_ok"), sem("xs_ok"), sem("halves_ok"), sem("blk_ps")
    gelu_ok, kc_ps, kc_ok, g4_ok, vc_ps, vc_ok = (
        sem(n) for n in ("gelu_ok", "kc_ps", "kc_ok", "g4_ok", "vc_ps", "vc_ok"))
    bn_loaded = [sem("bn_loaded0"), sem("bn_loaded1")]
    q_ready = sem("q_ready")
    qh_ok, ql_ok = sem("qh_ok"), sem("ql_ok")
    kh_ok, kl_ok = sem("kh_ok"), sem("kl_ok")
    ns_ready, ns_read = sem("ns_ready"), sem("ns_read")
    max_ready, cmp_shift = sem("max_ready"), sem("cmp_shift")
    exp_done, r_ready, p_ready, p3_ready = sem("exp_done"), sem("r_ready"), sem("p_ready"), sem("p3_ready")
    nt_ready, nt_act, nt_dve = sem("nt_ready"), sem("nt_act"), sem("nt_dve")
    npv_done, no_read = sem("npv_done"), sem("no_read")
    yh_ok, y_ok = sem("yh_ok"), sem("y_ok")
    gate_read = [sem("gateA_read"), sem("gateB_read")]
    sig_done = [sem("sigA_done"), sem("sigB_done")]
    br_read = [sem("brA_read"), sem("brB_read")]
    bf_loaded = [sem("bf_loaded0"), sem("bf_loaded1")]
    fproj = sem("fproj")
    f_hi_ok, f_lo_ok = sem("f_hi_ok"), sem("f_lo_ok")
    fs_ready, fs_read, fmax_ready, fexp_done, fr_ready, fp_ready = (
        sem(n) for n in ("fs_ready", "fs_read", "fmax_ready", "fexp_done", "fr_ready", "fp_ready"))
    fv_ps, fv_ok, ft_ready, ft_act, ft_dve, fpv_done, fo_read = (
        sem(n) for n in ("fv_ps", "fv_ok", "ft_ready", "ft_act", "ft_dve", "fpv_done", "fo_read"))
    mh_ok, ml_ok = sem("mh_ok"), sem("ml_ok")
    xr_loaded, wo_done, x1_add, x1_put, x1t_ps, x1t_read = (
        sem(n) for n in ("xr_loaded", "wo_done", "x1_add", "x1_put", "x1t_ps", "x1t_read"))
    hh_ok, hl_ok, h3_hi, h3_lo = sem("hh_ok"), sem("hl_ok"), sem("h3_hi"), sem("h3_lo")
    rep2_ok, rbc2_ps, rbc2_ok = sem("rep2_ok"), sem("rbc2_ps"), sem("rbc2_ok")
    up_read, tap2, tap0, gelu2, g_ok = (sem(n) for n in ("up_read", "tap2", "tap0", "gelu2", "g_ok"))
    v_read, ah_ok, a_ok = sem("v_read"), sem("ah_ok"), sem("a_ok")
    dn_done, dn_add = sem("dn_done"), sem("dn_add")
    gf_in, sq3_done, xg_ok, rs3_ok, o_act, o_dve, stored = (
        sem(n) for n in ("gf_in", "sq3_done", "xg_ok", "rs3_ok", "o_act", "o_dve", "stored"))

    win = w_in[0].rearrange("(k p) n -> p k n", p=P)
    wup = w_up[0].rearrange("(k p) n -> p k n", p=P)
    wbr = [w_branch_nsa[0].rearrange("(k p) n -> p k n", p=P), w_branch_fox[0].rearrange("(k p) n -> p k n", p=P)]
    wo4 = w_out[0].rearrange("(s k p) n -> s p k n", p=P, k=4)
    wdn = w_down[0].rearrange("(k p) n -> p k n", p=P)
    w1 = [w[0].rearrange("(h q j d) n -> q d h j n", d=P, h=2, q=2) for w in (cmp_w1_k, cmp_w1_v)]
    x_t = x[0].rearrange("(t p) n -> p t n", p=P)
    out_t = out[0].rearrange("(t p) n -> t p n", p=P)

    def strides(i, g):
        return kv_fm[:, ds(i * 2 + g, 1), :].rearrange("p a (c j) -> p j (a c)", j=CMP_STRIDE)

    def positions(i):
        return cols[:, ds(i * CMP_BLOCK + C_POS, CMP_BLOCK)].rearrange("p (h j) -> p j h", h=2)

    def final_split(t):
        return 1536 if t < TOK - 1 else 1024

    waits_met = {"sp": sem("waits_met_sp"), "dve": sem("waits_met_dve"), "pool": sem("waits_met_pool")}

    def hold(eng, on, value):
        eng.wait_ge(on, value)
        eng.sem_inc(waits_met["sp" if eng is nc.sync else "dve" if eng is nc.vector else "pool"], 1)

    block = ctx.enter_context(nc.Block())

    @block.sync
    def _(sp):
        def load(s, src, **view):
            hold(sp, w_ready, s.n + 1)
            sp.dma_start(w_raw[:, s.par, :].rearrange("p (k n) -> p k n", **view), src).then_inc(w_loaded[s.par], 16)

        def load_cols(s, src, col):
            load(s, src[:, :, ds(col, P)], n=P)

        def load_row(src, j, r0, n):
            sp.dma_start(rows[r0:r0 + n, j, :], src.rearrange("(a b) -> a b", b=P)).then_inc(const_in, 16)

        sp.dma_start(ident[:], c_ident).then_inc(ident_in, 16)
        for c in range(4):
            sp.dma_start(x_in[:, :, 512 * c:512 * c + 512], x_t[:, :, 512 * c:512 * c + 512]).then_inc(x_loaded[c], 16)
            if c == 0:
                load_row(attn_norm_g[0], 0, 0, 16)
                load_row(ffn_norm_g[0], 0, 16, 16)
                load_row(conv_b[0], 0, 32, 44)
            if c < 2:
                load_cols(slot(c), win, COL_KV + c * P)
        for c in range(2, 4):
            load_cols(slot(c), win, COL_KV + c * P)
        for kv in range(2):
            for q in range(2):
                for j in range(2):
                    load_cols(slot(S_KW + 6 * kv + 3 * q + j), win, COL_KV + (4 + 4 * kv + 2 * q + j) * P)
                s = slot(S_KW + 6 * kv + 3 * q + 2)
                hold(sp, w_ready, s.n + 1)
                for half, done in ((0, w1_loaded), (1, w_loaded[s.par])):
                    sp.dma_start(w_raw[:, s.par, 1024 * half:1024 * half + 1024].rearrange("p (j n) -> p j n", n=P),
                                 w1[kv][q, :, half]).then_inc(done, 16)
        load_cols(slot(S_QN), win, COL_QN)
        sp.wait_ge(e_out, 16)

        def load_bias_n(s, b, it):
            hold(sp, ns_read, s * 9 + 9)
            head = b * 4 + it
            sp.dma_start(bias_n[:, b, :], e_dram[ds(head * P, P), :]).then_inc(bn_loaded[b], 16)

        load_bias_n(0, 0, 0)
        with sp.Fori(0, 3) as it:
            load_cols(slot(S_QN + 1, 2, it), win, it * P + (COL_QN + 4 * P))
            load_bias_n(it * 2 + 1, 1, it)
            load_cols(slot(S_QN + 2, 2, it), win, it * P + (COL_QN + P))
            load_bias_n(it * 2 + 2, 0, it + 1)
        load_cols(slot(S_QN + 7), win, COL_QN + 7 * P)
        load_bias_n(7, 1, 3)

        def load_merge(base, col, which):
            with sp.Fori(0, 4) as i:
                for pair in range(2):
                    for j in range(2):
                        load_cols(slot(base + 3 * pair + j, 6, i), win, i * (4 * P) + (col + (2 * pair + j) * P))
                    load(slot(base + 3 * pair + 2, 6, i), wbr[which][:, :, ds(i * (4 * P) + 2 * pair * P, 2 * P)], n=2 * P)

        load_merge(S_GA, COL_MA, 0)

        def load_bias_f(h, b):
            hold(sp, fs_read, h * 4 + 1)
            sp.dma_start(bias_f[:, b, :], c_dram[ds(h, 1), :].to_broadcast([P, SEQ])).then_inc(bf_loaded[b], 16)

        for j, col in enumerate((COL_QF, COL_KF, COL_VF)):
            load_cols(slot(S_FOX + j), win, col)
        sp.wait_ge(c_out, 16)
        load_bias_f(0, 0)

        def load_head(c, per, i, h, b):
            for j, col in enumerate((COL_QF, COL_KF, COL_VF)):
                load_cols(slot(c + j, per, i), win, h * P + col)
            load_bias_f(h, b)

        with sp.Fori(0, 3) as i:
            load_head(S_FOX + 3, 6, i, i * 2 + 1, 1)
            load_head(S_FOX + 6, 6, i, i * 2 + 2, 0)
        load_head(S_FOX + 21, 0, None, 7, 1)
        load_merge(S_GB, COL_MB, 1)
        with sp.Fori(0, 4) as i:
            for s4 in range(4):
                load(slot(S_WO + s4, 4, i), wo4[s4][:, :, ds(i * 512, 512)], n=512)
        for j in range(4):
            load_cols(slot(S_U0 + j), wup, j * P)
        with sp.Fori(0, CHUNKS - 1) as c:
            for j in range(4):
                load_cols(slot(S_FF + j, 12, c), wup, c * 512 + (D_FF + j * P))
            for j in range(4):
                load_cols(slot(S_FF + 4 + j, 12, c), wup, c * 512 + (512 + j * P))
            for j in range(4):
                load(slot(S_FF + 8 + j, 12, c), wdn[:, ds(c * 4, 4), 512 * j:512 * j + 512], n=512)
        last = S_FF + 12 * (CHUNKS - 1)
        for j in range(4):
            load_cols(slot(last + j), wup, 2 * D_FF - 512 + j * P)
        for j in range(4):
            load(slot(last + 4 + j), wdn[:, 4 * (CHUNKS - 1):4 * CHUNKS, 512 * j:512 * j + 512], n=512)
        for t in range(TOK):
            sp.wait_ge(o_act, t + 1)
            sp.wait_ge(o_dve, t + 1)
            sp.dma_start(out_t[t], x1[:, t, :]).then_inc(stored, 16)
        sp.wait_ge(stored, 16 * TOK)

    @block.tensor
    def _(pe):
        mm = nc.tensor.matmul
        pe.sem_inc(w_used, 2)

        def three(dst, l_hi, l_lo, r_hi, r_lo, first, final):
            mm(dst, l_hi, r_hi, start=first, stop=False)
            mm(dst, l_hi, r_lo, start=False, stop=False)
            return mm(dst, l_lo, r_hi, start=False, stop=final)

        def slot_cols(s, bank, ks=range(KT), wait=True):
            if ks[0] == 0 and wait:
                pe.wait_ge(w_ready, s.n + 3)
            for k in ks:
                w = slice(k * P, k * P + P)
                last = three(pb[bank][:], w_hi[:, s.par, w], w_lo[:, s.par, w], h_hi[:, k, :], h_lo[:, k, :],
                             k == 0, k == KT - 1)
            if ks[-1] == KT - 1:
                last.then_inc(w_used, 1)

        def slot_parts(s, bank, nth, parts=range(4)):
            for part in parts:
                if part < 3:
                    pe.wait_ge(part_ready, nth * 3 + (part + 1))
                else:
                    pe.wait_ge(w_ready, s.n + 3)
                slot_cols(s, bank, range(4 * part, 4 * part + 4), False)

        def slot_tokens(s, banks, k0, n_k, a, b, first, final, done, free=None):
            pe.wait_ge(w_ready, s.n + 3)
            for t in range(TOK):
                if free is not None:
                    pe.wait_ge(*free(t))
                for k in range(4):
                    w = slice(k * 512, k * 512 + 512)
                    tk = slice(t * P, t * P + P)
                    last = three(pb[banks + t][:], a[:, k0 + k, tk], b[:, k0 + k, tk], w_hi[:, s.par, w],
                                 w_lo[:, s.par, w], first and k == 0, final and k == 3)
                if final and t < TOK - 1:
                    last.then_inc(done, 1)
            last.then_inc(w_used, 1)

        pe.wait_ge(ident_in, 16)
        for _ in range(10):
            mm(pb[7][:, 0:P], ident[:], ident[:], start=True, stop=True)
        pe.wait_ge(const_in, 16 * 7)
        for j, (c, n) in enumerate(((0, 120), (120, 88), (208, 64))):
            last = nc.tensor.transpose(pb[2][:, c:c + n], rows[0:n, j, :], ident[0:n, 0:n])
        last.then_inc(cols_t, 1)

        def transpose_x(k):
            pe.wait_ge(x_loaded[k // 4], 16)
            if k >= 4:
                pe.wait_ge(xl_done, k - 3)
            for t in range(TOK):
                last = nc.tensor.transpose(pb[4 + k % 4][:, t * P:t * P + P], x_in[:, t, k * P:k * P + P], ident[:])
            last.then_inc(xt_ready, 1)

        def wait_part(n, part):
            if part < 3:
                pe.wait_ge(part_ready, n * 3 + part + 1)
            else:
                pe.wait_ge(w_ready, n + 3)

        for k in range(3):
            transpose_x(k)
        for k in range(KT + 8):
            if k + 3 < KT:
                transpose_x(k + 3)
            if k < KT:
                pe.wait_ge(xl_done, k + 1)
                wait_part(0, k // 4)
                slot_cols(slot(0), 0, [k], False)
            if k >= 8:
                wait_part(1, (k - 8) // 4)
                slot_cols(slot(1), 1, [k - 8], False)
            if k == 12:
                pe.wait_ge(misc_in, 48)
                pe.wait_ge(dve_own, 1)
                pe.wait_ge(cols_ok, 1)
                mm(pb[3][0:8, 0:512], tabx[:], onehot[:, 0:512], start=True, stop=True)
                mm(pb[2][0:8, 0:P], tabx[:], onehot[:, 512:R_LEN], start=True, stop=True).then_inc(r_ps, 1)
        pe.wait_ge(r_ok, 1)
        pe.wait_ge(rep_ok, 1)
        for t in range(TOK):
            last = mm(pb[3][:, t * P:t * P + P], rs_rep[:, t, :], ident[:], start=True, stop=True)
        last.then_inc(rbc_ps, 1)
        pe.wait_ge(wg_ok, 1)
        for k in range(KT):
            last = three(pb[2][0:NG, :], wg_hi[:, k, :], wg_lo[:, k, :], h_hi[:, k, :], h_lo[:, k, :], k == 0, k == KT - 1)
        last.then_inc(gl_ps, 1)
        for j in range(2):
            pe.wait_ge(kv_done, j + 1)
            slot_cols(slot(2 + j), j)
        pe.wait_ge(gl_ok, 1)
        pe.wait_ge(rbc_ok, 1)
        for t in range(TOK):
            last = nc.tensor.transpose(pb[3][:, t * NG:t * NG + NG], gl[:, t * P:t * P + P], ident[0:NG, 0:NG])
        last.then_inc(gt_ps, 1)
        with pe.Fori(0, 2) as i:
            for q in range(2):
                for j in range(2):
                    pe.wait_ge(kv_done, i * 4 + (3 + 2 * q + j))
                    s = slot(S_KW + 3 * q + j, 6, i)
                    if j == 0:
                        slot_parts(s, j, i * 2 + (2 + q))
                    else:
                        slot_cols(s, j)
                s = slot(S_KW + 3 * q + 2, 6, i)
                pe.wait_ge(w_ready, s.n + 3)
                if q == 0:
                    pe.wait_ge(xs_ok, i + 1)
                    pe.wait_ge(halves_ok, i + 1)
                wh, wl = (w[:, s.par, :].rearrange("p (h j n) -> p j h n", h=2, n=P) for w in (w_hi, w_lo))
                for j in range(8):
                    last = three(pb[2][0:X_COLS, 0:2 * P].rearrange("p (h n) -> p h n", h=2), xs_hi[:, 8 * q + j, :], xs_lo[:, 8 * q + j, :],
                                 wh[:, j], wl[:, j], q == 0 and j == 0, q == 1 and j == 7)
                last.then_inc(w_used, 1)
        slot_parts(slot(S_QN), 0, 6, range(1))
        pe.wait_ge(kv_done, 12)
        for v, src in enumerate((6, 7, 10, 11)):
            for j in range(TOK):
                last = nc.tensor.transpose(pb[4 + v][:, j * P:j * P + P], kv_fm[:, src, j * P:j * P + P], ident[:])
            last.then_inc(vt_ps, 1)
        pe.wait_ge(halves_ok, 3)
        pe.wait_ge(gates_ok, 1)
        for kv in range(2):
            for half in range(2):
                last = mm(pb[3][:, kv * 64:kv * 64 + 64], halves[:, kv, half * P:half * P + P], sel[:, half, :],
                          start=half == 0, stop=half == 1)
        last.then_inc(blk_ps, 1)
        slot_parts(slot(S_QN), 0, 6, range(1, 3))
        pe.wait_ge(gelu_ok, 1)
        pe.wait_ge(w2_in, 32)
        mm(pb[2][:, 0:64], w2_sb[:, 0, :], gk[:], start=True, stop=True).then_inc(kc_ps, 1)
        pe.wait_ge(g4_ok, 1)
        pe.wait_ge(vt_ok, 4)
        for g in range(GROUPS):
            for t in range(TOK):
                last = mm(pb[5 + g][:, t * P:t * P + P], g4[:, g, t, :], w2_sb[:, 1, :], start=True, stop=True)
        last.then_inc(vc_ps, 1)
        slot_parts(slot(S_QN), 0, 6, range(3, 4))
        pe.wait_ge(kc_ok, 1)
        pe.wait_ge(vc_ok, 1)

        def scores(i, q, k, bias_mm):
            b, c = S_PLACE[i]
            dst = pb[b][:, c:c + P * (i + 1)]
            last = mm(dst, q[:, i * P:i * P + P], k[:, 0:P * (i + 1)], start=True, stop=not bias_mm)
            if bias_mm:
                last = mm(pb[b][:, c + P * i:c + P * i + P], ident_b[:], tri_b[:], start=False, stop=True)
            return last

        def scores_split(i, u, g):
            if i == 0:
                return scores(0, q_n, kv_fm[:, (4, 8)[u] + g, :], False)
            b, c = S_PLACE[i]
            k_hi, k_lo = (k_split[:, n + g, 0:P * (i + 1)] for n in K_PLACE[u])
            tq = slice(i * P, i * P + P)
            return three(pb[b][:, c:c + P * (i + 1)], q_hi[:, tq], q_lo[:, tq], k_hi, k_lo, True, True)

        def fox_scores(i):
            if i == 0:
                return scores(0, q_f, k_f, True)
            b, c = S_PLACE[i]
            tq, tk = slice(i * P, i * P + P), slice(0, P * (i + 1))
            three(pb[b][:, c:c + P * (i + 1)], qf_hi[:, tq], qf_lo[:, tq], kf_hi[:, tk], kf_lo[:, tk], True, False)
            return mm(pb[b][:, c + P * i:c + P * i + P], ident_b[:], tri_b[:], start=False, stop=True)

        def transposes(js, bank, lt):
            for j in js:
                c = PT_COL[j] - PT_COL[js[0]]
                for i in range(j, TOK):
                    last = nc.tensor.transpose(pb[bank][:, c + (i - j) * P:c + (i - j) * P + P],
                                               lt[:, L_COL[i] + j * P:L_COL[i] + j * P + P], ident[:])
            return last

        def weigh(j, v, pt, first, final):
            return mm(pb[7][:, j * P:SEQ], v[:, j, :], pt[:, PT_COL[j]:PT_COL[j] + SEQ - j * P], start=first, stop=final)

        def nsa_step(s, g, filler):
            pe.wait_ge(q_ready, s + 1)
            pe.wait_ge(ns_read, s * 9 + 18)
            for i in range(TOK):
                last = mm(pb[g][:, CP * i:CP * i + CP], q_n[:, i * P:i * P + P], kc_fm[:, g * CP:g * CP + CP],
                          start=True, stop=True)
            last.then_inc(ns_ready, 1)
            pe.wait_ge(ql_ok, s + 1)
            pe.wait_ge(kl_ok, 2)
            for u in range(2):
                if u == 1:
                    slot_cols(filler, 1 - g, [0])
                for k, i in enumerate(TILES):
                    if u == 1:
                        pe.wait_ge(ns_read, s * 9 + (18 + 2 + max(k, 2) if k else 18 + 2))
                    scores_split(i, u, g).then_inc(ns_ready, 1)
            slot_cols(filler, 1 - g, range(1, 13))
            for u in range(2):
                lt = (l_slc, l_win)[u]
                pe.wait_ge(p_ready, s * 3 + (2 if u == 0 else 3))
                pe.wait_ge(p3_ready, s * 2 + (u + 1))
                pe.wait_ge(nt_act, s * 4 + (2 * u + 2))
                if u == 1:
                    slot_cols(filler, 1 - g, [14])
                transposes([0], 5, lt).then_inc(nt_ready, 1)
                pe.wait_ge(nt_dve, s * 2 + (u + 1))
                transposes([1, 3], 6, lt).then_inc(nt_ready, 1)
                slot_cols(filler, 1 - g, [13 + 2 * u])
                pe.wait_ge(nt_act, s * 4 + (2 * u + 3))
                last = transposes([2], 5, lt)
                if u == 0:
                    last = nc.tensor.transpose(pb[5][:, 256:384], p_cmp[:].rearrange("p t c -> p (t c)"), ident[:])
                last.then_inc(nt_ready, 1)
                if u == 0:
                    pe.wait_ge(no_read, s + 1)
                v = v_tm[:, 2 * u + g]
                weigh(0, v, pt_n, u == 0, False)
                pe.wait_ge(nt_dve, s * 2 + (u + 2))
                weigh(1, v, pt_n, False, False)
                weigh(3, v, pt_n, False, False)
                pe.wait_ge(nt_act, s * 4 + (2 * u + 4))
                last = weigh(2, v, pt_n, False, u == 1)
                if u == 0:
                    for i in range(TOK):
                        last = mm(pb[7][:, i * P:i * P + P], vc4[:, g, i, :], pt_n[:, CMP_COL:CMP_COL + P], start=False, stop=False)
                last.then_inc(npv_done, 1)

        with pe.Fori(0, 3) as it:
            nsa_step(it * 2, 0, slot(S_QN + 1, 2, it))
            nsa_step(it * 2 + 1, 1, slot(S_QN + 2, 2, it))
        nsa_step(6, 0, slot(S_QN + 7))
        nsa_step(7, 1, slot(S_GA))

        def merge(base, which):
            def iteration(c, per, i, nth, pairs, more):
                for pair in range(2):
                    for j in range(1 - pair, 2):
                        pe.wait_ge(gate_read[which], nth + (2 * pair + j + 1))
                        slot_cols(slot(c + 3 * pair + j, per, i), j)
                    s = slot(c + 3 * pair + 2, per, i)
                    pe.wait_ge(w_ready, s.n + 3)
                    pe.wait_ge(y_ok, 2 * which + 2)
                    pe.wait_ge(br_read[which], pairs + (pair + 1))
                    for j in range(2):
                        for k in range(8):
                            w = slice(k * 2 * P + j * P, k * 2 * P + j * P + P)
                            last = three(pb[2 + j][:], w_hi[:, s.par, w], w_lo[:, s.par, w], y_hi[:, k, :], y_lo[:, k, :],
                                         k == 0, k == 7)
                    last.then_inc(w_used, 1)
                if more:
                    pe.wait_ge(gate_read[which], nth + 5)
                    slot_cols(slot(c + 6, per, i), 0)

            with pe.Fori(0, 3 if which else 4) as i:
                iteration(base, 6, i, i * 4, i * 2, True)
            if which:
                iteration(base + 18, 0, None, 12, 6, False)

        merge(S_GA, 0)

        def fox_slot(s, m, bank, ks=range(KT)):
            if ks[0] == 0:
                pe.wait_ge(fproj, m + 1)
            slot_cols(s, bank, ks)

        pe.wait_ge(gate_read[0], 18)
        for j in range(1, 3):
            fox_slot(slot(S_FOX + j), j, j % 2)

        def fox_step(h, c, per, i, fill):
            pe.wait_ge(fproj, h * 3 + 4)
            pe.wait_ge(f_lo_ok, h * 2 + 2)
            for k, t in enumerate(TILES):
                pe.wait_ge(fs_read, h * 4 + (7 if k == 1 else 5 + k))
                if k == 3:
                    pe.wait_ge(fv_ok, h + 1)
                fox_scores(t).then_inc(fs_ready, 1)
            fox_slot(slot(c, per, i), h * 3 + 3, c % 2, range(0, KT - 1))
            pe.wait_ge(fproj, h * 3 + 5)
            pe.wait_ge(fs_read, h * 4 + 12)
            for j in range(TOK):
                last = nc.tensor.transpose(pb[4][:, j * P:j * P + P], vf_fm[:, j * P:j * P + P], ident[:])
            last.then_inc(fv_ps, 1)
            pe.wait_ge(fp_ready, h + 1)
            pe.wait_ge(ft_act, h * 2 + 2)
            transposes([0], 5, l_fox).then_inc(ft_ready, 1)
            pe.wait_ge(ft_dve, h + 1)
            transposes([1, 3], 6, l_fox).then_inc(ft_ready, 1)
            fox_slot(slot(c, per, i), h * 3 + 3, c % 2, [KT - 1])
            pe.wait_ge(ft_act, h * 2 + 3)
            transposes([2], 5, l_fox).then_inc(ft_ready, 1)
            if fill > 1:
                fox_slot(slot(c + 1, per, i), h * 3 + 4, (c + 1) % 2)
            pe.wait_ge(fo_read, h + 1)
            pe.wait_ge(fv_ok, h + 2)
            weigh(0, vf_tm, pt_f, True, False)
            pe.wait_ge(ft_dve, h + 2)
            weigh(1, vf_tm, pt_f, False, False)
            weigh(3, vf_tm, pt_f, False, False)
            pe.wait_ge(ft_act, h * 2 + 4)
            weigh(2, vf_tm, pt_f, False, True).then_inc(fpv_done, 1)
            if fill > 1:
                fox_slot(slot(c + 2, per, i), h * 3 + 5, c % 2)

        with pe.Fori(0, 3) as i:
            fox_step(i * 2, S_FOX + 3, 6, i, 3)
            fox_step(i * 2 + 1, S_FOX + 6, 6, i, 3)
        fox_step(6, S_FOX + 21, 0, None, 3)
        fox_step(7, S_GB, 0, None, 1)
        merge(S_GB, 1)

        def wo_slot(c, per, i, sub, free):
            slot_tokens(slot(c, per, i), 0, 4 * sub, 4, h_hi, h_lo, sub == 0, sub == 3, wo_done, free)

        def x1_transposes(g):
            pe.wait_ge(x1_add, g * 4 + 4)
            for k in range(4):
                pe.wait_ge(x1t_read, g * 4 + (k + 1))
                for t in range(TOK):
                    last = nc.tensor.transpose(pb[4 + k][:, t * P:t * P + P], x1_new[:, t, k * P:k * P + P], ident[:])
                last.then_inc(x1t_ps, 1)

        pe.wait_ge(ml_ok, 1)
        wo_slot(S_WO, 0, None, 0, lambda t: (br_read[1], 8 if t < 2 else 9))
        pe.wait_ge(ml_ok, 4)
        with pe.Fori(0, 3) as g:
            for sub in range(1, 4):
                wo_slot(S_WO + sub, 4, g, sub, None)
            wo_slot(S_WO + 4, 4, g, 0, lambda t: (x1_add, g * 4 + (t + 1)))
            x1_transposes(g)
        for sub in range(1, 4):
            wo_slot(S_WO + 12 + sub, 0, None, sub, None)

        pe.wait_ge(hl_ok, 3)
        s0 = slot(S_U0)
        pe.wait_ge(x1_add, 14)
        slot_cols(s0, 0, range(0, 8))
        x1_transposes(3)
        slot_cols(s0, 0, range(8, 12))
        for k in range(12, KT):
            pe.wait_ge(h3_lo, k - 11)
            slot_cols(s0, 0, [k])
        slot_cols(slot(S_U0 + 1), 1, range(0, 8))
        pe.wait_ge(rep2_ok, 1)
        for t in range(TOK):
            last = mm(pb[6][:, t * P:t * P + P], rs_rep2[:, t, :], ident[:], start=True, stop=True)
        last.then_inc(rbc2_ps, 1)
        slot_cols(slot(S_U0 + 1), 1, range(8, KT))
        for j in (2, 3):
            pe.wait_ge(up_read, j - 1)
            slot_cols(slot(S_U0 + j), j % 2)

        def v_slots(c, per, i, u_n):
            for j in range(4):
                if j < 2:
                    pe.wait_ge(up_read, u_n + (3 + j))
                else:
                    pe.wait_ge(v_read, u_n + (j - 1))
                slot_cols(slot(c + j, per, i), j % 2)

        def down_slots(c, per, i, chunk):
            for j in range(4):
                if j == 0 and i is None:
                    s = slot(c)
                    pe.wait_ge(w_ready, s.n + 3)
                    pe.wait_ge(dn_add, chunk * 16 + 4)
                    for k in range(4):
                        pe.wait_ge(a_ok, chunk * 4 + k + 1)
                        for t in range(TOK):
                            last = three(pb[2 + t][:], a_hi[:, k, t * P:t * P + P], a_lo[:, k, t * P:t * P + P],
                                         w_hi[:, s.par, k * 512:k * 512 + 512], w_lo[:, s.par, k * 512:k * 512 + 512], k == 0, k == 3)
                            if k == 3:
                                last.then_inc(dn_done if t < TOK - 1 else w_used, 1)
                    continue
                if j == 0:
                    pe.wait_ge(a_ok, chunk * 4 + 4)
                slot_tokens(slot(c + j, per, i), 2, 0, 4, a_hi, a_lo, True, True, dn_done, lambda t: (dn_add, chunk * 16 + (4 * j + t + 1)))

        pe.wait_ge(x1_add, 16)
        with pe.Fori(0, CHUNKS - 1) as c:
            v_slots(S_FF, 12, c, c * 4)
            for j in range(4):
                if j < 2:
                    pe.wait_ge(v_read, c * 4 + (3 + j))
                else:
                    pe.wait_ge(up_read, c * 4 + (4 + j - 1))
                slot_cols(slot(S_FF + 4 + j, 12, c), j % 2)
            down_slots(S_FF + 8, 12, c, c)
        tail = S_FF + 12 * (CHUNKS - 1)
        v_slots(tail, 0, None, 4 * (CHUNKS - 1))
        down_slots(tail + 4, 0, None, CHUNKS - 1)

    @block.scalar
    def _(act):
        A = nc.scalar.activation
        own = Chain(act, act_own)

        def hi(s):
            act.wait_ge(w_loaded[s.par], s.half * 16 + 16)
            act.wait_ge(w_used, s.n + 1)
            A(w_hi[:, s.par, :], w_raw[:, s.par, :], ACT.Copy).then_inc(w_hi_done, 1)

        def hi_parts(s, parts=range(4)):
            if parts[0] == 0:
                act.wait_ge(w_loaded[s.par], s.half * 16 + 16)
                act.wait_ge(w_used, s.n + 1)
            for q in parts:
                c = slice(512 * q, 512 * q + 512)
                A(w_hi[:, s.par, c], w_raw[:, s.par, c], ACT.Copy).then_inc(part_hi if q < 3 else w_hi_done, 1)

        act.dma_start(rows[76:120, 0, :], conv_w[0, 0].rearrange("(a b) -> a b", b=P)).then_inc(const_in, 16)
        act.dma_start(rows[0:88, 1, :], conv_w[0, 1:3].rearrange("c (a b) -> (c a) b", b=P)).then_inc(const_in, 16)
        act.dma_start(rows[0:32, 2, :], cmp_pos_k[0]).then_inc(const_in, 16)
        act.dma_start(rows[32:64, 2, :], cmp_pos_v[0]).then_inc(const_in, 16)
        act.wait_ge(ident_in, 16)
        own.link(A(sq_junk[:, 0:1], ident[:, 0:1], ACT.Copy))
        act.wait_ge(cols_ok, 1)
        for k in range(KT):
            act.wait_ge(xt_ready, k + 1)
            A(h_hi[:, k, :], pb[4 + k % 4][:], ACT.Copy, scale=cols[:, G_ATTN + k:G_ATTN + k + 1]).then_inc(xh_done, 1)
            if k < 4:
                hi_parts(slot(0), [k])
            elif k in (5, 7, 9, 11):
                hi_parts(slot(1), [(k - 5) // 2])
        for t in range(TOK):
            if t:
                act.wait_ge(ss_done, t)
            A(sq_junk[:], x_in[:, t, :], ACT.Square, accum_out=ss[:, t:t + 1]).then_inc(ss_done, 1)
        act.wait_ge(sqrt_in, 1)
        A(ss[:, 8:12], ss[:, 4:8], ACT.Sqrt).then_inc(sqrt_out, 1)
        act.wait_ge(wg_loaded, 64)
        A(wg_hi[:], wg_raw[:], ACT.Copy).then_inc(wg_hi_ok, 1)
        act.wait_ge(r_ok, 1)
        act.dma_start(r_dram, r_sb[:]).then_inc(r_out, 16)
        hi(slot(2))
        act.wait_ge(r_out, 16)
        act.dma_start(e_dram.rearrange("(h p) c -> h p c", p=P),
                      bass.AP(tensor=r_dram.tensor, offset=P - 1, ap=[[R_LEN, HEADS], [-1, P], [1, SEQ]])).then_inc(e_out, 16)
        act.wait_ge(fz_ok, 1)
        own.link(A(fz[:, 1], fz[:, 2], ACT.Abs))
        own.link(A(fz[:, 1], fz[:, 1], ACT.Exp, scale=-1.0))
        A(fz[:, 1], fz[:, 1], ACT.Ln, bias=1.0).then_inc(fe_ok, 1)
        hi(slot(3))
        act.wait_ge(fcum_ok, 1)
        act.dma_start(c_dram, cum_f[:]).then_inc(c_out, 16)
        hi_parts(slot(S_KW))
        act.wait_ge(gt_ps, 1)
        A(gates[:], pb[3][:, 0:TOK * NG].rearrange("p (t n) -> p t n", n=NG)[:, :, HEADS:NG], ACT.Sigmoid).then_inc(gates_ok, 1)
        with act.Fori(0, 2) as i:
            hi(slot(S_KW + 1, 6, i))
            act.wait_ge(kv_done, i * 2 + 2)
            act.wait_ge(w_used, i * 6 + (S_KW - 1 + 3))
            for g in range(GROUPS):
                A(xs_hi[:, :, g * CP:g * CP + CP], strides(i, g), ACT.Copy)
            A(xs_hi[:, :, 2 * CP:X_COLS], positions(i), ACT.Copy).then_inc(xs_hi_ok, 1)
            for j in range(2, 7):
                if j in (2, 5):
                    act.wait_ge(w1_loaded, i * 32 + (16 if j == 2 else 32))
                (hi_parts if j % 3 == 0 else hi)(slot(S_KW + j, 6, i))

        def keys_hi(u):
            a = K_PLACE[u][0]
            A(k_split[:, a:a + 2, :], kv_fm[:, 4 + 4 * u:6 + 4 * u, :], ACT.Copy).then_inc(kh_ok, 1)

        act.wait_ge(kv_done, 12)
        act.wait_ge(xs_ok, 2)
        keys_hi(0)
        act.dma_start(w2_sb[:, 0, :], cmp_w2_k[0]).then_inc(w2_in, 16)
        act.dma_start(w2_sb[:, 1, :], cmp_w2_v[0]).then_inc(w2_in, 16)
        act.wait_ge(blk_ps, 1)
        A(gv[:], pb[3][:, 64:128], ACT.Gelu_apprx_tanh)
        A(gk[:], pb[3][:, 0:64], ACT.Gelu_apprx_tanh).then_inc(gelu_ok, 1)
        for v in range(4):
            act.wait_ge(vt_ps, v + 1)
            A(v_tm[:, v].rearrange("p j d -> p (j d)"), pb[4 + v][:], ACT.Copy).then_inc(vt_ok, 1)
        keys_hi(1)
        hi(slot(S_QN + 1))
        act.wait_ge(kc_ps, 1)
        A(kc_fm[:], pb[2][:, 0:64], ACT.Copy).then_inc(kc_ok, 1)

        def q_high(s):
            act.wait_ge(q_ready, s + 1)
            A(q_hi[:], q_n[:], ACT.Copy).then_inc(qh_ok, 1)

        q_high(0)

        def exps(lt, c):
            for i in TILES:
                cols_ = slice(L_COL[i], L_COL[i] + P * (i + 1))
                last = A(lt[:, cols_], lt[:, cols_], ACT.Exp, bias=nmx[:, c + i:c + i + 1], accum_out=sm[:, c + i:c + i + 1])
            return last

        def nsa_step(s, head, fill):
            hi(fill)
            act.wait_ge(cmp_shift, s + 1)
            A(p_cmp[:], p_cmp[:], ACT.Exp).then_inc(exp_done, 1)
            act.wait_ge(max_ready, s * 2 + 1)
            exps(l_slc, 4).then_inc(exp_done, 1)
            act.wait_ge(max_ready, s * 2 + 2)
            exps(l_win, 8).then_inc(exp_done, 1)
            for u in range(2):
                act.wait_ge(nt_ready, s * 6 + (3 * u + 1) + 6)
                act.wait_ge(npv_done, s * 2 + (u + 1))
                A(pt_n[:, 0:512], pb[5][:], ACT.Copy).then_inc(nt_act, 1)
                act.wait_ge(nt_ready, s * 6 + (3 * u + 3) + 6)
                n = 384 if u == 0 else 256
                A(pt_n[:, 1024:1024 + n], pb[5][:, 0:n], ACT.Copy).then_inc(nt_act, 1)
            if not isinstance(s, int) or s < HEADS - 1:
                q_high(s + 1)
            act.wait_ge(npv_done, s * 2 + 3)
            A(y32[:, ds(head, 1), :].rearrange("p a n -> p (a n)"), pb[7][:], ACT.Copy).then_inc(no_read, 1)

        act.sem_inc(nt_act, 2)
        act.sem_inc(no_read, 1)
        with act.Fori(0, 3) as it:
            nsa_step(it * 2, it, slot(S_QN + 2, 2, it))
            nsa_step(it * 2 + 1, it + 4, slot(S_QN + 3, 2, it))
        nsa_step(6, 3, slot(S_QN + 8))
        nsa_step(7, 7, slot(S_GA + 1))

        def merge(base, which):
            def iteration(c, per, i, count, last):
                for pair in range(2):
                    for j in range(2):
                        act.wait_ge(gate_read[which], count + (2 * pair + j + 3))
                        A(gate_t[:, j, :], gate_t[:, j, :], ACT.Sigmoid).then_inc(sig_done[which], 1)
                        if pair or j:
                            hi(slot(c + 3 * pair + j + 2, per, i))
                    if last and pair == 1:
                        for q in range(3):
                            merged_hi(q)
                    hi(slot(c + 3 * pair + 4, per, i))
                if not last:
                    hi(slot(c + 8, per, i))

            hi(slot(base + 2))
            if which == 0:
                act.wait_ge(npv_done, 2 * HEADS + 1)
                act.wait_ge(no_read, HEADS + 1)
            else:
                act.wait_ge(fpv_done, HEADS + 1)
                act.wait_ge(fo_read, HEADS + 1)
            for q in range(2):
                A(y_hi[:, 4 * q:4 * q + 4, :], y32[:, 4 * q:4 * q + 4, :], ACT.Copy).then_inc(yh_ok, 1)
            with act.Fori(0, 3 if which else 4) as i:
                iteration(base, 6, i, i * 4, False)
            if which:
                iteration(base + 18, 0, None, 12, True)
                merged_hi(3)

        def merged_hi(q):
            act.wait_ge(br_read[1], 8 if q < 3 else 9)
            A(h_hi[:, 4 * q:4 * q + 4, :], m32[:, 4 * q:4 * q + 4, :], ACT.Copy).then_inc(mh_ok, 1)

        merge(S_GA, 0)
        act.sem_inc(ft_act, 2)
        act.sem_inc(fo_read, 1)
        act.sem_inc(fv_ok, 1)

        def fox_hi(h):
            for j, (dst, src) in enumerate(((qf_hi, q_f), (kf_hi, k_f))):
                act.wait_ge(fproj, h * 3 + (j + 3))
                A(dst[:], src[:], ACT.Copy).then_inc(f_hi_ok, 1)

        hi(slot(S_FOX + 3))
        fox_hi(0)

        def fox_step(h, c, per, i, fill):
            hi(slot(c + 1, per, i))
            act.wait_ge(fmax_ready, h + 1)
            exps(l_fox, 4).then_inc(fexp_done, 1)
            act.wait_ge(fv_ps, h + 1)
            act.wait_ge(fpv_done, h + 1)
            A(vf_tm[:].rearrange("p j d -> p (j d)"), pb[4][:], ACT.Copy).then_inc(fv_ok, 1)
            act.wait_ge(ft_ready, h * 3 + 1)
            A(pt_f[:, 0:512], pb[5][:], ACT.Copy).then_inc(ft_act, 1)
            act.wait_ge(ft_ready, h * 3 + 3)
            A(pt_f[:, 1024:1280], pb[5][:, 0:256], ACT.Copy).then_inc(ft_act, 1)
            if fill > 1:
                hi(slot(c + 2, per, i))
                hi(slot(c + 3, per, i))
                fox_hi(h + 1)
            act.wait_ge(fpv_done, h + 2)
            A(y32[:, ds(h, 1), :].rearrange("p a n -> p (a n)"), pb[7][:], ACT.Copy).then_inc(fo_read, 1)

        with act.Fori(0, 3) as i:
            fox_step(i * 2, S_FOX + 3, 6, i, 3)
            fox_step(i * 2 + 1, S_FOX + 6, 6, i, 3)
        fox_step(6, S_FOX + 21, 0, None, 3)
        fox_step(7, S_GB, 0, None, 1)
        merge(S_GB, 1)
        act.wait_ge(w_used, S_WO + 2)
        for c in range(4):
            act.dma_start(x1[:, :, 512 * c:512 * c + 512], x_t[:, :, 512 * c:512 * c + 512]).then_inc(xr_loaded, 16)

        def wo_out(g):
            for t in range(TOK):
                act.wait_ge(x1_add, g * 4 + (t + 1))
                own.link(A(sq2[:], x1_new[:, t, :], ACT.Square, accum_out=ss[:, ds(g * 4 + t, 1)]))
                A(x1[:, t, ds(g * 512, 512)], x1_new[:, t, :], ACT.Copy).then_inc(x1_put, 1)

        def wo_trans(g):
            for k in range(4):
                act.wait_ge(x1t_ps, g * 4 + (k + 2))
                A(m32[:, ds(g * 4 + k, 1), :].rearrange("p a n -> p (a n)"), pb[4 + k][:], ACT.Copy,
                  scale=cols[:, ds(g * 4 + (G_FFN + k), 1)]).then_inc(x1t_read, 1)

        act.sem_inc(x1t_read, 4)
        with act.Fori(0, 3) as g:
            own.enter(g, 4)
            for sub in range(1, 4):
                hi(slot(S_WO + sub + 1, 4, g))
            wo_out(g)
            hi(slot(S_WO + 5, 4, g))
            wo_trans(g)
        own.leave(3)
        for sub in range(1, 4):
            hi(slot(S_WO + 12 + sub + 1))
            act.wait_ge(x1t_read, 16)
            A(h_hi[:, 4 * sub - 4:4 * sub, :], m32[:, 4 * sub - 4:4 * sub, :], ACT.Copy).then_inc(hh_ok, 1)
        wo_out(3)
        act.wait_ge(w_used, S_U0 + 2)
        for k in range(4):
            act.wait_ge(x1t_ps, 12 + (k + 2))
            A(h_hi[:, 12 + k, :], pb[4 + k][:], ACT.Copy, scale=cols[:, G_FFN + 12 + k:G_FFN + 13 + k]).then_inc(h3_hi, 1)
        hi(slot(S_U0 + 1))
        act.wait_ge(sqrt_in, 2)
        A(nmx[:, 4:8], nmx[:, 0:4], ACT.Sqrt).then_inc(sqrt_out, 1)
        hi(slot(S_U0 + 2))

        def conv_tap(n, f, j):
            if not isinstance(n, int) or n >= 2:
                act.wait_ge(g_ok, n - 1)
            act.wait_ge(up_read, n + 1)
            A(conv_t[:, j % 2, :], u_pad[:, j % 2, 2:SEQ + 2], ACT.Identity, bias=cols[:, ds(f + C_B, 1)],
              scale=cols[:, ds(f + C_W[2], 1)]).then_inc(tap2, 1)
            act.wait_ge(tap0, n + 1)
            A(conv_t[:, j % 2, :], conv_t[:, j % 2, :], ACT.Gelu_apprx_tanh).then_inc(gelu2, 1)

        def hidden_hi(n, j):
            act.wait_ge(v_read, n + 1)
            A(a_hi[:, j, :], a_t[:, j % 2, :], ACT.Copy).then_inc(ah_ok, 1)

        for j in range(4):
            if j in (1, 2):
                hi(slot(S_U0 + j + 2))
            conv_tap(j, j, j)
        with act.Fori(0, CHUNKS - 1) as c:
            for j in range(4):
                hi(slot(S_FF + j + 1, 12, c))
                hidden_hi(c * 4 + j, j)
            for j in range(4):
                hi(slot(S_FF + 5 + j, 12, c))
                conv_tap(c * 4 + (4 + j), c * 4 + (4 + j), j)
            for j in range(4):
                hi(slot(S_FF + 9 + j, 12, c))
        tail = S_FF + 12 * (CHUNKS - 1)
        for j in range(4):
            hi(slot(tail + j + 1))
            hidden_hi(4 * (CHUNKS - 1) + j, j)

        def final_square(j, t):
            act.wait_ge(dn_add, 16 * (CHUNKS - 1) + 4 * j + t + 1 + 4)
            own.link(A(sq3[:], x1[:, t, 512 * j:512 * j + 512], ACT.Square, accum_out=ss[:, 4 * j + t:4 * j + t + 1]))
            act.sem_inc(sq3_done, 1)

        def final_scale(t):
            n = final_split(t)
            act.wait_ge(rs3_ok, t + 1)
            act.wait_ge(xg_ok, 8 + t + 1)
            A(x1[:, t, 0:n], x1[:, t, 0:n], ACT.Copy, scale=rr[:, t:t + 1]).then_inc(o_act, 1)

        for j in range(3):
            hi(slot(tail + 5 + j))
            for t in range(TOK):
                final_square(j, t)
        own.link(A(sq3[:, 0:4], ss[:, 0:4], ACT.Sqrt))
        for t in range(TOK):
            final_square(3, t)
            act.wait_ge(sqrt_in, 3 + t)
            A(nmx[:, 4 + t:5 + t], nmx[:, t:t + 1], ACT.Sqrt).then_inc(sqrt_out, 1)
            if t:
                final_scale(t - 1)
        final_scale(TOK - 1)

    @block.vector
    def _(dve):
        V = nc.vector
        own = Chain(dve, dve_own)
        link = own.link

        def lo(s):
            dve.wait_ge(w_hi_done, s.n + 1)
            V.tensor_tensor(w_lo[:, s.par, :], w_raw[:, s.par, :], w_hi[:, s.par, :].bitcast(F32), ALU.subtract).then_inc(w_ready, 1)

        def lo_parts(s, nth, parts=range(4)):
            for q in parts:
                if q < 3:
                    dve.wait_ge(part_hi, nth * 3 + (q + 1))
                else:
                    dve.wait_ge(w_hi_done, s.n + 1)
                c = slice(512 * q, 512 * q + 512)
                V.tensor_tensor(w_lo[:, s.par, c], w_raw[:, s.par, c], w_hi[:, s.par, c].bitcast(F32), ALU.subtract).then_inc(part_ready if q < 3 else w_ready, 1)

        def rstd(total, v, t0, t1, dst, nth):
            V.tensor_scalar(v, total, 1.0 / D_MODEL, EPS, ALU.mult, ALU.add).then_inc(sqrt_in, 1)
            dve.wait_ge(sqrt_in, nth)
            dve.wait_ge(sqrt_out, nth)
            link(V.reciprocal(t0, t0))
            link(V.tensor_tensor(t1, v, t0, ALU.mult))
            link(V.tensor_tensor(t1, t1, t0, ALU.mult))
            link(V.tensor_scalar(t1, t1, -0.5, 1.5, ALU.mult, ALU.add))
            link(V.tensor_tensor(dst, t0, t1, ALU.mult))

        link(V.memset(tabx[32:33, :], NEG))
        dve.sem_inc(w_ready, 2)
        V.memset(ones_f[:], 1.0)
        V.memset(l_cmp[:], NEG)
        dve.wait_ge(ident_in, 16)
        V.tensor_copy(ident_b[:], ident[:])
        dve.wait_ge(cols_t, 1)
        V.tensor_copy(cols[:], pb[2][:, 0:272]).then_inc(cols_ok, 1)
        dve.wait_ge(cols_ok, 1)
        for k in range(KT):
            dve.wait_ge(xh_done, k + 1)
            V.scalar_tensor_tensor(h_lo[:, k, :], pb[4 + k % 4][:], cols[:, G_ATTN + k:G_ATTN + k + 1],
                                   h_hi[:, k, :].bitcast(F32), ALU.mult, ALU.subtract).then_inc(xl_done, 1)
            if k < 4:
                lo_parts(slot(0), 0, [k])
            elif k in (5, 7, 9, 11):
                lo_parts(slot(1), 1, [(k - 5) // 2])
        dve.wait_ge(misc_in, 48)
        V.tensor_copy(tri_b[:], tri32[:])
        dve.wait_ge(r_ps, 1)
        V.tensor_copy(r_sb[:, 0:512], pb[3][0:8, 0:512])
        V.tensor_copy(r_sb[:, 512:R_LEN], pb[2][0:8, 0:P]).then_inc(r_ok, 1)
        dve.wait_ge(ss_done, TOK)
        rstd(ss[:, 0:4], ss[:, 4:8], ss[:, 8:12], ss[:, 12:16], rr[:, 0:4], 1)
        for t in range(TOK):
            last = V.tensor_copy(rs_rep[:, t, :], rr[:, t:t + 1].to_broadcast([P, P]))
        last.then_inc(rep_ok, 1)
        dve.wait_ge(wg_hi_ok, 1)
        V.tensor_tensor(wg_lo[:], wg_raw[:], wg_hi[:].bitcast(F32), ALU.subtract).then_inc(wg_ok, 1)
        lo(slot(2))
        dve.wait_ge(rbc_ps, 1)
        V.tensor_copy(rbc[:], pb[3][:]).then_inc(rbc_ok, 1)
        dve.wait_ge(rbc_ok, 1)

        def kv_out(n, bank, after):
            dve.wait_ge(w_used, after + 3)
            V.tensor_tensor(kv_fm[:, ds(n, 1), :].rearrange("p a n -> p (a n)"), pb[bank][:], rbc[:], ALU.mult).then_inc(kv_done, 1)

        kv_out(0, 0, 0)
        kv_out(1, 1, 1)
        dve.wait_ge(gl_ps, 1)
        V.tensor_tensor(gl[:], pb[2][0:NG, :], rbc[0:NG, :], ALU.mult).then_inc(gl_ok, 1)
        dve.wait_ge(gl_ok, 1)
        V.tensor_scalar(fz[:, 2], gl[0:HEADS, :], fb[:], None, ALU.add).then_inc(fz_ok, 1)
        dve.wait_ge(fz_ok, 1)
        link(V.tensor_scalar(fz[:, 0], fz[:, 2], 0.0, None, ALU.min))
        dve.wait_ge(fe_ok, 1)
        link(V.tensor_tensor(fz[:, 2], fz[:, 1], fz[:, 0], ALU.subtract))
        V.tensor_tensor_scan(cum_f[:], ones_f[:], fz[:, 2], 0.0, ALU.mult, ALU.add).then_inc(fcum_ok, 1)
        lo(slot(3))
        kv_out(2, 0, 2)
        lo_parts(slot(S_KW), 2)
        kv_out(3, 1, 3)
        V.memset(g4[:], 0.0)
        with dve.Fori(0, 2) as i:
            for q in range(2):
                for j in range(2):
                    lo(slot(S_KW + 3 * q + j + 1, 6, i))
                    if q == 0 and j == 0:
                        dve.wait_ge(xs_hi_ok, i + 1)
                        for g in range(GROUPS):
                            c = slice(g * CP, g * CP + CP)
                            V.tensor_tensor(xs_lo[:, :, c], strides(i, g), xs_hi[:, :, c].bitcast(F32), ALU.subtract)
                        c = slice(2 * CP, X_COLS)
                        V.tensor_tensor(xs_lo[:, :, c], positions(i), xs_hi[:, :, c].bitcast(F32), ALU.subtract).then_inc(xs_ok, 1)
                    if j == 1:
                        lo_parts(slot(S_KW + 3 * q + 3, 6, i), i * 2 + (3 + q))
                    kv_out(i * 4 + (4 + 2 * q + j), j, slot(S_KW + 3 * q + j, 6, i).n)
            dve.wait_ge(w_used, i * 6 + (S_KW + 5 + 3))
            V.tensor_copy(halves[:, ds(i, 1), :].rearrange("p a n -> p (a n)"), pb[2][0:X_COLS, 0:2 * P]).then_inc(halves_ok, 1)
        dve.wait_ge(c_out, 16)
        dve.wait_ge(gelu_ok, 1)
        for g in range(GROUPS):
            for t in range(TOK):
                last = V.tensor_copy(g4[:, g, t, t * CP:t * CP + CP], gv[:, g * CP:g * CP + CP])
        last.then_inc(g4_ok, 1)

        def keys_lo(u):
            a, b = K_PLACE[u]
            dve.wait_ge(kh_ok, u + 1)
            V.tensor_tensor(k_split[:, b:b + 2, :], kv_fm[:, 4 + 4 * u:6 + 4 * u, :], k_split[:, a:a + 2, :].bitcast(F32),
                            ALU.subtract).then_inc(kl_ok, 1)

        keys_lo(0)
        dve.wait_ge(vt_ok, 4)
        keys_lo(1)
        lo(slot(S_QN + 1))
        dve.wait_ge(vc_ps, 1)
        for g in range(GROUPS):
            last = V.tensor_copy(vc4[:, g].rearrange("p t d -> p (t d)"), pb[5 + g][:])
        last.then_inc(vc_ok, 1)

        def q_out(dst, bank, after, done, scale):
            dve.wait_ge(w_used, after + 3)
            if scale is None:
                V.tensor_tensor(dst, pb[bank][:], rbc[:], ALU.mult).then_inc(done, 1)
            else:
                V.scalar_tensor_tensor(dst, pb[bank][:], scale, rbc[:], ALU.mult, ALU.mult).then_inc(done, 1)

        def q_low(s):
            dve.wait_ge(qh_ok, s + 1)
            V.tensor_tensor(q_lo[:], q_n[:], q_hi[:].bitcast(F32), ALU.subtract).then_inc(ql_ok, 1)

        q_out(q_n[:], 0, S_QN, q_ready, SCALE)
        q_low(0)

        def logits(lt, bias, c, ready, base, done):
            for k, i in enumerate(TILES):
                b, col = S_PLACE[i]
                n = P * (i + 1)
                hold(dve, ready, base + (3 if k == 1 else k + 1))
                V.tensor_tensor_reduce(out=lt[:, L_COL[i]:L_COL[i] + n], in0=pb[b][:, col:col + n], in1=bias(i), scale=1.0,
                                       scalar=-3.0e38, op0=ALU.add, op1=ALU.max, accum_out=mx[:, c + i:c + i + 1]).then_inc(done, 1)

        def nsa_step(s, g, it, bias_n_use, head, fill):
            dve.wait_ge(bn_loaded[g], bias_n_use * 16 + 16)
            dve.wait_ge(ns_ready, s * 9 + 1)
            for i in range(TOK):
                n = (96 + P * i) // CMP_STRIDE + 1
                start = SEQ - P - P * i + CMP_BLOCK - 1
                b = bias_n[:, g, start:start + (n - 1) * CMP_STRIDE + 1:CMP_STRIDE]
                last = V.tensor_tensor(l_cmp[:, i, 0:n], pb[g][:, CP * i:CP * i + n], b, ALU.add)
            last.then_inc(ns_read, 1)
            dve.wait_ge(ns_read, s * 9 + 19)
            link(V.tensor_reduce(mx[:, 0:4], l_cmp[:], AX.X, ALU.max))
            link(V.tensor_scalar(nmx[:, 0:4], mx[:, 0:4], -1.0e20, -1.0, ALU.max, ALU.mult))
            V.tensor_tensor(p_cmp[:], l_cmp[:], nmx[:, 0:4].unsqueeze(2).to_broadcast([P, TOK, CP]), ALU.add).then_inc(cmp_shift, 1)
            for u, lt in enumerate((l_slc, l_win)):
                logits(lt, lambda i: bias_n[:, g, SEQ - P - P * i:SEQ], 4 + 4 * u, ns_ready, s * 9 + (1 + 4 * u), ns_read)
                dve.wait_ge(ns_read, s * 9 + (23 + 4 * u))
                V.tensor_scalar(nmx[:, 4 + 4 * u:8 + 4 * u], mx[:, 4 + 4 * u:8 + 4 * u], -1.0, None, ALU.mult).then_inc(max_ready, 1)
            for u in range(3):
                c = slice(4 * u, 4 * u + 4)
                dve.wait_ge(exp_done, s * 3 + (u + 1))
                if u == 0:
                    link(V.tensor_reduce(sm[:, 0:4], p_cmp[:], AX.X, ALU.add))
                    link(V.tensor_scalar(sm[:, 0:4], sm[:, 0:4], 1.0e-30, None, ALU.max))
                link(V.reciprocal(rr[:, c], sm[:, c]))
                V.tensor_tensor(rr[:, c], rr[:, c], gates[:, :, ds(head * 3 + u, 1)].rearrange("p t a -> p (t a)"),
                                ALU.mult).then_inc(r_ready, 1)
                if u:
                    dve.wait_ge(r_ready, s * 3 + (u + 1))
                    d = (l_slc, l_win)[u - 1][:, L_COL[3]:L_COL[3] + SEQ]
                    V.tensor_scalar(d, d, rr[:, 4 * u + 3:4 * u + 4], None, ALU.mult).then_inc(p3_ready, 1)
            lo(fill)
            for u in range(2):
                dve.wait_ge(nt_ready, s * 6 + (3 * u + 2) + 6)
                dve.wait_ge(npv_done, s * 2 + (u + 1))
                V.tensor_copy(pt_n[:, 512:1024], pb[6][:]).then_inc(nt_dve, 1)
            if not isinstance(s, int) or s < HEADS - 1:
                q_out(q_n[:], 1 - g, fill.n - 1, q_ready, SCALE)
                q_low(s + 1)

        dve.wait_ge(gates_ok, 1)
        with dve.Fori(0, 3) as it:
            own.enter(it, 14)
            nsa_step(it * 2, 0, it, it, it, slot(S_QN + 2, 2, it))
            nsa_step(it * 2 + 1, 1, it, it, it + 4, slot(S_QN + 3, 2, it))
        own.leave(3)
        nsa_step(6, 0, 3, 3, 3, slot(S_QN + 8))
        nsa_step(7, 1, 3, 3, 7, slot(S_GA + 1))

        def merge(base, which):
            lo(slot(base + 2))
            for q in range(2):
                dve.wait_ge(yh_ok, 2 * which + q + 1)
                V.tensor_tensor(y_lo[:, 4 * q:4 * q + 4, :], y32[:, 4 * q:4 * q + 4, :], y_hi[:, 4 * q:4 * q + 4, :].bitcast(F32),
                                ALU.subtract).then_inc(y_ok, 1)

            def iteration(c, per, i, nth, pairs, last):
                for pair in range(2):
                    for j in range(2):
                        dve.wait_ge(w_used, slot(c + 3 * pair + j, per, i).n + 3)
                        V.tensor_tensor(gate_t[:, j, :], pb[j][:], rbc[:], ALU.mult).then_inc(gate_read[which], 1)
                        if pair or j:
                            lo(slot(c + 3 * pair + j + 2, per, i))
                    if last and pair == 1:
                        for q in range(3):
                            merged_lo(q)
                    dve.wait_ge(sig_done[which], nth + (2 * pair + 2))
                    dve.wait_ge(w_used, slot(c + 3 * pair + 2, per, i).n + 3)
                    for j in range(2):
                        dst = m32[:, ds(nth + (2 * pair + j), 1), :].rearrange("p a n -> p (a n)")
                        if which == 0:
                            r = V.tensor_tensor(dst, pb[2 + j][:], gate_t[:, j, :], ALU.mult)
                        else:
                            link(V.tensor_tensor(gate_t[:, j, :], pb[2 + j][:], gate_t[:, j, :], ALU.mult))
                            r = V.tensor_tensor(dst, dst, gate_t[:, j, :], ALU.add)
                    r.then_inc(br_read[which], 1)
                    dve.wait_ge(br_read[which], pairs + (pair + 2))
                    lo(slot(c + 3 * pair + 4, per, i))
                if not last:
                    lo(slot(c + 8, per, i))

            with dve.Fori(0, 3 if which else 4) as i:
                own.enter(i, 4 if which else 0)
                iteration(base, 6, i, i * 4, i * 2, False)
            own.leave(3 if which else 4)
            if which:
                iteration(base + 18, 0, None, 12, 6, True)

        def merged_lo(q):
            dve.wait_ge(mh_ok, q + 1)
            V.tensor_tensor(h_lo[:, 4 * q:4 * q + 4, :], m32[:, 4 * q:4 * q + 4, :], h_hi[:, 4 * q:4 * q + 4, :].bitcast(F32),
                            ALU.subtract).then_inc(ml_ok, 1)

        merge(S_GA, 0)

        def fox_lo(h):
            for j, (dst, src, high) in enumerate(((qf_lo, q_f, qf_hi), (kf_lo, k_f, kf_hi))):
                dve.wait_ge(f_hi_ok, h * 2 + (j + 1))
                V.tensor_tensor(dst[:], src[:], high[:].bitcast(F32), ALU.subtract).then_inc(f_lo_ok, 1)


        for j in range(3):
            if j == 2:
                lo(slot(S_FOX + 3))
                fox_lo(0)
            q_out((q_f, k_f, vf_fm)[j][:], j % 2, S_FOX + j, fproj, SCALE if j == 0 else None)

        def fox_step(h, b, use, c, per, i, fill):
            dve.wait_ge(bf_loaded[b], use * 16 + 16)
            logits(l_fox, lambda t: bias_f[:, b, 0:P * (t + 1)], 4, fs_ready, h * 4, fs_read)
            dve.wait_ge(fs_read, h * 4 + 12)
            V.tensor_scalar(nmx[:, 4:8], mx[:, 4:8], -1.0, None, ALU.mult).then_inc(fmax_ready, 1)
            lo(slot(c + 1, per, i))
            dve.wait_ge(fexp_done, h + 1)
            V.reciprocal(rr[:, 4:8], sm[:, 4:8]).then_inc(fr_ready, 1)
            dve.wait_ge(ft_ready, h * 3 + 2)
            dve.wait_ge(fpv_done, h + 1)
            V.tensor_copy(pt_f[:, 512:1024], pb[6][:]).then_inc(ft_dve, 1)
            if fill > 1:
                q_out(q_f[:], c % 2, slot(c, per, i).n, fproj, SCALE)
                lo(slot(c + 2, per, i))
                q_out(k_f[:], (c + 1) % 2, slot(c + 1, per, i).n, fproj, None)
                lo(slot(c + 3, per, i))
                fox_lo(h + 1)
                q_out(vf_fm[:], c % 2, slot(c + 2, per, i).n, fproj, None)

        with dve.Fori(0, 3) as i:
            fox_step(i * 2, 0, i, S_FOX + 3, 6, i, 3)
            fox_step(i * 2 + 1, 1, i, S_FOX + 6, 6, i, 3)
        fox_step(6, 0, 3, S_FOX + 21, 0, None, 3)
        fox_step(7, 1, 3, S_GB, 0, None, 1)
        merge(S_GB, 1)
        merged_lo(3)

        def wo_add(g, after):
            for t in range(TOK):
                if t < TOK - 1:
                    dve.wait_ge(wo_done, g * 3 + (t + 1))
                else:
                    dve.wait_ge(w_used, after + 3)
                if t == 0:
                    dve.wait_ge(x1t_ps, g * 4 + 1)
                    dve.wait_ge(x1_put, g * 4 + 1)
                V.tensor_tensor(x1_new[:, t, :], pb[t][:], x1[:, t, ds(g * 512, 512)], ALU.add).then_inc(x1_add, 1)

        dve.wait_ge(xr_loaded, 64)
        with dve.Fori(0, 3) as g:
            for sub in range(1, 4):
                lo(slot(S_WO + sub + 1, 4, g))
            wo_add(g, slot(S_WO + 3, 4, g).n)
            lo(slot(S_WO + 5, 4, g))

        def h2_lo(q):
            dve.wait_ge(hh_ok, q + 1)
            V.tensor_tensor(h_lo[:, 4 * q:4 * q + 4, :], m32[:, 4 * q:4 * q + 4, :], h_hi[:, 4 * q:4 * q + 4, :].bitcast(F32),
                            ALU.subtract).then_inc(hl_ok, 1)

        for sub in range(1, 4):
            lo(slot(S_WO + 12 + sub + 1))
            h2_lo(sub - 1)
        wo_add(3, S_U0 - 1)
        for k in range(4):
            dve.wait_ge(h3_hi, k + 1)
            V.scalar_tensor_tensor(h_lo[:, 12 + k, :], pb[4 + k][:], cols[:, G_FFN + 12 + k:G_FFN + 13 + k],
                                   h_hi[:, 12 + k, :].bitcast(F32), ALU.mult, ALU.subtract).then_inc(h3_lo, 1)
        lo(slot(S_U0 + 1))
        dve.wait_ge(x1_put, 4 * TOK + 1)
        link(V.tensor_reduce(mx[:, 0:4], ss.rearrange("p (g t) -> p t g", t=TOK), AX.X, ALU.add))
        rstd(mx[:, 0:4], nmx[:, 0:4], nmx[:, 4:8], nmx[:, 8:12], rr[:, 0:4], 2)
        for t in range(TOK):
            last = V.tensor_copy(rs_rep2[:, t, :], rr[:, t:t + 1].to_broadcast([P, P]))
        last.then_inc(rep2_ok, 1)
        V.memset(u_pad[:, :, 0:CONV - 1], 0.0)
        lo(slot(S_U0 + 2))
        dve.wait_ge(rbc2_ps, 1)
        link(V.tensor_copy(rbc[:], pb[6][:]))
        dve.sem_inc(rbc2_ok, 1)

        def up_out(n, f, j, bank_slot):
            dve.wait_ge(w_used, bank_slot.n + 3)
            V.tensor_tensor(u_pad[:, j % 2, 2:SEQ + 2], pb[j % 2][:], rbc[:], ALU.mult).then_inc(up_read, 1)
            dve.wait_ge(up_read, n + 1)
            dve.wait_ge(tap2, n + 1)
            link(V.scalar_tensor_tensor(conv_t[:, j % 2, :], u_pad[:, j % 2, 1:SEQ + 1], cols[:, ds(f + C_W[1], 1)],
                                        conv_t[:, j % 2, :], ALU.mult, ALU.add))
            V.scalar_tensor_tensor(conv_t[:, j % 2, :], u_pad[:, j % 2, 0:SEQ], cols[:, ds(f + C_W[0], 1)],
                                   conv_t[:, j % 2, :], ALU.mult, ALU.add).then_inc(tap0, 1)

        def hidden(n, j, s, g_n):
            dve.wait_ge(w_used, s.n + 3)
            dve.wait_ge(g_ok, g_n + 1)
            V.tensor_tensor(a_t[:, j % 2, :], pb[j % 2][:], g_rs[:, j, :], ALU.mult).then_inc(v_read, 1)
            dve.wait_ge(ah_ok, n + 1)
            V.tensor_tensor(a_lo[:, j, :], a_t[:, j % 2, :], a_hi[:, j, :].bitcast(F32), ALU.subtract).then_inc(a_ok, 1)

        def down_add(c, per, i, chunk, j, ts=range(TOK)):
            s = slot(c + j, per, i)
            for t in ts:
                if t < TOK - 1:
                    dve.wait_ge(dn_done, chunk * 12 + (3 * j + t + 1))
                else:
                    dve.wait_ge(w_used, s.n + 3)
                d = x1[:, t, 512 * j:512 * j + 512]
                V.tensor_tensor(d, pb[2 + t][:], d, ALU.add).then_inc(dn_add, 1)

        for j in range(4):
            if j in (1, 2):
                lo(slot(S_U0 + j + 2))
            up_out(j, j, j, slot(S_U0 + j))
        with dve.Fori(0, CHUNKS - 1) as c:
            own.enter(c, 4)
            for j in range(4):
                lo(slot(S_FF + j + 1, 12, c))
                hidden(c * 4 + j, j, slot(S_FF + j, 12, c), c * 4 + j)
            for j in range(4):
                lo(slot(S_FF + 5 + j, 12, c))
                up_out(c * 4 + (4 + j), c * 4 + (4 + j), j, slot(S_FF + 4 + j, 12, c))
            for j in range(4):
                lo(slot(S_FF + 9 + j, 12, c))
                down_add(S_FF + 8, 12, c, c, j)
        own.leave(CHUNKS - 1)
        tail = S_FF + 12 * (CHUNKS - 1)
        for j in range(4):
            lo(slot(tail + j + 1))
            hidden(4 * (CHUNKS - 1) + j, j, slot(tail + j), 4 * (CHUNKS - 1) + j)
        for j in range(3):
            lo(slot(tail + 5 + j))
            down_add(tail + 4, 0, None, CHUNKS - 1, j)
        def final_scale(t):
            n = final_split(t)
            if n < 1536:
                dve.wait_ge(xg_ok, 8 + t + 1)
                V.tensor_scalar(x1[:, t, n:1536], x1[:, t, n:1536], rr[:, t:t + 1], None, ALU.mult)
            d = x1[:, t, 1536:2048]
            V.scalar_tensor_tensor(d, d, rr[:, t:t + 1], gfin[:, 1536:2048], ALU.mult, ALU.mult).then_inc(o_dve, 1)

        dve.wait_ge(gf_in, 16)
        for t in range(TOK):
            down_add(tail + 4, 0, None, CHUNKS - 1, 3, [t])
            if t:
                final_scale(t - 1)
            dve.wait_ge(sq3_done, 12 + t + 1)
            link(V.tensor_reduce(mx[:, t:t + 1], ss.rearrange("p (g t) -> p t g", t=TOK)[:, t, :], AX.X, ALU.add))
            c = [nmx[:, 4 * n + t:4 * n + t + 1] for n in range(3)]
            rstd(mx[:, t:t + 1], c[0], c[1], c[2], rr[:, t:t + 1], 3 + t)
            dve.sem_inc(rs3_ok, 1)
        final_scale(TOK - 1)

    @block.gpsimd
    def _(pool):
        G = nc.gpsimd
        pool.dma_start(onehot[:], c_onehot).then_inc(misc_in, 16)
        pool.dma_start(tabx[0:32, :], rel_bias_table).then_inc(misc_in, 16)
        pool.dma_start(tri32[:], c_tri).then_inc(misc_in, 16)
        pool.dma_start(wg_raw[:, :, 0:HEADS], win[:, :, COL_FL:COL_FL + HEADS]).then_inc(wg_loaded, 16)
        pool.dma_start(wg_raw[:, :, HEADS:NG], win[:, :, COL_GN:COL_GN + NG - HEADS]).then_inc(wg_loaded, 16)
        pool.dma_start(fb[:], fox_forget_bias.rearrange("a h -> h a")).then_inc(wg_loaded, 16)
        pool.dma_start(sel[:], c_sel).then_inc(wg_loaded, 16)
        for s_, n in ((ns_read, 18), (nt_ready, 6), (nt_dve, 1), (npv_done, 1), (gate_read[0], 2), (gate_read[1], 2),
                      (br_read[0], 1), (br_read[1], 1), (fproj, 2), (fs_read, 8), (ft_dve, 1), (fpv_done, 1),
                      (x1t_ps, 1), (x1_put, 1), (dn_add, 4), (halves_ok, 1)):
            pool.sem_inc(s_, n)

        def scale(lt, c, tiles=TILES):
            for i in tiles:
                d = lt[:, L_COL[i]:L_COL[i] + P * (i + 1)]
                last = G.tensor_scalar(d, d, rr[:, c + i:c + i + 1], None, ALU.mult)
            return last

        with pool.Fori(0, HEADS) as s:
            hold(pool, r_ready, s * 3 + 1)
            G.tensor_tensor(p_cmp[:], p_cmp[:], rr[:, 0:4].unsqueeze(2).to_broadcast([P, TOK, CP]), ALU.mult).then_inc(p_ready, 1)
            hold(pool, r_ready, s * 3 + 2)
            scale(l_slc, 4, TILES[1:]).then_inc(p_ready, 1)
            hold(pool, r_ready, s * 3 + 3)
            scale(l_win, 8, TILES[1:]).then_inc(p_ready, 1)
        with pool.Fori(0, HEADS) as h:
            hold(pool, fr_ready, h + 1)
            scale(l_fox, 4).then_inc(fp_ready, 1)
        pool.wait_ge(rbc2_ok, 1)
        pool.dma_start(gfin[:], final_norm_g.rearrange("(a n) -> a n", a=1).to_broadcast([P, D_MODEL])).then_inc(gf_in, 16)

        def g_out(n, j):
            hold(pool, gelu2, n + 1)
            G.tensor_tensor(g_rs[:, j, :], conv_t[:, j % 2, :], rbc[:], ALU.mult).then_inc(g_ok, 1)

        with pool.Fori(0, CHUNKS) as c:
            for j in range(4):
                g_out(c * 4 + j, j)
        pool.wait_ge(gf_in, 16)
        for j in range(3):
            for t in range(TOK):
                pool.wait_ge(sq3_done, 4 * j + t + 1)
                d = x1[:, t, 512 * j:512 * j + 512]
                G.tensor_tensor(d, d, gfin[:, 512 * j:512 * j + 512], ALU.mult).then_inc(xg_ok, 1)

    ctx.close()


_INS = ['x', 'attn_norm_g', 'w_in', 'cmp_pos_k', 'cmp_w1_k', 'cmp_w2_k', 'cmp_pos_v', 'cmp_w1_v', 'cmp_w2_v',
        'rel_bias_table', 'fox_forget_bias', 'w_branch_nsa', 'w_branch_fox', 'w_out', 'ffn_norm_g', 'w_up', 'conv_w',
        'conv_b', 'w_down', 'final_norm_g']


def _constants():
    import math
    import numpy as np
    ident = np.eye(P, dtype=np.float32)
    onehot = np.zeros((REL_BUCKETS + 1, R_LEN), np.float32)
    exact = REL_BUCKETS // 2
    for j in range(R_LEN):
        dist = SEQ - 1 - j
        if dist < 0:
            onehot[REL_BUCKETS, j] = 1
        elif dist < exact:
            onehot[dist, j] = 1
        else:
            b = exact + int(math.log(dist / exact) / math.log(REL_MAX_DIST / exact) * (REL_BUCKETS - exact))
            onehot[min(b, REL_BUCKETS - 1), j] = 1
    sel = np.zeros((X_COLS, 2, GROUPS * CP), np.float32)
    for half in range(2):
        for g in range(GROUPS):
            for c in range(N_CMP):
                sel[g * CP + c + half, half, g * CP + c] = 1
                sel[GROUPS * CP + half, half, g * CP + c] = 1
    tri = np.where(np.arange(P)[None, :] > np.arange(P)[:, None], np.float32(NEG), np.float32(0)).astype(np.float32)
    return {"c_ident": ident, "c_onehot": onehot, "c_tri": tri, "c_sel": sel}


def kernel(**inputs):
    import numpy as _np
    import concourse.bacc as _bacc
    from concourse import mybir as _mybir
    from concourse.bass_utils import run_bass_kernel_spmd as _run

    nc = _bacc.Bacc("TRN2", target_bir_lowering=False, num_devices=1)
    arrays, args = {}, []
    given = {n: _np.ascontiguousarray(inputs[n]) for n in _INS}
    given.update(_constants())
    for name, a in given.items():
        arrays[f"in_{name}_dram"] = a
        args.append(nc.dram_tensor(f"in_{name}_dram", a.shape, _mybir.dt.from_np(a.dtype), kind="ExternalInput").ap())
    args.append(nc.dram_tensor("out_0_dram", (1, SEQ, D_MODEL), _mybir.dt.float32, kind="ExternalOutput").ap())
    build(nc, *args)
    r = _run(nc, [arrays], core_ids=[0])
    return r.results[0]["out_0_dram"]
```
